# Optimizing a Trainium2 kernel written in Bass

```python
import math
import jax
import jax.numpy as jnp
from jax import lax
import numpy as np

D_MODEL = 1024
BATCH = 1
SEQ = 1024
DEPTH = 2

GRID_W = 64
CTX_LEN = 256
EPS = 1e-6
CONV_DIM = 256
CONV_K = 3
NA_HEADS = 8
NA_HEAD_DIM = 64
NA_DIM = NA_HEADS * NA_HEAD_DIM
WIN_H = 8
WIN_W = 16
SSD_HEADS = 4
SSD_HEAD_DIM = 64
SSD_DIM = SSD_HEADS * SSD_HEAD_DIM
SSD_GROUPS = 2
SSD_STATE = 128
SSD_CONV_K = 3
SSD_CHUNK = 128
XBC_DIM = SSD_DIM + 2 * SSD_GROUPS * SSD_STATE
D_MIX = CONV_DIM + NA_DIM + SSD_DIM
ROPE_BASE = 10000.0
DT_MIN = 1e-3
DT_MAX = 1e-1
IN_SPLITS = (CONV_DIM, CONV_DIM, CONV_DIM, CONV_DIM, NA_DIM, NA_DIM, NA_DIM, NA_DIM, XBC_DIM, SSD_DIM, 2 * SSD_HEADS)
IN_DIM = 4 * CONV_DIM + 4 * NA_DIM + XBC_DIM + SSD_DIM + 2 * SSD_HEADS
F32 = jnp.float32

kernel_name = 'hybrid_conv_natten_ssd_dit'

def rms_norm(x, g):
    xf = x.astype(F32)
    y = xf * lax.rsqrt(jnp.mean(jnp.square(xf), axis=-1, keepdims=True) + EPS)
    return (y * g.astype(F32)).astype(x.dtype)

def depthwise_conv(x, w, b=None):
    k = w.shape[0]
    pad = k // 2
    y = lax.conv_general_dilated(x, w.astype(x.dtype)[:, None, :], window_strides=(1,),
                                 padding=[(pad, k - 1 - pad)],
                                 dimension_numbers=('NWC', 'WIO', 'NWC'),
                                 feature_group_count=x.shape[-1])
    if b is not None:
        y = y + b.astype(x.dtype)
    return y

def split_heads(t, n_heads):
    return t.reshape(*t.shape[:-1], n_heads, t.shape[-1] // n_heads)

def split_projection(u):
    return jnp.split(u, np.cumsum(IN_SPLITS)[:-1].tolist(), axis=-1)

def axial_rope(t, row_pos, col_pos):
    n_freq = t.shape[-1] // 4
    inv_freq = ROPE_BASE ** (-jnp.arange(n_freq, dtype=F32) / n_freq)
    ang = jnp.stack([row_pos[:, None] * inv_freq, col_pos[:, None] * inv_freq], axis=1)
    cos = jnp.cos(ang)[None, :, None]
    sin = jnp.sin(ang)[None, :, None]
    tr = t.astype(F32).reshape(*t.shape[:-1], 2, 2, n_freq)
    t1, t2 = tr[..., 0, :], tr[..., 1, :]
    out = jnp.stack([t1 * cos - t2 * sin, t1 * sin + t2 * cos], axis=-2)
    return out.reshape(t.shape).astype(t.dtype)

def ssd_chunked(xh, dt, a, bh, ch, init_state):
    bsz, seq = xh.shape[:2]
    nc = seq // SSD_CHUNK
    chunk = lambda t: t.astype(F32).reshape(bsz, nc, SSD_CHUNK, *t.shape[2:])
    x_c, dt_c, b_c, c_c = chunk(xh), chunk(dt), chunk(bh), chunk(ch)
    acs = jnp.cumsum(dt_c * a, axis=2)
    lower = jnp.tril(jnp.ones((SSD_CHUNK, SSD_CHUNK), dtype=bool))
    seg = acs[:, :, :, None, :] - acs[:, :, None, :, :]
    decay = jnp.exp(jnp.where(lower[None, None, :, :, None], seg, -jnp.inf))
    mix = jnp.einsum('bcihn,bcjhn->bcijh', c_c, b_c) * decay * dt_c[:, :, None, :, :]
    y_diag = jnp.einsum('bcijh,bcjhp->bcihp', mix, x_c)
    w_end = jnp.exp(acs[:, :, -1:, :] - acs) * dt_c
    states = jnp.einsum('bcjhn,bcjhp->bchpn', b_c * w_end[..., None], x_c)
    chunk_decay = jnp.exp(acs[:, :, -1, :])

    def step(s, inp):
        st, dec = inp
        return s * dec[:, :, None, None] + st, s

    final, prev = lax.scan(step, init_state.astype(F32),
                           (jnp.moveaxis(states, 1, 0), jnp.moveaxis(chunk_decay, 1, 0)))
    prev = jnp.moveaxis(prev, 0, 1)
    y_off = jnp.einsum('bcihn,bchpn->bcihp', c_c * jnp.exp(acs)[..., None], prev)
    return (y_diag + y_off).reshape(bsz, seq, *xh.shape[2:]), final

def ssd_bidirectional(xh, bh, ch, dt_f, dt_b, a_f, a_b, init_f, init_b):
    flip = lambda t: jnp.flip(t, axis=1)
    y_f, fin_f = ssd_chunked(xh, dt_f, a_f, bh, ch, init_f)
    y_b, fin_b = ssd_chunked(flip(xh), flip(dt_b), a_b, flip(bh), flip(ch), init_b)
    return y_f + flip(y_b), fin_f, fin_b

def ssd_inputs(u_xbc, u_dt, conv_w, conv_b, dt_bias_f, dt_bias_b, row_pos=None, col_pos=None):
    xbc = jax.nn.silu(depthwise_conv(u_xbc, conv_w, conv_b))
    xs, bs, cs = jnp.split(xbc, [SSD_DIM, SSD_DIM + SSD_GROUPS * SSD_STATE], axis=-1)
    bs = split_heads(bs, SSD_GROUPS)
    cs = split_heads(cs, SSD_GROUPS)
    if row_pos is not None:
        bs = axial_rope(bs, row_pos, col_pos)
        cs = axial_rope(cs, row_pos, col_pos)
    rep = SSD_HEADS // SSD_GROUPS
    bh = jnp.repeat(bs, rep, axis=2)
    ch = jnp.repeat(cs, rep, axis=2)
    xh = split_heads(xs, SSD_HEADS)
    dt_f = jax.nn.softplus(u_dt[..., :SSD_HEADS].astype(F32) + dt_bias_f.astype(F32))
    dt_b = jax.nn.softplus(u_dt[..., SSD_HEADS:].astype(F32) + dt_bias_b.astype(F32))
    return xh, bh, ch, dt_f, dt_b

def ssd_finish(y, xh, z, ssd_d, norm_w):
    y = y + ssd_d.astype(F32)[:, None] * xh.astype(F32)
    y = y.reshape(*y.shape[:2], SSD_DIM).astype(z.dtype)
    return rms_norm(y * jax.nn.silu(z), norm_w)

def neighborhood_attention(q, k, v, k_ctx, v_ctx, rpb):
    bsz, seq, heads, dh = q.shape
    rows = seq // GRID_W
    kh = min(WIN_H, rows)
    kw = WIN_W
    scale = dh ** -0.5
    qg = q.reshape(bsz, rows, GRID_W, heads, dh)
    kg = k.reshape(bsz, rows, GRID_W, heads, dh)
    vg = v.reshape(bsz, rows, GRID_W, heads, dh)
    cols = jnp.arange(GRID_W)
    col_idx = jnp.clip(cols - kw // 2, 0, GRID_W - kw)[:, None] + jnp.arange(kw)[None, :]
    rpb_cols = rpb[:, :, col_idx - cols[:, None] + (WIN_W - 1)]
    n_win = kh * kw

    def row_block(r):
        r0 = jnp.clip(r - kh // 2, 0, rows - kh)
        q_r = lax.dynamic_index_in_dim(qg, r, axis=1, keepdims=False)
        k_win = lax.dynamic_slice_in_dim(kg, r0, kh, axis=1)[:, :, col_idx]
        v_win = lax.dynamic_slice_in_dim(vg, r0, kh, axis=1)[:, :, col_idx]
        bias = jnp.take(rpb_cols, r0 + jnp.arange(kh) - r + (WIN_H - 1), axis=1)
        s_win = (jnp.einsum('bqhd,biqjhd->bhqij', q_r, k_win).astype(F32) * scale
                 + bias.transpose(0, 2, 1, 3)[None].astype(F32))
        s_ctx = jnp.einsum('bqhd,bkhd->bhqk', q_r, k_ctx).astype(F32) * scale
        s = jnp.concatenate([s_win.reshape(bsz, heads, GRID_W, n_win), s_ctx], axis=-1)
        p = jax.nn.softmax(s, axis=-1).astype(v.dtype)
        p_win = p[..., :n_win].reshape(bsz, heads, GRID_W, kh, kw)
        return (jnp.einsum('bhqij,biqjhd->bqhd', p_win, v_win)
                + jnp.einsum('bhqk,bkhd->bqhd', p[..., n_win:], v_ctx))

    out = lax.map(row_block, jnp.arange(rows))
    return jnp.moveaxis(out, 0, 1).reshape(bsz, seq, heads * dh)

def context_attention(q, k, v):
    s = jnp.einsum('bqhd,bkhd->bhqk', q, k).astype(F32) * (q.shape[-1] ** -0.5)
    p = jax.nn.softmax(s, axis=-1).astype(v.dtype)
    o = jnp.einsum('bhqk,bkhd->bqhd', p, v)
    return o.reshape(*o.shape[:2], NA_DIM)

def merge_project(y_sc, z_sc, y_na, z_na, y_ss, w_out):
    y = jnp.concatenate([y_sc * jax.nn.silu(z_sc), y_na * jax.nn.silu(z_na), y_ss], axis=-1)
    return y @ w_out

def hybrid_layer(x, x_ctx, c, c_ctx, w_ada, b_ada, g_pre, g_post, w_in, conv_a_w, rpb,
                 ssd_conv_w, ssd_conv_b, dt_bias_f, dt_bias_b, a_log_f, a_log_b, ssd_d,
                 ssd_norm_w, w_out, row_pos, col_pos, update_ctx):
    bsz = x.shape[0]
    shift, scale, gate = jnp.split((jax.nn.silu(c) @ w_ada + b_ada)[:, None, :], 3, axis=-1)
    shift_c, scale_c, gate_c = jnp.split(jax.nn.silu(c_ctx) @ w_ada + b_ada, 3, axis=-1)
    h = rms_norm(x, g_pre) * (1 + scale) + shift
    h_c = rms_norm(x_ctx, g_pre) * (1 + scale_c) + shift_c
    (sc_in, sc_b, sc_c, sc_z, na_q, na_k, na_v, na_z, ss_xbc, ss_z, ss_dt) = split_projection(h @ w_in)
    (c_sc_in, c_sc_b, c_sc_c, c_sc_z, c_na_q, c_na_k, c_na_v, c_na_z,
     c_ss_xbc, c_ss_z, c_ss_dt) = split_projection(h_c @ w_in)
    decay_f = -jnp.exp(a_log_f.astype(F32))
    decay_b = -jnp.exp(a_log_b.astype(F32))

    c_xh, c_bh, c_ch, c_dt_f, c_dt_b = ssd_inputs(c_ss_xbc, c_ss_dt, ssd_conv_w, ssd_conv_b, dt_bias_f, dt_bias_b)
    zero_state = jnp.zeros((bsz, SSD_HEADS, SSD_HEAD_DIM, SSD_STATE), F32)
    c_y_ss, fin_f, fin_b = ssd_bidirectional(c_xh, c_bh, c_ch, c_dt_f, c_dt_b, decay_f, decay_b,
                                             zero_state, zero_state)
    c_k = split_heads(c_na_k, NA_HEADS)
    c_v = split_heads(c_na_v, NA_HEADS)

    y_sc = sc_b * depthwise_conv(sc_c * sc_in, conv_a_w)
    y_na = neighborhood_attention(split_heads(na_q, NA_HEADS), split_heads(na_k, NA_HEADS),
                                  split_heads(na_v, NA_HEADS), c_k, c_v, rpb)
    xh, bh, ch, dt_f, dt_b = ssd_inputs(ss_xbc, ss_dt, ssd_conv_w, ssd_conv_b, dt_bias_f, dt_bias_b,
                                        row_pos, col_pos)
    y_ss, _, _ = ssd_bidirectional(xh, bh, ch, dt_f, dt_b, decay_f, decay_b, fin_f, fin_b)
    out = merge_project(y_sc, sc_z, y_na, na_z, ssd_finish(y_ss, xh, ss_z, ssd_d, ssd_norm_w), w_out)
    x = x + gate * rms_norm(out, g_post)

    if update_ctx:
        c_y_sc = c_sc_b * depthwise_conv(c_sc_c * c_sc_in, conv_a_w)
        c_y_na = context_attention(split_heads(c_na_q, NA_HEADS), c_k, c_v)
        c_out = merge_project(c_y_sc, c_sc_z, c_y_na, c_na_z,
                              ssd_finish(c_y_ss, c_xh, c_ss_z, ssd_d, ssd_norm_w), w_out)
        x_ctx = x_ctx + gate_c * rms_norm(c_out, g_post)
    return x, x_ctx

def setup_inputs(seed: int = 0) -> dict:
    key = jax.random.key(seed)
    ks = jax.random.split(key, 24)
    nrm = lambda k, shape, s: jax.random.normal(k, shape, F32) * s

    def dt_bias(k):
        dt = jnp.exp(jax.random.uniform(k, (DEPTH, SSD_HEADS), F32, math.log(DT_MIN), math.log(DT_MAX)))
        return dt + jnp.log(-jnp.expm1(-dt))

    return {
        'x': nrm(ks[0], (BATCH, SEQ, D_MODEL), 1.0),
        'c': nrm(ks[1], (BATCH, D_MODEL), 1.0),
        'ctx': nrm(ks[2], (BATCH, CTX_LEN, D_MODEL), 1.0),
        'c_ctx': nrm(ks[3], (D_MODEL,), 1.0),
        'w_ada': nrm(ks[4], (DEPTH, D_MODEL, 3 * D_MODEL), 0.5 * D_MODEL ** -0.5),
        'b_ada': nrm(ks[5], (DEPTH, 3 * D_MODEL), 0.01),
        'g_pre': 1.0 + nrm(ks[6], (DEPTH, D_MODEL), 0.05),
        'g_post': 1.0 + nrm(ks[7], (DEPTH, D_MODEL), 0.05),
        'w_in': nrm(ks[8], (DEPTH, D_MODEL, IN_DIM), D_MODEL ** -0.5),
        'conv_a_w': nrm(ks[9], (DEPTH, CONV_K, CONV_DIM), CONV_K ** -0.5),
        'rpb': nrm(ks[10], (DEPTH, NA_HEADS, 2 * WIN_H - 1, 2 * WIN_W - 1), 0.1),
        'ssd_conv_w': nrm(ks[11], (DEPTH, SSD_CONV_K, XBC_DIM), SSD_CONV_K ** -0.5),
        'ssd_conv_b': nrm(ks[12], (DEPTH, XBC_DIM), 0.01),
        'dt_bias_f': dt_bias(ks[13]),
        'dt_bias_b': dt_bias(ks[14]),
        'a_log_f': jnp.log(jax.random.uniform(ks[15], (DEPTH, SSD_HEADS), F32, 1.0, 16.0)),
        'a_log_b': jnp.log(jax.random.uniform(ks[16], (DEPTH, SSD_HEADS), F32, 1.0, 16.0)),
        'ssd_d': 1.0 + nrm(ks[17], (DEPTH, SSD_HEADS), 0.05),
        'ssd_norm_w': 1.0 + nrm(ks[18], (DEPTH, SSD_DIM), 0.05),
        'w_out': nrm(ks[19], (DEPTH, D_MIX, D_MODEL), D_MIX ** -0.5),
    }

def reference(x, c, ctx, c_ctx, w_ada, b_ada, g_pre, g_post, w_in, conv_a_w, rpb, ssd_conv_w,
              ssd_conv_b, dt_bias_f, dt_bias_b, a_log_f, a_log_b, ssd_d, ssd_norm_w, w_out):
    pos = jnp.arange(x.shape[1])
    row_pos = (pos // GRID_W).astype(F32)
    col_pos = (pos % GRID_W).astype(F32)
    x_ctx = ctx
    for layer in range(DEPTH):
        x, x_ctx = hybrid_layer(x, x_ctx, c, c_ctx, w_ada[layer], b_ada[layer], g_pre[layer],
                                g_post[layer], w_in[layer], conv_a_w[layer], rpb[layer],
                                ssd_conv_w[layer], ssd_conv_b[layer], dt_bias_f[layer],
                                dt_bias_b[layer], a_log_f[layer], a_log_b[layer], ssd_d[layer],
                                ssd_norm_w[layer], w_out[layer], row_pos, col_pos,
                                layer < DEPTH - 1)
    return x


_drawn_inputs = setup_inputs


def setup_inputs(seed=0):
    import zlib

    import numpy as np

    out = dict(_drawn_inputs(seed))
    spreads = {}
    factors = {'b_ada': 3.254,
     'g_post': 2.767,
     'rpb': 31.508,
     'ssd_conv_b': 8.0,
     'a_log_f': 24.712,
     'ssd_d': 124.16,
     'ssd_norm_w': 3.89,
     'ctx': 24.656,
     'c_ctx': 8.0,
     'dt_bias_f': 8.0,
     'dt_bias_b': 2.687,
     'a_log_b': 3.445}
    for name, (base, spread) in spreads.items():
        noise = np.random.default_rng([zlib.crc32(name.encode()), seed]).standard_normal(out[name].shape)
        drawn = base * np.exp(spread * noise) if base else spread * noise
        out[name] = jnp.asarray(drawn.astype(out[name].dtype))
    for name, factor in factors.items():
        out[name] = (out[name] * factor).astype(out[name].dtype)
    return out
```

```python
from contextlib import ExitStack

import numpy as np

import concourse.bass as bass
from concourse import mybir

F32 = mybir.dt.float32
F32R = mybir.dt.float32r
ACT = mybir.ActivationFunctionType
ALU = mybir.AluOpType
AX_X = mybir.AxisListType.X

P = 128
DM = 1024
KC = DM // P
SEQ, CTX, DEPTH = 1024, 256, 2
T = CTX + SEQ
NT = T // P
CT = CTX // P
LT = SEQ // P
GRID_W = 64
ROWS = SEQ // GRID_W
EPS = 1e-6
CONV, NA, SSD = 256, 512, 256
HEADS, DH = 8, 64
WIN_H, WIN_W = 8, 16
PAIRS = HEADS // 2
SH, SP_ = 4, 64
SG, SN = 2, 128
SCALE = DH ** -0.5
NEG = -1e30
TW = 16
NB_IN = 32
NB = NB_IN + DM // P
NADA = 3 * DM // P
CHUNKS = [(0, CTX), (CTX, 512), (CTX + 512, 512)]
Q0 = 16
BIG = -3.0e38
SPLIT_IN = np.cumsum([0, 256, 256, 256, 256, 512, 512, 512, 512, 768, 256, 8])


def block_columns():
    s_in, s_b, s_c, s_z, q, k, v, z, xbc, ssz, _ = SPLIT_IN[:11]
    cols = []
    for j in range(2):
        cols += [s_in + P * j, s_c + P * j, s_b + P * j, s_z + P * j]
    x, b, c = xbc, xbc + SSD, xbc + SSD + SG * SN
    cols += [c, c + P, b, b + P, x, x + P]
    cols += [ssz, ssz + P]
    for j in range(PAIRS):
        cols += [q + P * j, k + P * j, v + P * j, z + P * j]
    return [int(c) for c in cols]


def window(t):
    r = 2 * t
    r0 = min(max(r - WIN_H // 2, 0), ROWS - WIN_H)
    last = min(max(r + 1 - WIN_H // 2, 0), ROWS - WIN_H) + WIN_H
    return r0, last - r0, r0 - r + WIN_H - 1


def trunk(nc, A):
    ctx = ExitStack()
    with ctx:
        def sb(name, shape, dt=F32):
            return ctx.enter_context(nc.sbuf_tensor(name, shape, dt))

        def sem(name):
            return ctx.enter_context(nc.semaphore(name))

        def sems(name, n=DEPTH):
            return [sem(f"{name}{i}") for i in range(n)]

        hHi = sb("hHi", [P, KC, T], F32R)
        hLo = sb("hLo", [P, KC, T], F32R)
        yT = sb("yT", [P, KC, T])
        wraw = [sb(f"wraw{i}", [P, KC, P]) for i in range(2)]
        whi = [sb(f"whi{i}", [P, KC, P], F32R) for i in range(2)]
        wlo = [sb(f"wlo{i}", [P, KC, P], F32R) for i in range(2)]
        RN = 14848
        R = sb("region", [P, RN])
        ident = sb("ident", [P, P])
        maskF = sb("maskF", [P, P])
        maskB = sb("maskB", [P, P])
        perm = sb("perm", [P, P])
        colmask = sb("colmask", [P, GRID_W])
        rowmask = sb("rowmask", [P, WIN_H + 1])
        ccol = sb("ccol", [P, KC, 2])
        mod = sb("mod", [P, DEPTH, NADA, 2])
        bada = sb("bada", [P, DEPTH, NADA])
        gpre = sb("gpre", [P, DEPTH, KC])
        gpost = sb("gpost", [P, DEPTH, KC])
        cw = sb("cw", [P, DEPTH, 6, 4])
        caw = sb("caw", [P, DEPTH, 2, 3])
        nrmw = sb("nrmw", [P, DEPTH, 2])
        dtb = sb("dtb", [P, DEPTH, 8])
        alog = sb("alog", [P, DEPTH, 8])
        dsk = sb("dsk", [P, DEPTH, SH])
        wdtHi = sb("wdtHi", [P, KC, 8], F32R)
        wdtLo = sb("wdtLo", [P, KC, 8], F32R)
        st = sb("st", [P, 64])
        eps_col = sb("eps_col", [P, 1])
        sm = sb("sm", [P, 5, 80])

        def reg(a, n):
            return R[:, a:a + n]

        junk = reg(6144, DM)
        gbc = [reg(0, DM), reg(DM, DM)]
        xres = [reg(2048 + DM * i, DM) for i in range(2)]
        osb = [reg(4096 + DM * i, DM) for i in range(2)]
        xt = [reg(7168 + DM * i, DM) for i in range(3)]
        h32 = [reg(10240 + DM * i, DM).rearrange("p (k c) -> p k c", k=KC) for i in range(2)]
        adaw = [reg(12800 + DM * i, DM).rearrange("p (k c) -> p k c", k=KC) for i in range(2)]
        CTt = [reg(T * g, T) for g in range(2)]
        BTt = [reg(2 * T + T * g, T) for g in range(2)]
        xtok = reg(5120, 2560).rearrange("p (c n) -> p c n", c=NT)
        btok = reg(7680, 2560).rearrange("p (c g n) -> p c g n", c=NT, g=SG)
        gin, gc, gb, gz = [reg(5120 + T * i, T) for i in range(4)]
        ubuf = [reg(10240 + 1284 * i, 1284) for i in range(2)]
        cv = reg(12808, T)
        rtmp = reg(14088, 512)
        wdt = reg(12320, 64).rearrange("p (k n) -> p k n", k=KC)
        ztok = yT[:, 2:4, :].rearrange("p a (b n) -> p (a b) n", n=256)
        spare = yT[:, 4:6, :].rearrange("p a b -> p (a b)")
        cosT, sinT = spare[:, 0:1024], spare[:, 1024:2048]
        prevb = reg(10240, 2560).rearrange("p (c n) -> p c n", c=NT)
        Ed = [[reg(12800 + 1024 * s + 512 * d, 512).rearrange("p (h i) -> p h i", h=SH) for d in range(2)]
              for s in range(2)]
        xp = [spare[:, 256 * i:256 * i + 256] for i in range(2)]
        xw = spare[:, 512:768]
        prevf = [spare[:, 768 + 256 * i:1024 + 256 * i] for i in range(2)]
        GM = [spare[:, 1280 + 256 * i:1536 + 256 * i].rearrange("p (g i) -> p g i", g=SG) for i in range(2)]
        yacc, yt2, yxd = [spare[:, 1792 + 256 * i:2048 + 256 * i] for i in range(3)]
        qT, kT, zT = [reg(T * i, T) for i in range(3)]
        vtok = reg(3840, T).rearrange("p (c n) -> p c n", c=NT)
        tabF = [reg(5120 + 1600 * e, 1024).rearrange("p (k r) -> p k r", r=TW) for e in range(2)]
        tabI = [reg(6144 + 1600 * e, 576).rearrange("p (k r) -> p k r", r=WIN_H + 1) for e in range(2)]
        Pr = [reg(8320 + 832 * i, 832) for i in range(2)]
        PT = [reg(9984 + 896 * i, 896) for i in range(2)]
        vT = reg(9984, T)
        ysb = [reg(11776 + 128 * i, 128) for i in range(2)]

        ss, rstd = st[:, 0:10], st[:, 10:20]
        ss2, rstd2 = st[:, 20:30], st[:, 30:40]
        mx = [st[:, 40 + 2 * i:42 + 2 * i] for i in range(2)]
        sums = [st[:, 44 + 4 * i:48 + 4 * i] for i in range(4)]
        s_dt, s_ac, s_ea, s_we, s_de = [sm[:, i, :] for i in range(5)]
        s_t0, s_t1 = reg(14088, 80), reg(14168, 80)

        def dth(x, d, c):
            return x[:, 40 * d + 4 * c:40 * d + 4 * c + 4]

        def hb(x, n):
            return x.unsqueeze(2).broadcast_to([P, SH, n])

        def by_head(x, n=SP_):
            return x.rearrange("p (h n) -> p h n", h=SH)

        PS = ctx.enter_context(nc.psum_tensor("PS", [P, 4096], F32))

        def bank(b, n=1):
            return PS[:, 512 * b:512 * (b + n)]

        consts = sem("consts")
        silu_c = sem("silu_c")
        eps_ok = sem("eps_ok")
        aneg_ok = sem("aneg_ok")
        ada_loaded = sems("ada_loaded", 2)
        ada_mm, ada_taken, mod_ready = sems("ada_mm"), sems("ada_taken"), sems("mod_ready")
        x_loaded = sems("x_loaded", 3)
        rstd_ok, xn_ready = sems("rstd_ok"), sems("xn_ready")
        sd_done = sems("sd_done")
        xnT_done, xnT_taken, h32_ready = sems("xnT_done"), sems("xnT_taken"), sems("h32_ready")
        hhi_ready, hlo_ready = sems("hhi_ready"), sems("hlo_ready")
        w_loaded = sems("w_loaded", 2)
        w_split, proj_done, proj_taken = sems("w_split"), sems("proj_done"), sems("proj_taken")
        wdt_loaded, wdt_split = sems("wdt_loaded"), sems("wdt_split")
        rope_loaded = sems("rope_loaded")
        aux_done, aux_taken = sems("aux_done"), sems("aux_taken")
        dt_abs, dt_exp = sems("dt_abs"), sems("dt_exp")
        small_in, small_exp = sems("small_in"), sems("small_exp")
        da_ready, acs_ready = sems("da_ready"), sems("acs_ready")
        convA_done, conv_done, silu_done, rope_done = (sems("convA_done"), sems("conv_done"),
                                                       sems("silu_done"), sems("rope_done"))
        xwb_ready = sems("xwb_ready")
        g_done, bc_done, g_taken, sub_ready, exp_ready = (sems("g_done"), sems("bc_done"), sems("g_taken"),
                                                          sems("sub_ready"), sems("exp_ready"))
        mix_ready, xp_ready, prevf_ready = sems("mix_ready"), sems("xp_ready"), sems("prevf_ready")
        yo_done, stf_done, yd_done, yo_taken = (sems("yo_done"), sems("stf_done"), sems("yd_done"),
                                                sems("yo_taken"))
        y_gated, ysq_done, yn_ready, yss_done = (sems("y_gated"), sems("ysq_done"), sems("yn_ready"),
                                                 sems("yss_done"))
        tab_loaded, tab_ready = sems("tab_loaded"), sems("tab_ready")
        s_done, nm_ready, p_ready, pT_done = sems("s_done"), sems("nm_ready"), sems("p_ready"), sems("pT_done")
        ptA_ready, ptB_ready, o_done, o_taken = (sems("ptA_ready"), sems("ptB_ready"), sems("o_done"),
                                                 sems("o_taken"))
        yna_done, yna_taken = sems("yna_done"), sems("yna_taken")
        yhi_ready, ylo_ready = sems("yhi_ready"), sems("ylo_ready")
        gb_done, gb_taken = sems("gb_done"), sems("gb_taken")
        oT_done, osd_done, o_ready = sems("oT_done"), sems("osd_done"), sems("o_ready")
        xres_loaded = sems("xres_loaded", 2)
        res_added = sems("res_added")
        stored = sems("stored", 2)
        pair_chain = sems("pair_chain")
        act_chain, dve_chain, pool_chain = sem("act_chain"), sem("dve_chain"), sem("pool_chain")

        def chunks(l, j):
            if l < DEPTH - 1:
                return CHUNKS
            full = j in (10, 11, 12, 13) or (Q0 <= j < NB_IN and (j - Q0) % 4 in (1, 2))
            return CHUNKS if full else CHUNKS[1:]

        def tiles(l):
            return list(range(NT)) if l < DEPTH - 1 else list(range(CT, NT))

        def rounds(ts):
            return [ts[i:i + 4] for i in range(0, len(ts), 4)]

        def slot_cols(j):
            base = 1536 * (j % 2) + 256
            return base

        def aux_before_attention(l):
            return 3 + 8 + 4 * len(rounds(range(NT))) + 2 * len(rounds(tiles(l))) + NT - 1 + 2 * len(rounds(tiles(l)))

        def stores(l, i):
            return 16 * (l * (NT // 2) + i // 2 + 1)

        junk2 = bank(7)[:, 0:256]
        BO = [1, 0] + list(range(NT - 1, CT - 1, -1))
        x_in, x_mid = A["tokens"], A["x_mid"]

        block = ctx.enter_context(nc.Block())

        @block.sync
        def _(sp):
            for dst, src in [(ident, "ident"), (maskF, "maskF"), (maskB, "maskB"), (perm, "perm"),
                             (colmask, "colmask"), (rowmask, "rowmask"), (ccol, "ccol"), (bada, "b_ada"),
                             (gpre, "g_pre"), (gpost, "g_post"), (cw, "conv_w"), (caw, "conv_a"),
                             (nrmw, "norm_w")]:
                sp.dma_start(dst[:], A[src]).then_inc(consts, 16)
            for dst, src in [(dtb, "dt_bias"), (alog, "a_log"), (dsk, "ssd_d")]:
                sp.dma_start(dst[:].rearrange("p l n -> p (l n)"), A[src].partition_broadcast(P)).then_inc(consts, 16)

            def load_ada(l, b):
                if b >= 2:
                    sp.wait_ge(ada_mm[l], b - 1)
                sp.dma_start(adaw[b % 2], A["w_ada"][l, b]).then_inc(ada_loaded[b % 2], 16)

            def load_w(l, j):
                if j >= 2:
                    sp.wait_ge(w_split[l], j - 1)
                elif l:
                    sp.wait_ge(w_split[l - 1], NB - 1 + j)
                sp.dma_start(wraw[j % 2][:], A["w_blocks"][l, j]).then_inc(w_loaded[j % 2], 16)

            def load_x(l, t):
                if t >= 3:
                    sp.wait_ge(xnT_done[l], t - 2)
                if l:
                    sp.wait_ge(stored[t % 2], stores(0, t))
                src = x_mid if l else x_in
                sp.dma_start(xt[t % 3], src[P * t:P * t + P, :]).then_inc(x_loaded[t % 3], 16)

            def load_res(l, i, t):
                if i >= 2:
                    sp.wait_ge(res_added[l], i - 1)
                else:
                    sp.wait_ge(yna_taken[l], PAIRS * len(tiles(l)) + 1)
                src = x_mid if l else x_in
                sp.dma_start(xres[i % 2], src[P * t:P * t + P, :]).then_inc(xres_loaded[i % 2], 16)

            for l in range(DEPTH):
                load_w(l, 0)
                load_w(l, 1)
                if l:
                    sp.wait_ge(proj_done[l - 1], NB_IN + 1)
                sp.dma_start(wdt[:], A["w_dt"][l]).then_inc(wdt_loaded[l], 16)
                if l == 0:
                    for t in range(3):
                        load_x(l, t)
                    for b in range(NADA):
                        load_ada(0, b)
                    for t in range(3, NT):
                        load_x(l, t)
                else:
                    for i, t in enumerate(tiles(l - 1)):
                        load_res(l - 1, i, t)
                        if 2 <= i < 5:
                            load_x(l, t - 2)
                    for t in range(3, NT):
                        load_x(l, t)
                for j in range(2, Q0):
                    load_w(l, j)
                    if j == 7:
                        if l:
                            sp.wait_ge(proj_done[l], 1)
                        sp.dma_start(cosT, A["rope_cos"]).then_inc(rope_loaded[l], 16)
                        sp.dma_start(sinT, A["rope_sin"]).then_inc(rope_loaded[l], 16)
                n_steps = 2 * len(tiles(l))
                for hp in range(PAIRS):
                    for i in range(4):
                        load_w(l, Q0 + 4 * hp + i)
                    if hp == 0:
                        sp.wait_ge(yss_done[l], 1)
                    else:
                        sp.wait_ge(nm_ready[l], n_steps * hp)
                    for e in range(2):
                        for half in range(2):
                            src = bass.AP(tensor=A["rpb"].tensor,
                                          offset=((l * HEADS + 2 * hp + e) * (127 * TW + TW)
                                                  + TW - half),
                                          ap=[[TW, GRID_W], [1, GRID_W * TW]])
                            dst = tabF[e][GRID_W * half:GRID_W * (half + 1)].rearrange("p k r -> p (k r)")
                            sp.dma_start(dst, src).then_inc(tab_loaded[l], 16)
                    if l + 1 < DEPTH:
                        for b in range(6 * hp, 6 * hp + 6):
                            load_ada(l + 1, b)
                for j in range(NB_IN, NB):
                    load_w(l, j)
            for i, t in enumerate(tiles(DEPTH - 1)):
                load_res(DEPTH - 1, i, t)
            for i in (LT - 2, LT - 1):
                sp.wait_ge(stored[i % 2], stores(DEPTH - 1, i))

        @block.gpsimd
        def _(pool):
            chain = [0]

            def link(ins):
                chain[0] += 1
                ins.then_inc(pool_chain, 1)
                pool.wait_ge(pool_chain, chain[0])

            def split_w(l, j):
                s = j % 2
                pool.wait_ge(w_loaded[s], 16 * (l * (NB // 2) + j // 2 + 1))
                if j >= 2:
                    pool.wait_ge(proj_done[l], j - 1)
                elif l:
                    pool.wait_ge(proj_done[l - 1], NB - 1 + j)
                link(pool.tensor_copy(whi[s][:], wraw[s][:]))
                pool.tensor_tensor(wlo[s][:], wraw[s][:], whi[s][:].bitcast(F32), ALU.subtract).then_inc(w_split[l], 1)

            def residual(l, i, t):
                pool.wait_ge(o_ready[l], i + 1)
                pool.wait_ge(xres_loaded[i % 2], stores(l, i))
                link(pool.tensor_tensor(osb[i % 2], osb[i % 2], xres[i % 2], ALU.add))
                pool.sem_inc(res_added[l], 1)
                dst = x_mid[P * t:P * t + P, :] if l < DEPTH - 1 else A["out"][P * (t - CT):P * (t - CT) + P, :]
                pool.dma_start(dst, osb[i % 2]).then_inc(stored[i % 2], 16)

            for l in range(DEPTH):
                if l:
                    for i, t in enumerate(tiles(l - 1)):
                        residual(l - 1, i, t)
                split_w(l, 0)
                split_w(l, 1)
                for t in range(NT):
                    pool.wait_ge(hhi_ready[l], t + 1)
                    c = slice(P * t, P * t + P)
                    pool.tensor_tensor(hLo[:, :, c], h32[t % 2], hHi[:, :, c].bitcast(F32), ALU.subtract).then_inc(hlo_ready[l], 1)
                for j in range(2, NB):
                    split_w(l, j)
            for i, t in enumerate(tiles(DEPTH - 1)):
                residual(DEPTH - 1, i, t)

        @block.scalar
        def _(act):
            chain = [0]

            def link(ins):
                chain[0] += 1
                ins.then_inc(act_chain, 1)
                act.wait_ge(act_chain, chain[0])

            def take(l, j, dst, func=ACT.Copy, scale=1.0, padded=False):
                act.wait_ge(proj_done[l], j + 1)
                b = slot_cols(j)
                if padded:
                    if len(chunks(l, j)) == 3:
                        nc.scalar.activation(dst[:, 1:1 + CTX], PS[:, b:b + CTX], func, scale=scale)
                    last = nc.scalar.activation(dst[:, 2 + CTX:2 + CTX + SEQ], PS[:, b + CTX:b + T], func, scale=scale)
                else:
                    o = 0 if len(chunks(l, j)) == 3 else CTX
                    last = nc.scalar.activation(dst[:, o:T], PS[:, b + o:b + T], func, scale=scale)
                last.then_inc(proj_taken[l], 1)

            def norm_stats(l, t):
                act.wait_ge(x_loaded[t % 3], 16 * (l * len(range(t % 3, NT, 3)) + t // 3 + 1))
                link(nc.scalar.activation(junk, xt[t % 3], ACT.Square, accum_out=ss[:, t:t + 1]))
                nc.scalar.activation(rstd[:, t:t + 1], ss[:, t:t + 1], ACT.Sqrt, scale=1.0 / DM,
                                     bias=eps_col[:, 0:1]).then_inc(sd_done[l], 1)
                act.wait_ge(rstd_ok[l], t + 1)
                nc.scalar.activation(xt[t % 3], xt[t % 3], ACT.Copy, scale=rstd[:, t:t + 1]).then_inc(xn_ready[l], 1)

            def high_part(l, t):
                act.wait_ge(h32_ready[l], t + 1)
                if t == 0 and l:
                    act.wait_ge(proj_done[l - 1], NB)
                nc.scalar.activation(hHi[:, :, P * t:P * t + P], h32[t % 2], ACT.Copy).then_inc(hhi_ready[l], 1)

            act.wait_ge(consts, 16 * 16)
            act.wait_ge(eps_ok, 1)
            link(nc.scalar.activation(ccol[:], ccol[:], ACT.Silu))
            act.sem_inc(silu_c, 1)
            nc.scalar.activation(alog[:], alog[:], ACT.Exp).then_inc(aneg_ok, 1)

            for l in range(DEPTH):
                for t in range(NT):
                    norm_stats(l, t)
                    if t >= 1:
                        high_part(l, t - 1)
                high_part(l, NT - 1)

                act.wait_ge(dt_abs[l], 1)
                nc.scalar.activation(s_t1, s_t1, ACT.Exp, scale=-1.0).then_inc(dt_exp[l], 1)
                for j2 in range(2):
                    if j2:
                        act.wait_ge(convA_done[l], 1)
                    for i, (dst, func) in enumerate([(gin, ACT.Copy), (gc, ACT.Copy), (gb, ACT.Copy), (gz, ACT.Silu)]):
                        take(l, 4 * j2 + i, dst, func)
                act.wait_ge(small_in[l], 1)
                nc.scalar.activation(s_ea, s_ac, ACT.Exp)
                nc.scalar.activation(s_we, s_we, ACT.Exp)
                nc.scalar.activation(s_de, s_de, ACT.Exp).then_inc(small_exp[l], 1)

                def silu(j):
                    act.wait_ge(conv_done[l], j - 7)
                    o = 0 if len(chunks(l, j)) == 3 else CTX
                    dst = {8: CTt[0], 9: CTt[1], 10: BTt[0], 11: BTt[1], 12: cv, 13: cv}[j]
                    nc.scalar.activation(dst[:, o:T], cv[:, o:T], ACT.Silu).then_inc(silu_done[l], 1)

                for j in range(8, 14):
                    if j == 8:
                        act.wait_ge(convA_done[l], 2)
                    if j >= 10:
                        act.wait_ge(conv_done[l], j - 9)
                    take(l, j, ubuf[j % 2], padded=True)
                    if j >= 9:
                        silu(j - 1)
                act.wait_ge(conv_done[l], 5)
                take(l, 14, ubuf[0], ACT.Silu)
                silu(13)
                act.wait_ge(conv_done[l], 6)
                take(l, 15, ubuf[1], ACT.Silu)

                ys = tiles(l)
                for i, c in enumerate(ys):
                    for d in range(2):
                        act.wait_ge(sub_ready[l], 2 * i + d + 1)
                        nc.scalar.activation(Ed[i % 2][d], Ed[i % 2][d], ACT.Exp).then_inc(exp_ready[l], 1)
                for i, c in enumerate(ys):
                    act.wait_ge(y_gated[l], i + 1)
                    link(nc.scalar.activation(junk2, ztok[:, c, :], ACT.Square, accum_out=ss[:, c:c + 1]))
                a = ys[0]
                nc.scalar.activation(rstd[:, a:NT], ss[:, a:NT], ACT.Sqrt, scale=1.0 / SSD,
                                     bias=eps_col[:, 0:1]).then_inc(ysq_done[l], 1)

                steps = [(t, e) for t in tiles(l) for e in range(2)]
                n = len(steps)

                def soft(hp, i):
                    t, e = steps[i]
                    s = i % 2
                    act.wait_ge(nm_ready[l], hp * n + i + 1)
                    if t >= CT:
                        nw = 64 * window(t - CT)[1]
                        nc.scalar.activation(Pr[s][:, 0:nw], Pr[s][:, 0:nw], ACT.Exp, bias=mx[s][:, 1:2],
                                             accum_out=sums[i % 4][:, 0:1])
                    nc.scalar.activation(Pr[s][:, 576:832], PS[:, 1024 * s + 576:1024 * s + 832], ACT.Exp,
                                         bias=mx[s][:, 1:2], accum_out=sums[i % 4][:, 1:2]).then_inc(p_ready[l], 1)

                def pt_high(hp, i):
                    t, e = steps[i]
                    act.wait_ge(pT_done[l], hp * n + i + 1)
                    if t >= CT and window(t - CT)[1] == 9:
                        nc.scalar.activation(PT[i % 2][0:64, 512:640], PS[0:64, 2560:2688], ACT.Copy)
                    nc.scalar.activation(PT[i % 2][:, 640:896], PS[:, 2688:2944], ACT.Copy).then_inc(ptB_ready[l], 1)

                with act.Fori(0, PAIRS) as hp:
                    for i, (dst, func, sc) in enumerate([(qT, ACT.Copy, SCALE), (kT, ACT.Copy, 1.0),
                                                         (vT, ACT.Copy, 1.0), (zT, ACT.Silu, 1.0)]):
                        j = Q0 + i
                        act.wait_ge(proj_done[l], 4 * hp + (j + 1))
                        if i == 3:
                            act.wait_ge(yna_taken[l], hp * len(tiles(l)) + 1)
                        b = slot_cols(j)
                        o = 0 if len(chunks(l, j)) == 3 else CTX
                        nc.scalar.activation(dst[:, o:T], PS[:, b + o:b + T], func, scale=sc).then_inc(proj_taken[l], 1)
                    act.wait_ge(aux_taken[l], aux_before_attention(l) + 3 * hp + 3)
                    soft(hp, 0)
                    for i in range(n):
                        if i + 1 < n:
                            soft(hp, i + 1)
                        pt_high(hp, i)

                act.wait_ge(yna_taken[l], PAIRS * len(tiles(l)) + 1)
                act.wait_ge(yss_done[l], 1)
                o = 0 if l < DEPTH - 1 else CTX
                for k in range(KC):
                    nc.scalar.activation(hHi[:, k, o:T], yT[:, k, o:T], ACT.Copy).then_inc(yhi_ready[l], 1)
                for m in range(KC):
                    j = NB_IN + m
                    take(l, j, yT[:, m, :])
                for i, t in enumerate(tiles(l)):
                    act.wait_ge(oT_done[l], i + 1)
                    link(nc.scalar.activation(junk, bank(2 * (i % 2), 2), ACT.Square, accum_out=ss2[:, t:t + 1]))
                    nc.scalar.activation(rstd2[:, t:t + 1], ss2[:, t:t + 1], ACT.Sqrt, scale=1.0 / DM,
                                         bias=eps_col[:, 0:1]).then_inc(osd_done[l], 1)

        @block.vector
        def _(dve):
            chain = [0]

            def link(ins):
                chain[0] += 1
                ins.then_inc(dve_chain, 1)
                dve.wait_ge(dve_chain, chain[0])

            TT, TS, STT = nc.vector.tensor_tensor, nc.vector.tensor_scalar, nc.vector.scalar_tensor_tensor
            nc.vector.memset(eps_col[:], EPS).then_inc(eps_ok, 1)

            def ada_take(l, b):
                dve.wait_ge(ada_mm[l], b + 1)
                nc.vector.tensor_copy(mod[:, l, b, :], bank(7)[:, 0:2]).then_inc(ada_taken[l], 1)

            def finish_mod(l):
                dve.wait_ge(ada_taken[l], NADA)
                link(TT(mod[:, l], mod[:, l], bada[:, l].unsqueeze(2).broadcast_to([P, NADA, 2]), ALU.add))
                for v in range(2):
                    STT(mod[:, l, KC:2 * KC, v], mod[:, l, KC:2 * KC, v], 1.0, gpre[:, l], ALU.add, ALU.mult)
                    last = TT(mod[:, l, 2 * KC:, v], mod[:, l, 2 * KC:, v], gpost[:, l], ALU.mult)
                link(last)
                dve.sem_inc(mod_ready[l], 1)

            def norm_rstd(l, t):
                dve.wait_ge(sd_done[l], t + 1)
                nc.vector.reciprocal(rstd[:, t:t + 1], rstd[:, t:t + 1]).then_inc(rstd_ok[l], 1)

            def norm_mod(l, t):
                v = 1 if t < CT else 0
                dve.wait_ge(xnT_done[l], t + 1)
                if t >= 2:
                    dve.wait_ge(hlo_ready[l], t - 1)
                src = bank(4 + 2 * (t % 2), 2).rearrange("p (k c) -> p k c", k=KC)
                TT(h32[t % 2], src, mod[:, l, KC:2 * KC, v].unsqueeze(2).broadcast_to([P, KC, P]), ALU.mult).then_inc(xnT_taken[l], 1)
                dve.wait_ge(xnT_taken[l], t + 1)
                TT(h32[t % 2], h32[t % 2], mod[:, l, 0:KC, v].unsqueeze(2).broadcast_to([P, KC, P]),
                   ALU.add).then_inc(h32_ready[l], 1)

            dve.wait_ge(consts, 16 * 16)
            dve.wait_ge(aneg_ok, 1)
            link(TS(alog[:], alog[:], -1.0, None, ALU.mult))
            for b in range(NADA):
                ada_take(0, b)
                if b % 8 == 7 and b // 8 < 2:
                    norm_rstd(0, b // 8)
            finish_mod(0)

            for l in range(DEPTH):
                aux = [0]

                def aux_wait():
                    dve.wait_ge(aux_done[l], aux[0] + 1)
                    b = bank(6 + aux[0] % 2)
                    aux[0] += 1
                    return b

                for t in range(NT):
                    if l or t >= 2:
                        norm_rstd(l, t)
                    if t >= 1:
                        norm_mod(l, t - 1)
                norm_mod(l, NT - 1)

                dve.wait_ge(wdt_loaded[l], 16)
                link(nc.vector.tensor_copy(wdtHi[:], wdt[:]))
                TT(wdtLo[:], wdt[:], wdtHi[:].bitcast(F32), ALU.subtract).then_inc(wdt_split[l], 1)

                raw = aux_wait()
                bias = dtb[:, l].rearrange("p (d h) -> p d h", d=2).unsqueeze(2).broadcast_to([P, 2, NT, SH])
                v4 = lambda x: x.rearrange("p (d c h) -> p d c h", d=2, c=NT)
                link(TT(v4(s_t0), v4(raw[:, 0:80]), bias, ALU.add))
                dve.sem_inc(aux_taken[l], 1)
                link(TS(s_t1, s_t0, -1.0, None, ALU.mult))
                TT(s_t1, s_t0, s_t1, ALU.max).then_inc(dt_abs[l], 1)
                dve.wait_ge(dt_exp[l], 1)
                link(TS(s_dt, s_t1, 2.0, None, ALU.add))
                link(nc.vector.reciprocal(s_dt, s_dt))
                link(TT(s_t1, s_t1, s_dt, ALU.mult))
                link(TT(s_dt, s_t1, s_t1, ALU.mult))
                link(TS(s_we, s_dt, 1.0 / 17, None, ALU.mult))
                for k in range(7, 0, -1):
                    link(STT(s_we, s_we, 1.0 / (2 * k + 1), s_dt, ALU.add, ALU.mult))
                link(STT(s_we, s_we, 1.0, s_t1, ALU.add, ALU.mult))
                link(TS(s_t0, s_t0, 0.0, None, ALU.max))
                link(STT(s_dt, s_we, 2.0, s_t0, ALU.mult, ALU.add))
                an = alog[:, l].rearrange("p (d h) -> p d h", d=2).unsqueeze(2).broadcast_to([P, 2, NT, SH])
                TT(v4(s_t0), v4(s_dt), an, ALU.mult).then_inc(da_ready[l], 1)
                cs = aux_wait()
                nc.vector.tensor_copy(s_ac, cs[:, 0:80]).then_inc(aux_taken[l], 1)
                dve.wait_ge(aux_taken[l], 2)
                dve.sem_inc(acs_ready[l], 1)

                def gated_conv(j2):
                    dve.wait_ge(proj_taken[l], 4 * j2 + 4)
                    u = ubuf[0]
                    o = 0 if l < DEPTH - 1 else CTX
                    if o == 0:
                        TT(u[:, 1:1 + CTX], gin[:, 0:CTX], gc[:, 0:CTX], ALU.mult)
                    link(TT(u[:, 2 + CTX:2 + T], gin[:, CTX:T], gc[:, CTX:T], ALU.mult))
                    conv_taps(u, caw[:, l, j2], None, o)
                    link(TT(cv[:, o:T], cv[:, o:T], gb[:, o:T], ALU.mult))
                    TT(yT[:, j2, o:T], cv[:, o:T], gz[:, o:T], ALU.mult).then_inc(convA_done[l], 1)
                    dve.wait_ge(convA_done[l], j2 + 1)

                def conv_taps(u, w, b, o):
                    spans = ([(0, 0, CTX)] if o == 0 else []) + [(CTX, CTX + 1, SEQ)]
                    for a, s, n in spans:
                        if b is None:
                            last = TS(cv[:, a:a + n], u[:, s:s + n], w[:, 0:1], None, ALU.mult)
                        else:
                            last = TS(cv[:, a:a + n], u[:, s:s + n], w[:, 0:1], b, ALU.mult, ALU.add)
                    link(last)
                    for k in (1, 2):
                        for a, s, n in spans:
                            last = STT(cv[:, a:a + n], u[:, s + k:s + k + n], w[:, k:k + 1], cv[:, a:a + n],
                                       ALU.mult, ALU.add)
                        if k == 1:
                            link(last)
                    if b is None:
                        link(last)
                    return last

                for u in ubuf:
                    for a in (0, 1 + CTX, 2 + T):
                        last = nc.vector.memset(u[:, a:a + 1], 0.0)
                link(last)
                gated_conv(0)
                ends = aux_wait()
                nc.vector.tensor_copy(s_de, ends[:, 0:80]).then_inc(aux_taken[l], 1)
                dve.wait_ge(aux_taken[l], 3)
                link(TT(s_we, s_de, s_ac, ALU.subtract))
                link(TS(s_we, s_we, 0.0, None, ALU.min))
                dve.sem_inc(small_in[l], 1)
                gated_conv(1)
                dve.wait_ge(small_exp[l], 1)
                link(TT(s_we, s_we, s_dt, ALU.mult))

                def conv(j):
                    dve.wait_ge(proj_taken[l], j + 1)
                    if j >= 9:
                        dve.wait_ge(silu_done[l], j - 8)
                    o = 0 if len(chunks(l, j)) == 3 else CTX
                    conv_taps(ubuf[j % 2], cw[:, l, j - 8], cw[:, l, j - 8, 3:4], o).then_inc(conv_done[l], 1)

                def rope(j):
                    dst = {8: CTt[0], 9: CTt[1], 10: BTt[0], 11: BTt[1]}[j]
                    if j == 8:
                        dve.wait_ge(rope_loaded[l], 32)
                    for h in range(2):
                        rot = aux_wait()
                        c = slice(CTX + 512 * h, CTX + 512 * h + 512)
                        f = slice(512 * h, 512 * h + 512)
                        TT(rtmp, rot, sinT[:, f], ALU.mult).then_inc(aux_taken[l], 1)
                        dve.wait_ge(aux_taken[l], aux[0])
                        link(TT(dst[:, c], dst[:, c], cosT[:, f], ALU.mult))
                        last = TT(dst[:, c], dst[:, c], rtmp, ALU.add)
                        if h == 0:
                            link(last)
                    last.then_inc(rope_done[l], 1)
                    dve.wait_ge(rope_done[l], j - 7)

                def to_tok(dst, ts):
                    for r in rounds(ts):
                        b = aux_wait()
                        nc.vector.tensor_copy(dst(r[0], r[-1] + 1), b[:, 0:P * len(r)].rearrange("p (c n) -> p c n", n=P)).then_inc(aux_taken[l], 1)
                        dve.wait_ge(aux_taken[l], aux[0])

                allt = list(range(NT))
                conv(8)
                conv(9)
                rope(8)
                conv(10)
                rope(9)
                conv(11)
                rope(10)
                conv(12)
                rope(11)
                to_tok(lambda a, b: btok[:, a:b, 0, :], allt)
                to_tok(lambda a, b: btok[:, a:b, 1, :], allt)
                to_tok(lambda a, b: xtok[:, a:b, 0:P], allt)
                conv(13)
                to_tok(lambda a, b: xtok[:, a:b, P:2 * P], allt)
                to_tok(lambda a, b: ztok[:, a:b, 0:P], tiles(l))
                to_tok(lambda a, b: ztok[:, a:b, P:2 * P], tiles(l))

                nc.vector.memset(prevb[:, BO[0], :], 0.0)
                link(nc.vector.memset(prevf[0], 0.0))

                def xwb(i):
                    if i >= 2:
                        dve.wait_ge(aux_done[l], aux[0])
                    c = BO[i]
                    TT(by_head(xp[i % 2]), by_head(xtok[:, c, :]), hb(dth(s_we, 1, c), SP_), ALU.mult).then_inc(xwb_ready[l], 1)

                xwb(0)
                for i in range(NT - 1):
                    if i + 1 < NT - 1:
                        xwb(i + 1)
                    c, nxt = BO[i], BO[i + 1]
                    link(TT(by_head(prevb[:, nxt, :]), by_head(prevb[:, c, :]), hb(dth(s_de, 1, c), SP_), ALU.mult))
                    b = aux_wait()
                    TT(prevb[:, nxt, :], prevb[:, nxt, :], b[:, 0:256], ALU.add).then_inc(aux_taken[l], 1)
                    dve.wait_ge(aux_taken[l], aux[0])

                ys = tiles(l)

                def decay(i):
                    c = ys[i]
                    for d in range(2):
                        if i >= 2:
                            dve.wait_ge(yd_done[l], i - 1)
                        dve.wait_ge(bc_done[l], 2 * i + d + 1)
                        for h in range(SH):
                            last = TS(Ed[i % 2][d][:, h, :], bank(1 + d)[:, P * h:P * h + P],
                                      dth(s_ac, d, c)[:, h:h + 1], 0.0, ALU.subtract, ALU.min)
                        last.then_inc(sub_ready[l], 1)

                decay(0)
                for c in range(NT):
                    yi = c - ys[0]
                    x_c = by_head(xtok[:, c, :])
                    if yi >= 1:
                        dve.wait_ge(yd_done[l], yi)
                    if c >= 1:
                        dve.wait_ge(stf_done[l], c)
                    if yi >= 0:
                        for d in range(2):
                            TT(by_head(xp[d]), x_c, hb(dth(s_dt, d, c), SP_), ALU.mult)
                    if c < NT - 1:
                        link(TT(by_head(xw), x_c, hb(dth(s_we, 0, c), SP_), ALU.mult))
                    else:
                        link(TT(by_head(yxd), x_c, hb(dsk[:, l], SP_), ALU.mult))
                    dve.sem_inc(xp_ready[l], 1)
                    if yi >= 0:
                        if yi + 1 < len(ys):
                            decay(yi + 1)
                        dve.wait_ge(g_done[l], yi + 1)
                        gsrc = bank(0)[:, 0:256].rearrange("p (g i) -> p g i", g=SG)
                        TT(GM[0], gsrc, maskF[:].unsqueeze(1).broadcast_to([P, SG, P]), ALU.mult)
                        link(TT(GM[1], gsrc, maskB[:].unsqueeze(1).broadcast_to([P, SG, P]), ALU.mult))
                        dve.sem_inc(g_taken[l], 1)
                        for d in range(2):
                            dve.wait_ge(exp_ready[l], 2 * yi + d + 1)
                            e = Ed[yi % 2][d].rearrange("p (g r) i -> p g r i", g=SG)
                            last = TT(e, e, GM[d].unsqueeze(2).broadcast_to([P, SG, SH // SG, P]), ALU.mult)
                        link(last)
                        dve.sem_inc(mix_ready[l], 1)
                        dve.wait_ge(yo_done[l], yi + 1)
                        yo = bank(4)
                        TT(by_head(yacc), by_head(yo[:, 0:256]), hb(dth(s_ea, 0, c), SP_), ALU.mult)
                        link(TT(by_head(yt2), by_head(yo[:, 256:512]), hb(dth(s_ea, 1, c), SP_), ALU.mult))
                        dve.sem_inc(yo_taken[l], 1)
                        link(TT(yacc, yacc, yt2, ALU.add))
                        if c < NT - 1:
                            link(TT(by_head(yxd), x_c, hb(dsk[:, l], SP_), ALU.mult))
                        link(TT(yacc, yacc, yxd, ALU.add))
                    if c < NT - 1:
                        nf = prevf[(c + 1) % 2]
                        link(TT(by_head(nf), by_head(prevf[c % 2]), hb(dth(s_de, 0, c), SP_), ALU.mult))
                        dve.wait_ge(stf_done[l], c + 1)
                        link(TT(nf, nf, bank(5)[:, 0:256], ALU.add))
                        dve.sem_inc(prevf_ready[l], 1)
                    if yi >= 0:
                        dve.wait_ge(yd_done[l], yi + 1)
                        link(TT(yacc, yacc, bank(3)[:, 0:256], ALU.add))
                        TT(ztok[:, c, :], ztok[:, c, :], yacc, ALU.mult).then_inc(y_gated[l], 1)
                a = ys[0]
                dve.wait_ge(ysq_done[l], 1)
                link(nc.vector.reciprocal(rstd[:, a:NT], rstd[:, a:NT]))
                TT(ztok[:, a:NT, :], ztok[:, a:NT, :], rstd[:, a:NT].unsqueeze(2).broadcast_to([P, NT - a, 256]),
                   ALU.mult).then_inc(yn_ready[l], 1)
                for j in range(2):
                    for r in rounds(ys):
                        b = aux_wait()
                        TS(yT[:, 6 + j, P * r[0]:P * (r[-1] + 1)], b[:, 0:P * len(r)], nrmw[:, l, j:j + 1], None,
                           ALU.mult).then_inc(aux_taken[l], 1)
                dve.wait_ge(aux_taken[l], aux[0])
                dve.sem_inc(yss_done[l], 1)

                steps = [(t, e) for t in tiles(l) for e in range(2)]
                n = len(steps)
                aux0 = aux[0]
                assert aux0 == aux_before_attention(l)

                pair_links = 2 + sum(3 if t >= CT else 2 for t, e in steps)
                linked = [0]

                def link_pair(hp, ins):
                    linked[0] += 1
                    ins.then_inc(pair_chain[l], 1)
                    dve.wait_ge(pair_chain[l], hp * pair_links + linked[0])

                def row_max(hp, i):
                    t, e = steps[i]
                    s = i % 2
                    dve.wait_ge(s_done[l], hp * n + i + 1)
                    sc = PS[:, 1024 * s:1024 * s + 1024]
                    top = nc.vector.tensor_reduce(mx[s][:, 0:1], sc[:, 576:832], AX_X, ALU.max)
                    if t >= CT:
                        r0, nr, first = window(t - CT)
                        tab = tabI[e] if nr == 9 else tabF[e][:, :, first:first + 8]
                        link_pair(hp, nc.vector.tensor_tensor_reduce(
                            out=Pr[s][:, 0:64 * nr].rearrange("p (r k) -> p r k", k=64),
                            in0=sc[:, 0:64 * nr].rearrange("p (r k) -> p r k", k=64),
                            in1=tab.rearrange("p k r -> p r k")[:, :, ::-1], scale=1.0, scalar=BIG,
                            op0=ALU.add, op1=ALU.max, accum_out=mx[s][:, 1:2]))
                        TS(mx[s][:, 1:2], mx[s][:, 1:2], mx[s][:, 0:1], -1.0, ALU.max,
                           ALU.mult).then_inc(nm_ready[l], 1)
                    else:
                        link_pair(hp, top)
                        TS(mx[s][:, 1:2], mx[s][:, 0:1], -1.0, None, ALU.mult).then_inc(nm_ready[l], 1)

                def out_rows(hp, i):
                    t, e = steps[i]
                    s = i % 2
                    if t >= CT:
                        link_pair(hp, TT(sums[i % 4][:, 2:3], sums[i % 4][:, 0:1], sums[i % 4][:, 1:2], ALU.add))
                        link_pair(hp, nc.vector.reciprocal(sums[i % 4][:, 3:4], sums[i % 4][:, 2:3]))
                    else:
                        link_pair(hp, nc.vector.reciprocal(sums[i % 4][:, 3:4], sums[i % 4][:, 1:2]))
                    dve.wait_ge(o_done[l], hp * n + i + 1)
                    TS(ysb[(i // 2) % 2][:, 64 * e:64 * e + 64], bank(6)[:, 64 * e:64 * e + 64], sums[i % 4][:, 3:4],
                       None, ALU.mult).then_inc(o_taken[l], 1)

                def gate_rows(hp, k):
                    t = tiles(l)[k]
                    dve.wait_ge(yna_done[l], hp * (n // 2) + k + 1)
                    TT(yna(hp)[:, P * t:P * t + P], bank(7)[:, 128:256], zT[:, P * t:P * t + P],
                       ALU.mult).then_inc(yna_taken[l], 1)

                def yna(hp):
                    return yT[:, bass.ds(hp + 2, 1), :].rearrange("p a b -> p (a b)")

                dve.sem_inc(o_taken[l], 1)
                dve.sem_inc(yna_taken[l], 1)
                with dve.Fori(0, PAIRS) as hp:
                    for r, ts in enumerate(rounds(allt)):
                        dve.wait_ge(aux_done[l], 3 * hp + (aux0 + r + 1))
                        b = bank(6 + r % 2)
                        nc.vector.tensor_copy(vtok[:, ts[0]:ts[-1] + 1, :], b[:, 0:P * len(ts)].rearrange("p (c n) -> p c n", n=P)).then_inc(aux_taken[l], 1)
                    dve.wait_ge(tab_loaded[l], 64 * hp + 64)
                    for e in range(2):
                        cm = colmask[:].unsqueeze(2)
                        last = TT(tabF[e], tabF[e], cm.broadcast_to([P, GRID_W, TW]), ALU.add)
                    link_pair(hp, last)
                    for e in range(2):
                        last = TT(tabI[e], tabF[e][:, :, 3:12],
                                  rowmask[:].unsqueeze(1).broadcast_to([P, GRID_W, WIN_H + 1]), ALU.add)
                    link_pair(hp, last)
                    row_max(hp, 0)
                    row_max(hp, 1)
                    for i in range(n):
                        dve.wait_ge(pT_done[l], hp * n + i + 1)
                        if steps[i][0] >= CT:
                            nc.vector.tensor_copy(PT[i % 2][:, 0:512], bank(4)).then_inc(ptA_ready[l], 1)
                        else:
                            dve.sem_inc(ptA_ready[l], 1)
                        if i + 2 < n:
                            row_max(hp, i + 2)
                        if i >= 2 and i % 2 == 0:
                            gate_rows(hp, i // 2 - 1)
                        out_rows(hp, i)
                        if l + 1 < DEPTH and i % 2 == 0 and i < 12:
                            dve.wait_ge(ada_mm[l + 1], 6 * hp + (i // 2 + 1))
                            nc.vector.tensor_copy(mod[:, l + 1, bass.ds(6 * hp + i // 2, 1), :].rearrange("p a b -> p (a b)"), bank(7)[:, 0:2]).then_inc(ada_taken[l + 1], 1)
                    gate_rows(hp, n // 2 - 1)
                    assert linked[0] == pair_links
                if l + 1 < DEPTH:
                    finish_mod(l + 1)

                o = 0 if l < DEPTH - 1 else CTX
                dve.wait_ge(yna_taken[l], PAIRS * (n // 2) + 1)
                for k in range(KC):
                    dve.wait_ge(yhi_ready[l], k + 1)
                    TT(hLo[:, k, o:T], yT[:, k, o:T], hHi[:, k, o:T].bitcast(F32), ALU.subtract).then_inc(ylo_ready[l], 1)
                for v in range(2 if l < DEPTH - 1 else 1):
                    dve.wait_ge(gb_done[l], v + 1)
                    nc.vector.tensor_copy(gbc[v], bank(6, 2)).then_inc(gb_taken[l], 1)
                dve.wait_ge(gb_taken[l], 2 if l < DEPTH - 1 else 1)
                for i, t in enumerate(tiles(l)):
                    dve.wait_ge(osd_done[l], i + 1)
                    link(nc.vector.reciprocal(rstd2[:, t:t + 1], rstd2[:, t:t + 1]))
                    if i >= 2:
                        dve.wait_ge(stored[i % 2], stores(l, i - 2))
                    STT(osb[i % 2], bank(2 * (i % 2), 2), rstd2[:, t:t + 1], gbc[1 if t < CT else 0],
                        ALU.mult, ALU.mult).then_inc(o_ready[l], 1)

        @block.tensor
        def _(pe):
            mm, tp = nc.tensor.matmul, nc.tensor.transpose

            def ada(l, b):
                pe.wait_ge(ada_loaded[b % 2], 16 * (b // 2 + 1))
                if b:
                    pe.wait_ge(ada_taken[l], b)
                for k in range(KC):
                    last = mm(bank(7)[:, 0:2], adaw[b % 2][:, k, :], ccol[:, k, :], start=(k == 0), stop=(k == KC - 1))
                last.then_inc(ada_mm[l], 1)

            def proj_mm(l, j, s):
                for ci, (a, n) in enumerate(CHUNKS):
                    if (a, n) not in chunks(l, j):
                        continue
                    out = PS[:, slot_cols(s) + a:slot_cols(s) + a + n]
                    k3 = [(w, x, k) for k in range(KC) for w, x in ((whi, hHi), (whi, hLo), (wlo, hHi))]
                    for q, (w, x, k) in enumerate(k3):
                        last = mm(out, w[s][:, k, :], x[:, k, a:a + n], start=(q == 0), stop=(q == len(k3) - 1))
                return last

            def proj(l, j):
                pe.wait_ge(w_split[l], j + 1)
                if j >= 2:
                    pe.wait_ge(proj_taken[l], j - 1)
                proj_mm(l, j, j % 2).then_inc(proj_done[l], 1)

            pe.wait_ge(consts, 16 * 16)
            pe.wait_ge(silu_c, 1)
            for b in range(NADA):
                ada(0, b)
            pe.wait_ge(ada_taken[0], NADA)

            for l in range(DEPTH):
                aux = [0]

                def aux_open():
                    if aux[0] >= 2:
                        pe.wait_ge(aux_taken[l], aux[0] - 1)
                    return bank(6 + aux[0] % 2)

                def aux_close(last):
                    aux[0] += 1
                    last.then_inc(aux_done[l], 1)

                for t in range(NT):
                    pe.wait_ge(xn_ready[l], t + 1)
                    if l and t == 0:
                        pe.wait_ge(gb_taken[l - 1], 2)
                    if t >= 2:
                        pe.wait_ge(xnT_taken[l], t - 1)
                    for k in range(KC):
                        last = tp(bank(4 + 2 * (t % 2), 2)[:, P * k:P * k + P], xt[t % 3][:, P * k:P * k + P], ident[:])
                    last.then_inc(xnT_done[l], 1)

                pe.wait_ge(xnT_taken[l], NT)
                pe.wait_ge(hhi_ready[l], NT)
                pe.wait_ge(hlo_ready[l], NT)
                pe.wait_ge(wdt_split[l], 1)
                if l:
                    pe.wait_ge(o_ready[l - 1], len(tiles(l - 1)))
                b = aux_open()
                for c in range(NT):
                    out = b[:, 0:80].rearrange("p (d c h) -> p d c h", d=2, c=NT)[:, :, c, :]
                    k3 = [(w, x, k) for k in range(KC) for w, x in ((wdtHi, hHi), (wdtHi, hLo), (wdtLo, hHi))]
                    for q, (w, x, k) in enumerate(k3):
                        last = mm(out, x[:, k, P * c:P * c + P], w[:, k, :].rearrange("p (d h) -> p d h", d=2),
                                  start=(q == 0), stop=(q == len(k3) - 1))
                aux_close(last)
                proj(l, 0)
                proj(l, 1)
                pe.wait_ge(da_ready[l], 1)
                b = aux_open()
                mm(b[:, 0:40], maskF[:], s_t0[:, 0:40], start=True, stop=True)
                aux_close(mm(b[:, 40:80], maskB[:], s_t0[:, 40:80], start=True, stop=True))
                proj(l, 2)
                proj(l, 3)
                pe.wait_ge(acs_ready[l], 1)
                b = aux_open()
                mm(b[:, 0:40], ident[:, P - 1:P].broadcast_to([P, P]), s_ac[:, 0:40], start=True, stop=True)
                aux_close(mm(b[:, 40:80], ident[:, 0:1].broadcast_to([P, P]), s_ac[:, 40:80], start=True, stop=True))
                for j in range(4, 10):
                    proj(l, j)

                def rot(j):
                    src = {8: CTt[0], 9: CTt[1], 10: BTt[0], 11: BTt[1]}[j]
                    pe.wait_ge(silu_done[l], j - 7)
                    for h in range(2):
                        b = aux_open()
                        aux_close(mm(b, perm[:], src[:, CTX + 512 * h:CTX + 512 * h + 512], start=True, stop=True))

                def to_tok(src, ts):
                    for r in rounds(ts):
                        b = aux_open()
                        for i, c in enumerate(r):
                            last = tp(b[:, P * i:P * i + P], src[:, P * c:P * c + P], ident[:])
                        aux_close(last)

                allt = list(range(NT))
                rot(8)
                proj(l, 10)
                rot(9)
                proj(l, 11)
                rot(10)
                proj(l, 12)
                rot(11)
                pe.wait_ge(rope_done[l], 4)
                to_tok(BTt[0], allt)
                proj(l, 13)
                to_tok(BTt[1], allt)
                pe.wait_ge(silu_done[l], 5)
                to_tok(cv, allt)
                proj(l, 14)
                pe.wait_ge(silu_done[l], 6)
                to_tok(cv, allt)
                proj(l, 15)
                pe.wait_ge(proj_taken[l], 16)
                to_tok(ubuf[0], tiles(l))
                to_tok(ubuf[1], tiles(l))

                for i in range(NT - 1):
                    c = BO[i]
                    pe.wait_ge(xwb_ready[l], i + 1)
                    b = aux_open()
                    for g in range(SG):
                        last = mm(b[:, P * g:P * g + P], btok[:, c, g, :], xp[i % 2][:, P * g:P * g + P],
                                  start=True, stop=True)
                    aux_close(last)
                pe.wait_ge(aux_taken[l], aux[0])

                ys = tiles(l)

                def ssd_front(i):
                    c = ys[i]
                    for d in range(2):
                        if i:
                            pe.wait_ge(sub_ready[l], 2 * (i - 1) + d + 1)
                        for h in range(SH):
                            a = 40 * d + 4 * c + h
                            last = tp(bank(1 + d)[:, P * h:P * h + P], s_ac[:, a:a + 1].broadcast_to([P, P]), ident[:])
                        last.then_inc(bc_done[l], 1)
                    if i:
                        pe.wait_ge(g_taken[l], i)
                    for g in range(SG):
                        last = mm(bank(0)[:, P * g:P * g + P], BTt[g][:, P * c:P * c + P], CTt[g][:, P * c:P * c + P],
                                  start=True, stop=True)
                    last.then_inc(g_done[l], 1)

                ssd_front(0)
                for c in range(NT):
                    yi = c - ys[0]
                    pe.wait_ge(xp_ready[l], c + 1)
                    if yi >= 0:
                        if yi + 1 < len(ys):
                            ssd_front(yi + 1)
                    if c:
                        pe.wait_ge(prevf_ready[l], c)
                    if c < NT - 1:
                        for g in range(SG):
                            last = mm(bank(5)[:, P * g:P * g + P], btok[:, c, g, :], xw[:, P * g:P * g + P],
                                      start=True, stop=True)
                        last.then_inc(stf_done[l], 1)
                    if yi >= 0:
                        if yi:
                            pe.wait_ge(yo_taken[l], yi)
                        for d, prev in enumerate([prevf[c % 2], prevb[:, c, :]]):
                            for g in range(SG):
                                last = mm(bank(4)[:, 256 * d + P * g:256 * d + P * g + P], CTt[g][:, P * c:P * c + P],
                                          prev[:, P * g:P * g + P], start=True, stop=True)
                        last.then_inc(yo_done[l], 1)
                        pe.wait_ge(mix_ready[l], yi + 1)
                        if yi:
                            pe.wait_ge(y_gated[l], yi)
                        for h in range(SH):
                            for d in range(2):
                                last = mm(bank(3)[:, SP_ * h:SP_ * h + SP_], Ed[yi % 2][d][:, h, :],
                                          xp[d][:, SP_ * h:SP_ * h + SP_], start=(d == 0), stop=(d == 1))
                        last.then_inc(yd_done[l], 1)
                pe.wait_ge(yn_ready[l], 1)
                for j in range(2):
                    for r in rounds(ys):
                        b = aux_open()
                        for i, c in enumerate(r):
                            last = tp(b[:, P * i:P * i + P], ztok[:, c, P * j:P * j + P], ident[:])
                        aux_close(last)
                pe.wait_ge(aux_taken[l], aux[0])

                steps = [(t, e) for t in tiles(l) for e in range(2)]
                n = len(steps)
                aux0 = aux[0]
                assert aux0 == aux_before_attention(l)

                def scores(i):
                    t, e = steps[i]
                    s = i % 2
                    rows = slice(64 * e, 64 * e + 64)
                    q = qT[rows, P * t:P * t + P]
                    if t >= CT:
                        r0, nr, _ = window(t - CT)
                        k0 = CTX + 64 * r0
                        mm(bank(2 * s)[:, 0:512], q, kT[rows, k0:k0 + 512], start=True, stop=True)
                        if nr == 9:
                            mm(bank(2 * s + 1)[:, 0:64], q, kT[rows, k0 + 512:k0 + 576], start=True, stop=True)
                    mm(bank(2 * s + 1)[:, 64:320], q, kT[rows, 0:CTX], start=True, stop=True).then_inc(s_done[l], 1)

                def flip(hp, i):
                    t, e = steps[i]
                    s = i % 2
                    pe.wait_ge(p_ready[l], hp * n + i + 1)
                    if t >= CT:
                        for m in range(4):
                            tp(bank(4)[:, P * m:P * m + P], Pr[s][:, P * m:P * m + P], ident[:])
                        if window(t - CT)[1] == 9:
                            tp(bank(5)[0:64, 0:P], Pr[s][:, 512:576], ident[:])
                    for m in range(2):
                        last = tp(bank(5)[:, P * (m + 1):P * (m + 2)], Pr[s][:, 576 + P * m:704 + P * m], ident[:])
                    last.then_inc(pT_done[l], 1)

                def values(hp, i):
                    t, e = steps[i]
                    s = i % 2
                    out = bank(6)[:, 64 * e:64 * e + 64]
                    pe.wait_ge(ptA_ready[l], hp * n + i + 1)
                    pe.wait_ge(ptB_ready[l], hp * n + i + 1)
                    pe.wait_ge(o_taken[l], hp * n + i + 1)
                    parts = [(PT[s][:, 640 + P * m:768 + P * m], vtok[:, m, 64 * e:64 * e + 64]) for m in range(2)]
                    if t >= CT:
                        r0, nr, _ = window(t - CT)
                        kt = CT + r0 // 2
                        parts += [(PT[s][:, P * m:P * m + P], vtok[:, kt + m, 64 * e:64 * e + 64]) for m in range(4)]
                        if nr == 9:
                            parts.append((PT[s][0:64, 512:640], vtok[0:64, kt + 4, 64 * e:64 * e + 64]))
                    for m, (a, b) in enumerate(parts):
                        last = mm(out, a, b, start=(m == 0), stop=(m == len(parts) - 1))
                    last.then_inc(o_done[l], 1)

                def y_turn(hp, k, ada_n):
                    pe.wait_ge(o_taken[l], hp * n + 2 * k + 2 + 1)
                    pe.wait_ge(yna_taken[l], hp * (n // 2) + k + 1)
                    if ada_n is not None:
                        pe.wait_ge(ada_taken[l + 1], 6 * hp + ada_n)
                    tp(bank(7)[:, P:2 * P], ysb[k % 2], ident[:]).then_inc(yna_done[l], 1)

                with pe.Fori(0, PAIRS) as hp:
                    for i in range(4):
                        j = Q0 + i
                        pe.wait_ge(w_split[l], 4 * hp + (j + 1))
                        pe.wait_ge(proj_taken[l], 4 * hp + (j - 1))
                        proj_mm(l, j, j % 2).then_inc(proj_done[l], 1)
                    pe.wait_ge(proj_taken[l], 4 * hp + (Q0 + 4))
                    pe.wait_ge(yna_taken[l], hp * (n // 2) + 1)
                    for r, ts in enumerate(rounds(allt)):
                        if r == 2:
                            pe.wait_ge(aux_taken[l], 3 * hp + (aux0 + 1))
                        for i, c in enumerate(ts):
                            last = tp(bank(6 + r % 2)[:, P * i:P * i + P], vT[:, P * c:P * c + P], ident[:])
                        last.then_inc(aux_done[l], 1)
                    scores(0)
                    scores(1)
                    pe.wait_ge(aux_taken[l], 3 * hp + (aux0 + 3))
                    for i in range(n):
                        flip(hp, i)
                        if i + 2 < n:
                            scores(i + 2)
                        if i >= 2 and i % 2 == 0:
                            y_turn(hp, i // 2 - 1, min(i // 2, 6) if l + 1 < DEPTH else None)
                        values(hp, i)
                        if l + 1 < DEPTH and i % 2 == 0 and i < 12:
                            b = i // 2
                            pe.wait_ge(ada_loaded[b % 2], 48 * hp + 16 * ((l + 1) * (NADA // 2) + b // 2 + 1))
                            if i:
                                pe.wait_ge(yna_taken[l], hp * (n // 2) + i // 2 + 1)
                            for k in range(KC):
                                last = mm(bank(7)[:, 0:2], adaw[b % 2][:, k, :], ccol[:, k, :], start=(k == 0), stop=(k == KC - 1))
                            last.then_inc(ada_mm[l + 1], 1)
                    y_turn(hp, n // 2 - 1, 6 if l + 1 < DEPTH else None)

                pe.wait_ge(yna_taken[l], PAIRS * (n // 2) + 1)
                pe.wait_ge(ylo_ready[l], KC)
                for v in range(2 if l < DEPTH - 1 else 1):
                    if v:
                        pe.wait_ge(gb_taken[l], v)
                    for k in range(KC):
                        last = tp(bank(6, 2)[:, P * k:P * k + P], mod[:, l, 2 * KC + k, v:v + 1].broadcast_to([P, P]), ident[:])
                    last.then_inc(gb_done[l], 1)
                for j in range(NB_IN, NB):
                    proj(l, j)
                pe.wait_ge(proj_taken[l], NB)
                for i, t in enumerate(tiles(l)):
                    if i >= 2:
                        pe.wait_ge(o_ready[l], i - 1)
                    for k in range(KC):
                        last = tp(bank(2 * (i % 2), 2)[:, P * k:P * k + P], yT[:, k, P * t:P * t + P], ident[:])
                    last.then_inc(oT_done[l], 1)


def _constants():
    f = np.float32
    j, i = np.arange(P)[:, None], np.arange(P)[None, :]
    n_freq = SN // 4
    inv_freq = (f(10000.0) ** (-np.arange(n_freq, dtype=f) / f(n_freq))).astype(f)
    pos = np.arange(SEQ)
    ang_r = (pos // GRID_W).astype(f)[None, :] * inv_freq[:, None]
    ang_c = (pos % GRID_W).astype(f)[None, :] * inv_freq[:, None]
    ang = np.concatenate([ang_r, ang_r, ang_c, ang_c]).astype(f)
    perm = np.zeros((P, P), f)
    for base in (0, SN // 2):
        for a in range(n_freq):
            perm[base + n_freq + a, base + a] = -1.0
            perm[base + a, base + n_freq + a] = 1.0
    cols = np.arange(GRID_W)
    lo = np.clip(cols - WIN_W // 2, 0, GRID_W - WIN_W)[:, None]
    inside = (cols[None, :] >= lo) & (cols[None, :] < lo + WIN_W)
    colmask = np.where(np.concatenate([inside, inside])[:, ::-1], 0.0, NEG).astype(f)
    rowmask = np.zeros((P, WIN_H + 1), f)
    rowmask[:GRID_W, WIN_H] = NEG
    rowmask[GRID_W:, 0] = NEG
    return dict(ident=np.eye(P, dtype=f), maskF=(j <= i).astype(f), maskB=(j >= i).astype(f), perm=perm,
                colmask=colmask, rowmask=rowmask, rope_cos=np.cos(ang).astype(f), rope_sin=np.sin(ang).astype(f))


def _layout(x, c, ctx, c_ctx, w_ada, b_ada, g_pre, g_post, w_in, conv_a_w, rpb, ssd_conv_w, ssd_conv_b,
            dt_bias_f, dt_bias_b, a_log_f, a_log_b, ssd_d, ssd_norm_w, w_out):
    def by_channel(a):
        return np.moveaxis(a.reshape(*a.shape[:-1], -1, P), -1, 0)

    def blocks(w):
        return w.reshape(KC, P, -1, P).transpose(2, 1, 0, 3)

    cols = block_columns()
    w_blocks = np.stack([np.concatenate([
        blocks(np.concatenate([w_in[l][:, s:s + P] for s in cols], axis=1)), blocks(w_out[l])]) for l in range(DEPTH)])
    conv_w = np.concatenate([ssd_conv_w, ssd_conv_b[:, None, :]], axis=1)
    conv_w = conv_w.reshape(DEPTH, 4, 6, P)[:, :, [4, 5, 2, 3, 0, 1]].transpose(3, 0, 2, 1)
    table = np.pad(rpb.transpose(0, 1, 3, 2)[:, :, ::-1], ((0, 0), (0, 0), (48, 48), (0, 1)))
    table = np.pad(table, ((0, 0), (0, 0), (1, 0), (0, 0)))
    arrays = dict(
        tokens=np.concatenate([ctx[0], x[0]]),
        ccol=np.stack([by_channel(c[0]), by_channel(c_ctx)], axis=-1),
        w_ada=np.stack([blocks(w_ada[l]) for l in range(DEPTH)]),
        b_ada=by_channel(b_ada), g_pre=by_channel(g_pre), g_post=by_channel(g_post),
        w_blocks=w_blocks,
        w_dt=w_in[:, :, SPLIT_IN[10]:].reshape(DEPTH, KC, P, 8).transpose(0, 2, 1, 3),
        conv_w=conv_w, conv_a=conv_a_w.reshape(DEPTH, 3, 2, P).transpose(3, 0, 2, 1),
        norm_w=by_channel(ssd_norm_w), rpb=table,
        dt_bias=np.concatenate([dt_bias_f, dt_bias_b], axis=1).reshape(-1),
        a_log=np.concatenate([a_log_f, a_log_b], axis=1).reshape(-1),
        ssd_d=ssd_d.reshape(-1))
    return arrays | _constants()


def build(nc, arrays):
    A = {name: nc.dram_tensor(f"in_{name}", a.shape, mybir.dt.from_np(a.dtype), kind="ExternalInput").ap()
         for name, a in arrays.items()}
    A["x_mid"] = nc.dram_tensor("x_mid", (T, DM), F32, kind="Internal").ap()
    A["out"] = nc.dram_tensor("out_x", (SEQ, DM), F32, kind="ExternalOutput").ap()
    trunk(nc, A)


def kernel(**inputs):
    import concourse.bacc as bacc
    from concourse.bass_utils import run_bass_kernel_spmd

    arrays = {k: np.ascontiguousarray(v) for k, v in _layout(**{k: np.asarray(v) for k, v in inputs.items()}).items()}
    nc = bacc.Bacc("TRN2", target_bir_lowering=False, num_devices=1)
    build(nc, arrays)
    r = run_bass_kernel_spmd(nc, [{f"in_{k}": v for k, v in arrays.items()}], core_ids=[0])
    return r.results[0]["out_x"].reshape(1, SEQ, DM)
```

```python
from contextlib import ExitStack

import numpy as np

import concourse.bass as bass
from concourse import mybir

F32 = mybir.dt.float32
F32R = mybir.dt.float32r
ACT = mybir.ActivationFunctionType
ALU = mybir.AluOpType
AX_X = mybir.AxisListType.X

P = 128
DM = 1024
KC = DM // P
SEQ, CTX, DEPTH = 1024, 256, 2
T = CTX + SEQ
NT = T // P
CT = CTX // P
LT = SEQ // P
GRID_W = 64
ROWS = SEQ // GRID_W
EPS = 1e-6
CONV, NA, SSD = 256, 512, 256
HEADS, DH = 8, 64
WIN_H, WIN_W = 8, 16
PAIRS = HEADS // 2
SH, SP_ = 4, 64
SG, SN = 2, 128
SCALE = DH ** -0.5
NEG = -1e30
TW = 16
NB_IN = 32
NB = NB_IN + DM // P
NADA = 3 * DM // P
CHUNKS = [(0, CTX), (CTX, 512), (CTX + 512, 512)]
Q0 = 16
BIG = -3.0e38
N_CONSTS = 15
SPLIT_IN = np.cumsum([0, 256, 256, 256, 256, 512, 512, 512, 512, 768, 256, 8])


def block_columns():
    s_in, s_b, s_c, s_z, q, k, v, z, xbc, ssz, _ = SPLIT_IN[:11]
    cols = []
    for j in range(2):
        cols += [s_in + P * j, s_c + P * j, s_b + P * j, s_z + P * j]
    x, b, c = xbc, xbc + SSD, xbc + SSD + SG * SN
    cols += [c, c + P, b, b + P, x, x + P]
    cols += [ssz, ssz + P]
    for j in range(PAIRS):
        cols += [q + P * j, k + P * j, v + P * j, z + P * j]
    return [int(c) for c in cols]


def window(r):
    r0 = min(max(r - WIN_H // 2, 0), ROWS - WIN_H)
    return r0, r0 - r + WIN_H - 1


def trunk(nc, A):
    ctx = ExitStack()
    with ctx:
        def sb(name, shape, dt=F32):
            return ctx.enter_context(nc.sbuf_tensor(name, shape, dt))

        def sem(name):
            return ctx.enter_context(nc.semaphore(name))

        def sems(name, n=DEPTH):
            return [sem(f"{name}{i}") for i in range(n)]

        hHi = sb("hHi", [P, KC, T], F32R)
        hLo = sb("hLo", [P, KC, T], F32R)
        yT = sb("yT", [P, KC, T])
        wraw = [sb(f"wraw{i}", [P, KC, P]) for i in range(2)]
        whi = [sb(f"whi{i}", [P, KC, P], F32R) for i in range(2)]
        wlo = [sb(f"wlo{i}", [P, KC, P], F32R) for i in range(2)]
        RN = 14848
        R = sb("region", [P, RN])
        ident = sb("ident", [P, P])
        maskF = sb("maskF", [P, P])
        maskB = sb("maskB", [P, P])
        perm = sb("perm", [P, P])
        colmask = sb("colmask", [P, GRID_W])
        ccol = sb("ccol", [P, KC, 2])
        mod = sb("mod", [P, DEPTH, NADA, 2])
        bada = sb("bada", [P, DEPTH, NADA])
        gpre = sb("gpre", [P, DEPTH, KC])
        gpost = sb("gpost", [P, DEPTH, KC])
        cw = sb("cw", [P, DEPTH, 6, 4])
        caw = sb("caw", [P, DEPTH, 2, 3])
        nrmw = sb("nrmw", [P, DEPTH, 2])
        dtb = sb("dtb", [P, DEPTH, 8])
        alog = sb("alog", [P, DEPTH, 8])
        dsk = sb("dsk", [P, DEPTH, SH])
        wdtHi = sb("wdtHi", [P, KC, 8], F32R)
        wdtLo = sb("wdtLo", [P, KC, 8], F32R)
        st = sb("st", [P, 64])
        eps_col = sb("eps_col", [P, 1])
        sm = sb("sm", [P, 5, 80])

        def reg(a, n):
            return R[:, a:a + n]

        junk = reg(6144, DM)
        gbc = [reg(0, DM), reg(DM, DM)]
        xres = [reg(2048 + DM * i, DM) for i in range(2)]
        osb = [reg(4096 + DM * i, DM) for i in range(2)]
        xt = [reg(7168 + DM * i, DM) for i in range(3)]
        h32 = [reg(10240 + DM * i, DM).rearrange("p (k c) -> p k c", k=KC) for i in range(2)]
        adaw = [reg(12800 + DM * i, DM).rearrange("p (k c) -> p k c", k=KC) for i in range(2)]
        yflat = yT[:, :, :].rearrange("p a b -> p (a b)")
        ADA0 = [(0, 2, reg(12800, 2 * DM)), (2, 3, reg(0, 3 * DM)), (5, 3, reg(3 * DM, 3 * DM)),
                (8, 5, yflat[:, 0:5 * DM]), (13, 5, yflat[:, 5 * DM:10 * DM]),
                (18, 3, reg(0, 3 * DM)), (21, 3, reg(3 * DM, 3 * DM))]
        CTt = [reg(T * g, T) for g in range(2)]
        BTt = [reg(2 * T + T * g, T) for g in range(2)]
        xtok = reg(5120, 2560).rearrange("p (c n) -> p c n", c=NT)
        btok = reg(7680, 2560).rearrange("p (c g n) -> p c g n", c=NT, g=SG)
        gin, gc, gb, gz = [reg(5120 + T * i, T) for i in range(4)]
        ubuf = [reg(10240 + 1284 * i, 1284) for i in range(2)]
        cv = reg(12808, T)
        rtmp = reg(14088, 512)
        dtT = cv[0:8, :]
        wdt = reg(12320, 64).rearrange("p (k n) -> p k n", k=KC)
        ztok = yT[:, 2:4, :].rearrange("p a (b n) -> p (a b) n", n=256)
        spare = yT[:, 4:6, :].rearrange("p a b -> p (a b)")
        cosT, sinT = spare[:, 0:1024], spare[:, 1024:2048]
        prevb = reg(10240, 2560).rearrange("p (c n) -> p c n", c=NT)
        Ed = [[reg(12800 + 1024 * s + 512 * d, 512).rearrange("p (h i) -> p h i", h=SH) for d in range(2)]
              for s in range(2)]
        xp = [[spare[:, 512 * d + 256 * s:512 * d + 256 * s + 256] for s in range(2)] for d in range(2)]
        xw = [spare[:, 1024 + 256 * i:1280 + 256 * i] for i in range(2)]
        prevf = [spare[:, 1536 + 256 * i:1792 + 256 * i] for i in range(2)]
        GM = [spare[:, 2048 + 256 * i:2304 + 256 * i].rearrange("p (g i) -> p g i", g=SG) for i in range(2)]
        late = yT[:, 6:8, :].rearrange("p a b -> p (a b)")
        yacc, yt2, yxd = [[late[:, 512 * j + 256 * i:512 * j + 256 * i + 256] for i in range(2)] for j in range(3)]
        qbd = reg(0, 2 * T).rearrange("p (g c) -> p g c", c=P)
        kT, zT = reg(2 * T, T), reg(3 * T, T)
        vtok = reg(4 * T, T).rearrange("p (c n) -> p c n", c=NT)
        vodd = reg(5 * T, P * (LT - 1)).rearrange("p (c n) -> p c n", c=LT - 1)
        tab = reg(7296, 1024).rearrange("p (k r) -> p k r", r=TW)
        Pr = [reg(8320 + 768 * i, 768) for i in range(2)]
        PT = [reg(9856 + 768 * i, 768) for i in range(2)]
        vT = reg(9856, T)
        zr = [reg(11392 + 128 * i, 128) for i in range(2)]
        adarow = [reg(11648 + 128 * i, 128) for i in range(2)]

        ss, rstd = st[:, 0:10], st[:, 10:20]
        ss2, rstd2 = st[:, 20:30], st[:, 30:40]
        mx = [st[:, 40 + 2 * i:42 + 2 * i] for i in range(2)]
        sums = st[:, 44:52].rearrange("p (s u) -> p s u", u=2)
        inv = [st[:, 52 + 2 * i:54 + 2 * i] for i in range(2)]
        s_dt, s_ac, s_ea, s_we, s_de = [sm[:, i, :] for i in range(5)]
        s_t0, s_t1 = reg(14088, 80), reg(14168, 80)

        def dth(x, d, c):
            return x[:, 40 * d + 4 * c:40 * d + 4 * c + 4]

        def hb(x, n):
            return x.unsqueeze(2).broadcast_to([P, SH, n])

        def by_head(x, n=SP_):
            return x.rearrange("p (h n) -> p h n", h=SH)

        PS = ctx.enter_context(nc.psum_tensor("PS", [P, 4096], F32))

        def bank(b, n=1):
            return PS[:, 512 * b:512 * (b + n)]

        def diagonal(b):
            x = b.rearrange("p (h r x) -> p h r x", h=SH, r=2)[:, 0::2, 0, :]
            (pstep, pn), (gstep, gn), (xs, xn) = x.ap
            return bass.AP(tensor=x.tensor, offset=x.offset, ap=[[pstep, pn], [gstep, gn], [P + SP_, 2], [xs, xn]])

        consts = sem("consts")
        silu_c = sem("silu_c")
        dtT_done, dtT_ready = sem("dtT_done"), sem("dtT_ready")
        eps_ok = sem("eps_ok")
        aneg_ok = sem("aneg_ok")
        ada_loaded = sems("ada_loaded", 2)
        ada_first = sems("ada_first", 7)
        ada_mm, ada_taken, mod_ready = sems("ada_mm"), sems("ada_taken"), sems("mod_ready")
        x_loaded = sems("x_loaded", 3)
        rstd_ok, xn_ready = sems("rstd_ok"), sems("xn_ready")
        sd_done = sems("sd_done")
        xnT_done, xnT_taken, h32_ready = sems("xnT_done"), sems("xnT_taken"), sems("h32_ready")
        hhi_ready, hlo_ready = sems("hhi_ready"), sems("hlo_ready")
        w_loaded = sems("w_loaded", 2)
        w_split, proj_done, proj_taken = sems("w_split"), sems("proj_done"), sems("proj_taken")
        wdt_loaded, wdt_split = sem("wdt_loaded"), sem("wdt_split")
        rope_loaded = sems("rope_loaded")
        aux_done, aux_taken = sems("aux_done"), sems("aux_taken")
        dt_abs, dt_exp = sem("dt_abs"), sem("dt_exp")
        small_in, small_exp = sem("small_in"), sem("small_exp")
        da_ready, acs_ready = sem("da_ready"), sem("acs_ready")
        convA_done, conv_done, silu_done, rope_done = (sems("convA_done"), sems("conv_done"),
                                                       sems("silu_done"), sems("rope_done"))
        xwb_ready = sems("xwb_ready")
        g_done, bc_done, g_taken, bc_taken, exp_ready = (sems("g_done"), sems("bc_done"), sems("g_taken"),
                                                          sems("bc_taken"), sems("exp_ready"))
        mix_ready, xp_ready, prevf_ready = sems("mix_ready"), sems("xp_ready"), sems("prevf_ready")
        ssd_in, nf_ready = sem("ssd_in"), sems("nf_ready")
        yo_done, stf_done, yd_done, yo_taken = (sems("yo_done"), sems("stf_done"), sems("yd_done"),
                                                sems("yo_taken"))
        y_gated, ysq_done, yn_ready, yss_done = (sems("y_gated"), sem("ysq_done"), sem("yn_ready"),
                                                 sem("yss_done"))
        tab_loaded = sems("tab_loaded")
        s_done, nm_ready, p_ready, pT_done = sems("s_done"), sems("nm_ready"), sems("p_ready"), sems("pT_done")
        ptA_ready, ptB_ready, o_done = sems("ptA_ready"), sems("ptB_ready"), sems("o_done")
        inv_ready, inv_done, yna_taken = sems("inv_ready"), sems("inv_done"), sems("yna_taken")
        row_ready, col_done = sem("row_ready"), sem("col_done")
        yhi_ready, ylo_ready = sems("yhi_ready"), sems("ylo_ready")
        gb_done, gb_taken = sems("gb_done"), sems("gb_taken")
        oT_done, osd_done, o_ready = sems("oT_done"), sems("osd_done"), sems("o_ready")
        xres_loaded = sems("xres_loaded", 2)
        res_added = sems("res_added")
        stored = sems("stored", 2)
        pair_chain = sems("pair_chain")
        act_chain, dve_chain, pool_chain = sem("act_chain"), sem("dve_chain"), sem("pool_chain")

        def chunks(l, j):
            if l < DEPTH - 1:
                return CHUNKS
            full = j in (10, 11, 12, 13) or (Q0 <= j < NB_IN and (j - Q0) % 4 in (1, 2))
            return CHUNKS if full else CHUNKS[1:]

        def tiles(l):
            return list(range(NT)) if l < DEPTH - 1 else list(range(CT, NT))

        def rounds(ts):
            return [ts[i:i + 4] for i in range(0, len(ts), 4)]

        def slot_cols(j):
            base = 1536 * (j % 2) + 256
            return base

        def aux_before_states(l):
            return 3 + 8 + 4 * len(rounds(range(NT))) + 2 * len(rounds(tiles(l)))

        def groups(l):
            return [g for t in tiles(l) for g in (2 * t, 2 * t + 1)]

        def aux_before_attention(l):
            return aux_before_states(l) + NT - 1 + 2 * len(rounds(tiles(l)))

        EVEN, ODD = rounds(list(range(NT))), rounds(list(range(LT - 1)))
        V_ROUNDS = len(EVEN) + len(ODD)

        def stores(l, i):
            return 16 * (l * (NT // 2) + i // 2 + 1)

        junk2 = bank(7)[:, 0:256]
        BO = [1, 0] + list(range(NT - 1, CT - 1, -1))
        x_in, x_mid = A["tokens"], A["x_mid"]

        block = ctx.enter_context(nc.Block())

        @block.sync
        def _(sp):
            for dst, src in [(ident, "ident"), (maskF, "maskF"), (maskB, "maskB"), (perm, "perm"),
                             (colmask, "colmask"), (ccol, "ccol"), (bada, "b_ada"),
                             (gpre, "g_pre"), (gpost, "g_post"), (cw, "conv_w"), (caw, "conv_a"),
                             (nrmw, "norm_w")]:
                sp.dma_start(dst[:], A[src]).then_inc(consts, 16)
            for dst, src in [(dtb, "dt_bias"), (alog, "a_log"), (dsk, "ssd_d")]:
                sp.dma_start(dst[:].rearrange("p l n -> p (l n)"), A[src].partition_broadcast(P)).then_inc(consts, 16)

            def load_ada(l, b):
                if b >= 2:
                    sp.wait_ge(ada_mm[l], b - 1)
                sp.dma_start(adaw[b % 2], A["w_ada"][l, b]).then_inc(ada_loaded[b % 2], 16)

            def load_w(l, j):
                if j >= 2:
                    sp.wait_ge(w_split[l], j - 1)
                elif l:
                    sp.wait_ge(w_split[l - 1], NB - 1 + j)
                sp.dma_start(wraw[j % 2][:], A["w_blocks"][l, j]).then_inc(w_loaded[j % 2], 16)

            def load_x(l, t):
                if t >= 3:
                    sp.wait_ge(xnT_done[l], t - 2)
                if l:
                    sp.wait_ge(stored[t % 2], stores(0, t))
                src = x_mid if l else x_in
                sp.dma_start(xt[t % 3], src[P * t:P * t + P, :]).then_inc(x_loaded[t % 3], 16)

            def load_res(l, i, t):
                if i >= 2:
                    sp.wait_ge(res_added[l], i - 1)
                else:
                    sp.wait_ge(yna_taken[l], PAIRS * len(tiles(l)) + 1)
                src = x_mid if l else x_in
                sp.dma_start(xres[i % 2], src[P * t:P * t + P, :]).then_inc(xres_loaded[i % 2], 16)

            for l in range(DEPTH):
                load_w(l, 0)
                load_w(l, 1)
                if l:
                    sp.wait_ge(proj_done[l - 1], NB_IN + 1)
                sp.dma_start(wdt[:], A["w_dt"][l]).then_inc(wdt_loaded, 16)
                if l == 0:
                    for t in range(3):
                        load_x(l, t)
                    for i, (b, n, dst) in enumerate(ADA0):
                        if i >= 5:
                            sp.wait_ge(ada_mm[0], b - 13)
                        sp.dma_start(dst.rearrange("p (b n) -> p b n", b=n),
                                     A["w_ada"][0, b:b + n].rearrange("b p k c -> p b (k c)")).then_inc(ada_first[i], 16)
                    for t in range(3, NT):
                        load_x(l, t)
                else:
                    for i, t in enumerate(tiles(l - 1)):
                        load_res(l - 1, i, t)
                        if 2 <= i < 5:
                            load_x(l, t - 2)
                    for t in range(3, NT):
                        load_x(l, t)
                for j in range(2, Q0):
                    load_w(l, j)
                    if j == 7:
                        sp.wait_ge(proj_done[l], 1)
                        sp.dma_start(cosT, A["rope_cos"]).then_inc(rope_loaded[l], 16)
                        sp.dma_start(sinT, A["rope_sin"]).then_inc(rope_loaded[l], 16)
                n_steps = len(groups(l))
                for hp in range(PAIRS):
                    for i in range(4):
                        load_w(l, Q0 + 4 * hp + i)
                    if hp == 0:
                        sp.wait_ge(yss_done, l + 1)
                    else:
                        sp.wait_ge(nm_ready[l], n_steps * hp)
                    for e in range(2):
                        src = bass.AP(tensor=A["rpb"].tensor,
                                      offset=(l * HEADS + 2 * hp + e) * 127 * TW,
                                      ap=[[TW, GRID_W], [1, GRID_W * TW]])
                        dst = tab[GRID_W * e:GRID_W * (e + 1)].rearrange("p k r -> p (k r)")
                        sp.dma_start(dst, src).then_inc(tab_loaded[l], 16)
                    if l + 1 < DEPTH:
                        for b in range(6 * hp, 6 * hp + 6):
                            load_ada(l + 1, b)
                for j in range(NB_IN, NB):
                    load_w(l, j)
            for i, t in enumerate(tiles(DEPTH - 1)):
                load_res(DEPTH - 1, i, t)
            for i in (LT - 2, LT - 1):
                sp.wait_ge(stored[i % 2], stores(DEPTH - 1, i))

        @block.gpsimd
        def _(pool):
            chain = [0]

            def link(ins):
                chain[0] += 1
                ins.then_inc(pool_chain, 1)
                pool.wait_ge(pool_chain, chain[0])

            def split_w(l, j):
                s = j % 2
                pool.wait_ge(w_loaded[s], 16 * (l * (NB // 2) + j // 2 + 1))
                if j >= 2:
                    pool.wait_ge(proj_done[l], j - 1)
                elif l:
                    pool.wait_ge(proj_done[l - 1], NB - 1 + j)
                link(pool.tensor_copy(whi[s][:], wraw[s][:]))
                pool.tensor_tensor(wlo[s][:], wraw[s][:], whi[s][:].bitcast(F32), ALU.subtract).then_inc(w_split[l], 1)

            def ssd_inputs(l):
                TT = nc.gpsimd.tensor_tensor
                y0, a0 = tiles(l)[0], aux_before_states(l)
                pool.wait_ge(ssd_in, l + 1)
                for i in range(NT - 1):
                    if i >= 2:
                        pool.wait_ge(aux_done[l], a0 + i - 1)
                    TT(by_head(xw[i % 2]), by_head(xtok[:, BO[i], :]), hb(dth(s_we, 1, BO[i]), SP_),
                       ALU.mult).then_inc(xwb_ready[l], 1)

                def scaled(c):
                    s, yi = c % 2, c - y0
                    x_c = by_head(xtok[:, c, :])
                    if c < 2:
                        pool.wait_ge(aux_done[l], a0 + NT - 1)
                    else:
                        pool.wait_ge(stf_done[l], c - 1)
                    if c < NT - 1:
                        last = TT(by_head(xw[s]), x_c, hb(dth(s_we, 0, c), SP_), ALU.mult)
                    if yi >= 2:
                        pool.wait_ge(y_gated[l], yi - 1)
                    if yi >= 0:
                        for d in range(2):
                            TT(by_head(xp[d][s]), x_c, hb(dth(s_dt, d, c), SP_), ALU.mult)
                        last = TT(by_head(yxd[s]), x_c, hb(dsk[:, l], SP_), ALU.mult)
                    last.then_inc(xp_ready[l], 1)

                scaled(0)
                for c in range(NT):
                    if c + 1 < NT:
                        scaled(c + 1)
                        if c:
                            pool.wait_ge(prevf_ready[l], c)
                        if c > y0:
                            pool.wait_ge(yo_done[l], c - y0)
                        TT(by_head(prevf[(c + 1) % 2]), by_head(prevf[c % 2]), hb(dth(s_de, 0, c), SP_),
                           ALU.mult).then_inc(nf_ready[l], 1)

            def residual(l, i, t):
                pool.wait_ge(o_ready[l], i + 1)
                pool.wait_ge(xres_loaded[i % 2], stores(l, i))
                link(pool.tensor_tensor(osb[i % 2], osb[i % 2], xres[i % 2], ALU.add))
                pool.sem_inc(res_added[l], 1)
                dst = x_mid[P * t:P * t + P, :] if l < DEPTH - 1 else A["out"][P * (t - CT):P * (t - CT) + P, :]
                pool.dma_start(dst, osb[i % 2]).then_inc(stored[i % 2], 16)

            for l in range(DEPTH):
                if l:
                    for i, t in enumerate(tiles(l - 1)):
                        residual(l - 1, i, t)
                split_w(l, 0)
                split_w(l, 1)
                for t in range(NT):
                    pool.wait_ge(hhi_ready[l], t + 1)
                    c = slice(P * t, P * t + P)
                    pool.tensor_tensor(hLo[:, :, c], h32[t % 2], hHi[:, :, c].bitcast(F32), ALU.subtract).then_inc(hlo_ready[l], 1)
                for j in range(2, Q0 + 2):
                    split_w(l, j)
                ssd_inputs(l)
                for j in range(Q0 + 2, NB):
                    split_w(l, j)
            for i, t in enumerate(tiles(DEPTH - 1)):
                residual(DEPTH - 1, i, t)

        @block.scalar
        def _(act):
            chain = [0]

            def link(ins):
                chain[0] += 1
                ins.then_inc(act_chain, 1)
                act.wait_ge(act_chain, chain[0])

            def take(l, j, dst, func=ACT.Copy, scale=1.0, padded=False):
                act.wait_ge(proj_done[l], j + 1)
                b = slot_cols(j)
                if padded:
                    if len(chunks(l, j)) == 3:
                        nc.scalar.activation(dst[:, 1:1 + CTX], PS[:, b:b + CTX], func, scale=scale)
                    last = nc.scalar.activation(dst[:, 2 + CTX:2 + CTX + SEQ], PS[:, b + CTX:b + T], func, scale=scale)
                else:
                    o = 0 if len(chunks(l, j)) == 3 else CTX
                    last = nc.scalar.activation(dst[:, o:T], PS[:, b + o:b + T], func, scale=scale)
                last.then_inc(proj_taken[l], 1)

            def norm_stats(l, t):
                act.wait_ge(x_loaded[t % 3], 16 * (l * len(range(t % 3, NT, 3)) + t // 3 + 1))
                link(nc.scalar.activation(junk, xt[t % 3], ACT.Square, accum_out=ss[:, t:t + 1]))
                nc.scalar.activation(rstd[:, t:t + 1], ss[:, t:t + 1], ACT.Sqrt, scale=1.0 / DM,
                                     bias=eps_col[:, 0:1]).then_inc(sd_done[l], 1)
                act.wait_ge(rstd_ok[l], t + 1)
                nc.scalar.activation(xt[t % 3], xt[t % 3], ACT.Copy, scale=rstd[:, t:t + 1]).then_inc(xn_ready[l], 1)

            def high_part(l, t):
                act.wait_ge(h32_ready[l], t + 1)
                if t == 0 and l:
                    act.wait_ge(proj_done[l - 1], NB)
                nc.scalar.activation(hHi[:, :, P * t:P * t + P], h32[t % 2], ACT.Copy).then_inc(hhi_ready[l], 1)

            act.wait_ge(consts, 16 * N_CONSTS)
            act.wait_ge(eps_ok, 1)
            link(nc.scalar.activation(ccol[:], ccol[:], ACT.Silu))
            act.sem_inc(silu_c, 1)
            nc.scalar.activation(alog[:], alog[:], ACT.Exp).then_inc(aneg_ok, 1)

            for l in range(DEPTH):
                for t in range(NT):
                    norm_stats(l, t)
                    if t >= 1:
                        high_part(l, t - 1)
                high_part(l, NT - 1)

                act.wait_ge(dt_abs, l + 1)
                nc.scalar.activation(s_t1, s_t1, ACT.Exp, scale=-1.0).then_inc(dt_exp, 1)
                for j2 in range(2):
                    if j2:
                        act.wait_ge(convA_done[l], 1)
                    for i, (dst, func) in enumerate([(gin, ACT.Copy), (gc, ACT.Copy), (gb, ACT.Copy), (gz, ACT.Silu)]):
                        take(l, 4 * j2 + i, dst, func)
                act.wait_ge(small_in, l + 1)
                nc.scalar.activation(s_ea, s_ac, ACT.Exp)
                nc.scalar.activation(s_we, s_we, ACT.Exp)
                nc.scalar.activation(s_de, s_de, ACT.Exp).then_inc(small_exp, 1)

                def silu(j):
                    act.wait_ge(conv_done[l], j - 7)
                    o = 0 if len(chunks(l, j)) == 3 else CTX
                    dst = {8: CTt[0], 9: CTt[1], 10: BTt[0], 11: BTt[1], 12: cv, 13: cv}[j]
                    nc.scalar.activation(dst[:, o:T], cv[:, o:T], ACT.Silu).then_inc(silu_done[l], 1)

                for j in range(8, 14):
                    if j == 8:
                        act.wait_ge(convA_done[l], 2)
                    if j >= 10:
                        act.wait_ge(conv_done[l], j - 9)
                    take(l, j, ubuf[j % 2], padded=True)
                    if j >= 9:
                        silu(j - 1)
                act.wait_ge(conv_done[l], 5)
                take(l, 14, ubuf[0], ACT.Silu)
                silu(13)
                act.wait_ge(conv_done[l], 6)
                take(l, 15, ubuf[1], ACT.Silu)

                ys = tiles(l)

                def square(i):
                    act.wait_ge(y_gated[l], i + 1)
                    c = ys[i]
                    link(nc.scalar.activation(junk2, ztok[:, c, :], ACT.Square, accum_out=ss[:, c:c + 1]))

                for i, c in enumerate(ys):
                    for d in range(2):
                        act.wait_ge(bc_done[l], 2 * i + d + 1)
                        if i >= 2:
                            act.wait_ge(yd_done[l], i - 1)
                        e = Ed[i % 2][d]
                        for h in range(SH):
                            last = nc.scalar.activation(e[:, h, :], bank(1 + d)[:, P * h:P * h + P], ACT.Relu,
                                                        scale=-1.0, bias=dth(s_ac, d, c)[:, h:h + 1])
                        last.then_inc(bc_taken[l], 1)
                        act.wait_ge(bc_taken[l], 2 * i + d + 1)
                        nc.scalar.activation(e, e, ACT.Exp, scale=-1.0).then_inc(exp_ready[l], 1)
                    if i >= 2:
                        square(i - 2)
                square(len(ys) - 2)
                square(len(ys) - 1)
                a = ys[0]
                nc.scalar.activation(rstd[:, a:NT], ss[:, a:NT], ACT.Sqrt, scale=1.0 / SSD,
                                     bias=eps_col[:, 0:1]).then_inc(ysq_done, 1)

                steps = groups(l)
                n = len(steps)

                def soft(hp, i):
                    s = i % 2
                    act.wait_ge(nm_ready[l], hp * n + i + 1)
                    if steps[i] >= 2 * CT:
                        nc.scalar.activation(Pr[s][:, 0:512], Pr[s][:, 0:512], ACT.Exp, bias=mx[s][:, 1:2],
                                             accum_out=sums[:, i % 4, 0:1])
                    nc.scalar.activation(Pr[s][:, 512:768], bank(2 * s + 1)[:, 0:256], ACT.Exp, bias=mx[s][:, 1:2],
                                         accum_out=sums[:, i % 4, 1:2]).then_inc(p_ready[l], 1)

                def pt_context(hp, i):
                    act.wait_ge(pT_done[l], hp * n + i + 1)
                    nc.scalar.activation(PT[i % 2][:, 512:768], bank(5)[:, 0:256], ACT.Copy).then_inc(ptB_ready[l], 1)

                with act.Fori(0, PAIRS) as hp:
                    for i, (dst, func) in enumerate([(None, ACT.Copy), (kT, ACT.Copy), (vT, ACT.Copy), (zT, ACT.Silu)]):
                        j = Q0 + i
                        act.wait_ge(proj_done[l], 4 * hp + (j + 1))
                        if i == 3:
                            act.wait_ge(yna_taken[l], hp * len(tiles(l)) + 1)
                        b = slot_cols(j)
                        o = 0 if len(chunks(l, j)) == 3 else CTX
                        if i == 0:
                            for e in range(2):
                                r = slice(64 * e, 64 * e + 64)
                                src = PS[r, b + o:b + T].rearrange("p (g c) -> p g c", c=64)
                                last = nc.scalar.activation(qbd[r, o // 64:, 64 * e:64 * e + 64], src, func, scale=SCALE)
                        else:
                            last = nc.scalar.activation(dst[:, o:T], PS[:, b + o:b + T], func)
                        last.then_inc(proj_taken[l], 1)
                    act.wait_ge(aux_taken[l], V_ROUNDS * hp + (aux_before_attention(l) + V_ROUNDS))
                    soft(hp, 0)
                    for i in range(n):
                        if i + 1 < n:
                            soft(hp, i + 1)
                        pt_context(hp, i)

                act.wait_ge(yna_taken[l], PAIRS * len(tiles(l)) + 1)
                act.wait_ge(yss_done, l + 1)
                o = 0 if l < DEPTH - 1 else CTX
                for k in range(KC):
                    nc.scalar.activation(hHi[:, k, o:T], yT[:, k, o:T], ACT.Copy).then_inc(yhi_ready[l], 1)
                for m in range(KC):
                    j = NB_IN + m
                    take(l, j, yT[:, m, :])
                for i, t in enumerate(tiles(l)):
                    act.wait_ge(oT_done[l], i + 1)
                    link(nc.scalar.activation(junk, bank(2 * (i % 2), 2), ACT.Square, accum_out=ss2[:, t:t + 1]))
                    nc.scalar.activation(rstd2[:, t:t + 1], ss2[:, t:t + 1], ACT.Sqrt, scale=1.0 / DM,
                                         bias=eps_col[:, 0:1]).then_inc(osd_done[l], 1)

        @block.vector
        def _(dve):
            chain = [0]

            def link(ins):
                chain[0] += 1
                ins.then_inc(dve_chain, 1)
                dve.wait_ge(dve_chain, chain[0])

            TT, TS, STT = nc.vector.tensor_tensor, nc.vector.tensor_scalar, nc.vector.scalar_tensor_tensor
            nc.vector.memset(eps_col[:], EPS).then_inc(eps_ok, 1)

            def ada_take(l, b):
                if b < NADA:
                    dve.wait_ge(ada_mm[l], b + 1)
                    nc.vector.tensor_copy(adarow[b % 2][0:2, :], bank(6 + b % 2)[0:2, 384:512]).then_inc(row_ready, 1)
                if b:
                    dve.wait_ge(col_done, b)
                    nc.vector.tensor_copy(mod[:, l, b - 1, :], bank(6 + (b - 1) % 2)[:, 256:258]).then_inc(ada_taken[l], 1)

            def finish_mod(l):
                dve.wait_ge(ada_taken[l], NADA)
                link(TT(mod[:, l], mod[:, l], bada[:, l].unsqueeze(2).broadcast_to([P, NADA, 2]), ALU.add))
                for v in range(2):
                    STT(mod[:, l, KC:2 * KC, v], mod[:, l, KC:2 * KC, v], 1.0, gpre[:, l], ALU.add, ALU.mult)
                    last = TT(mod[:, l, 2 * KC:, v], mod[:, l, 2 * KC:, v], gpost[:, l], ALU.mult)
                link(last)
                dve.sem_inc(mod_ready[l], 1)

            def norm_rstd(l, t):
                dve.wait_ge(sd_done[l], t + 1)
                nc.vector.reciprocal(rstd[:, t:t + 1], rstd[:, t:t + 1]).then_inc(rstd_ok[l], 1)

            def norm_mod(l, t):
                v = 1 if t < CT else 0
                dve.wait_ge(xnT_done[l], t + 1)
                if t >= 2:
                    dve.wait_ge(hlo_ready[l], t - 1)
                src = bank(4 + 2 * (t % 2), 2).rearrange("p (k c) -> p k c", k=KC)
                TT(h32[t % 2], src, mod[:, l, KC:2 * KC, v].unsqueeze(2).broadcast_to([P, KC, P]), ALU.mult).then_inc(xnT_taken[l], 1)
                dve.wait_ge(xnT_taken[l], t + 1)
                TT(h32[t % 2], h32[t % 2], mod[:, l, 0:KC, v].unsqueeze(2).broadcast_to([P, KC, P]),
                   ALU.add).then_inc(h32_ready[l], 1)

            dve.wait_ge(consts, 16 * N_CONSTS)
            dve.wait_ge(aneg_ok, 1)
            link(TS(alog[:], alog[:], -1.0, None, ALU.mult))
            for b in range(NADA + 1):
                ada_take(0, b)
                if b % 8 == 7 and b // 8 < 2:
                    norm_rstd(0, b // 8)
            finish_mod(0)

            for l in range(DEPTH):
                aux = [0]

                def aux_wait():
                    dve.wait_ge(aux_done[l], aux[0] + 1)
                    b = bank(6 + aux[0] % 2)
                    aux[0] += 1
                    return b

                for t in range(NT):
                    if l or t >= 2:
                        norm_rstd(l, t)
                    if t >= 1:
                        norm_mod(l, t - 1)
                norm_mod(l, NT - 1)

                dve.wait_ge(wdt_loaded, 16 * (l + 1))
                link(nc.vector.tensor_copy(wdtHi[:], wdt[:]))
                TT(wdtLo[:], wdt[:], wdtHi[:].bitcast(F32), ALU.subtract).then_inc(wdt_split, 1)

                dve.wait_ge(dtT_done, l + 1)
                nc.vector.tensor_copy(dtT, PS[0:8, slot_cols(1):slot_cols(1) + T]).then_inc(dtT_ready, 1)
                raw = aux_wait()
                bias = dtb[:, l].rearrange("p (d h) -> p d h", d=2).unsqueeze(2).broadcast_to([P, 2, NT, SH])
                v4 = lambda x: x.rearrange("p (d c h) -> p d c h", d=2, c=NT)
                raw = raw[:, 0:80].rearrange("p (c d h) -> p d c h", d=2, c=NT)
                link(TT(v4(s_t0), raw, bias, ALU.add))
                dve.sem_inc(aux_taken[l], 1)
                link(TS(s_t1, s_t0, -1.0, None, ALU.mult))
                TT(s_t1, s_t0, s_t1, ALU.max).then_inc(dt_abs, 1)
                dve.wait_ge(dt_exp, l + 1)
                link(TS(s_dt, s_t1, 2.0, None, ALU.add))
                link(nc.vector.reciprocal(s_dt, s_dt))
                link(TT(s_t1, s_t1, s_dt, ALU.mult))
                link(TT(s_dt, s_t1, s_t1, ALU.mult))
                link(TS(s_we, s_dt, 1.0 / 17, None, ALU.mult))
                for k in range(7, 0, -1):
                    link(STT(s_we, s_we, 1.0 / (2 * k + 1), s_dt, ALU.add, ALU.mult))
                link(STT(s_we, s_we, 1.0, s_t1, ALU.add, ALU.mult))
                link(TS(s_t0, s_t0, 0.0, None, ALU.max))
                link(STT(s_dt, s_we, 2.0, s_t0, ALU.mult, ALU.add))
                an = alog[:, l].rearrange("p (d h) -> p d h", d=2).unsqueeze(2).broadcast_to([P, 2, NT, SH])
                TT(v4(s_t0), v4(s_dt), an, ALU.mult).then_inc(da_ready, 1)
                cs = aux_wait()
                nc.vector.tensor_copy(s_ac, cs[:, 0:80]).then_inc(aux_taken[l], 1)
                dve.wait_ge(aux_taken[l], 2)
                dve.sem_inc(acs_ready, 1)

                def gated_conv(j2):
                    dve.wait_ge(proj_taken[l], 4 * j2 + 4)
                    u = ubuf[0]
                    o = 0 if l < DEPTH - 1 else CTX
                    if o == 0:
                        TT(u[:, 1:1 + CTX], gin[:, 0:CTX], gc[:, 0:CTX], ALU.mult)
                    link(TT(u[:, 2 + CTX:2 + T], gin[:, CTX:T], gc[:, CTX:T], ALU.mult))
                    conv_taps(u, caw[:, l, j2], None, o)
                    link(TT(cv[:, o:T], cv[:, o:T], gb[:, o:T], ALU.mult))
                    TT(yT[:, j2, o:T], cv[:, o:T], gz[:, o:T], ALU.mult).then_inc(convA_done[l], 1)
                    dve.wait_ge(convA_done[l], j2 + 1)

                def conv_taps(u, w, b, o):
                    spans = ([(0, 0, CTX)] if o == 0 else []) + [(CTX, CTX + 1, SEQ)]
                    for a, s, n in spans:
                        if b is None:
                            last = TS(cv[:, a:a + n], u[:, s:s + n], w[:, 0:1], None, ALU.mult)
                        else:
                            last = TS(cv[:, a:a + n], u[:, s:s + n], w[:, 0:1], b, ALU.mult, ALU.add)
                    link(last)
                    for k in (1, 2):
                        for a, s, n in spans:
                            last = STT(cv[:, a:a + n], u[:, s + k:s + k + n], w[:, k:k + 1], cv[:, a:a + n],
                                       ALU.mult, ALU.add)
                        if k == 1:
                            link(last)
                    if b is None:
                        link(last)
                    return last

                for u in ubuf:
                    for a in (0, 1 + CTX, 2 + T):
                        last = nc.vector.memset(u[:, a:a + 1], 0.0)
                link(last)
                gated_conv(0)
                ends = aux_wait()
                nc.vector.tensor_copy(s_de, ends[:, 0:80]).then_inc(aux_taken[l], 1)
                dve.wait_ge(aux_taken[l], 3)
                link(TT(s_we, s_de, s_ac, ALU.subtract))
                link(TS(s_we, s_we, 0.0, None, ALU.min))
                dve.sem_inc(small_in, 1)
                gated_conv(1)
                dve.wait_ge(small_exp, l + 1)
                link(TT(s_we, s_we, s_dt, ALU.mult))

                def conv(j):
                    dve.wait_ge(proj_taken[l], j + 1)
                    if j >= 9:
                        dve.wait_ge(silu_done[l], j - 8)
                    o = 0 if len(chunks(l, j)) == 3 else CTX
                    conv_taps(ubuf[j % 2], cw[:, l, j - 8], cw[:, l, j - 8, 3:4], o).then_inc(conv_done[l], 1)

                def rope(j):
                    dst = {8: CTt[0], 9: CTt[1], 10: BTt[0], 11: BTt[1]}[j]
                    if j == 8:
                        dve.wait_ge(rope_loaded[l], 32)
                    for h in range(2):
                        rot = aux_wait()
                        c = slice(CTX + 512 * h, CTX + 512 * h + 512)
                        f = slice(512 * h, 512 * h + 512)
                        TT(rtmp, rot, sinT[:, f], ALU.mult).then_inc(aux_taken[l], 1)
                        dve.wait_ge(aux_taken[l], aux[0])
                        link(TT(dst[:, c], dst[:, c], cosT[:, f], ALU.mult))
                        last = TT(dst[:, c], dst[:, c], rtmp, ALU.add)
                        if h == 0:
                            link(last)
                    last.then_inc(rope_done[l], 1)
                    dve.wait_ge(rope_done[l], j - 7)

                def to_tok(dst, ts):
                    for r in rounds(ts):
                        b = aux_wait()
                        nc.vector.tensor_copy(dst(r[0], r[-1] + 1), b[:, 0:P * len(r)].rearrange("p (c n) -> p c n", n=P)).then_inc(aux_taken[l], 1)
                        dve.wait_ge(aux_taken[l], aux[0])

                allt = list(range(NT))
                conv(8)
                conv(9)
                rope(8)
                conv(10)
                rope(9)
                conv(11)
                rope(10)
                conv(12)
                rope(11)
                to_tok(lambda a, b: btok[:, a:b, 0, :], allt)
                to_tok(lambda a, b: btok[:, a:b, 1, :], allt)
                to_tok(lambda a, b: xtok[:, a:b, 0:P], allt)
                conv(13)
                to_tok(lambda a, b: xtok[:, a:b, P:2 * P], allt)
                to_tok(lambda a, b: ztok[:, a:b, 0:P], tiles(l))
                to_tok(lambda a, b: ztok[:, a:b, P:2 * P], tiles(l))

                nc.vector.memset(prevb[:, BO[0], :], 0.0)
                link(nc.vector.memset(prevf[0], 0.0))

                dve.sem_inc(ssd_in, 1)
                for i in range(NT - 1):
                    c, nxt = BO[i], BO[i + 1]
                    link(TT(by_head(prevb[:, nxt, :]), by_head(prevb[:, c, :]), hb(dth(s_de, 1, c), SP_), ALU.mult))
                    b = aux_wait()
                    TT(prevb[:, nxt, :], prevb[:, nxt, :], b[:, 0:256], ALU.add).then_inc(aux_taken[l], 1)
                    dve.wait_ge(aux_taken[l], aux[0])

                ys = tiles(l)

                def mix(i):
                    dve.wait_ge(g_done[l], i + 1)
                    gsrc = bank(0)[:, 0:256].rearrange("p (g i) -> p g i", g=SG)
                    TT(GM[0], gsrc, maskF[:].unsqueeze(1).broadcast_to([P, SG, P]), ALU.mult)
                    link(TT(GM[1], gsrc, maskB[:].unsqueeze(1).broadcast_to([P, SG, P]), ALU.mult))
                    dve.sem_inc(g_taken[l], 1)
                    for d in range(2):
                        dve.wait_ge(exp_ready[l], 2 * i + d + 1)
                        e = Ed[i % 2][d].rearrange("p (g r) i -> p g r i", g=SG)
                        last = TT(e, e, GM[d].unsqueeze(2).broadcast_to([P, SG, SH // SG, P]), ALU.mult)
                    last.then_inc(mix_ready[l], 1)

                mix(0)
                for c in range(NT):
                    yi, s = c - ys[0], c % 2
                    if c < NT - 1:
                        nf = prevf[(c + 1) % 2]
                        dve.wait_ge(nf_ready[l], c + 1)
                        dve.wait_ge(stf_done[l], c + 1)
                        TT(nf, nf, bank(5)[:, 0:256], ALU.add).then_inc(prevf_ready[l], 1)
                    if yi < 0:
                        continue
                    dve.wait_ge(yo_done[l], yi + 1)
                    yo = bank(4)
                    TT(by_head(yacc[s]), by_head(yo[:, 0:256]), hb(dth(s_ea, 0, c), SP_), ALU.mult)
                    link(TT(by_head(yt2[s]), by_head(yo[:, 256:512]), hb(dth(s_ea, 1, c), SP_), ALU.mult))
                    dve.sem_inc(yo_taken[l], 1)
                    link(TT(yacc[s], yacc[s], yt2[s], ALU.add))
                    dve.wait_ge(xp_ready[l], c + 1)
                    link(TT(yacc[s], yacc[s], yxd[s], ALU.add))
                    if yi + 1 < len(ys):
                        mix(yi + 1)
                    dve.wait_ge(yd_done[l], yi + 1)
                    y4 = yacc[s].rearrange("p (g r x) -> p g r x", g=SG, r=2)
                    link(TT(y4, y4, diagonal(bank(3 if yi % 2 else 6)), ALU.add))
                    TT(ztok[:, c, :], ztok[:, c, :], yacc[s], ALU.mult).then_inc(y_gated[l], 1)
                a = ys[0]
                dve.wait_ge(ysq_done, l + 1)
                link(nc.vector.reciprocal(rstd[:, a:NT], rstd[:, a:NT]))
                TT(ztok[:, a:NT, :], ztok[:, a:NT, :], rstd[:, a:NT].unsqueeze(2).broadcast_to([P, NT - a, 256]),
                   ALU.mult).then_inc(yn_ready, 1)
                for j in range(2):
                    for r in rounds(ys):
                        b = aux_wait()
                        TS(yT[:, 6 + j, P * r[0]:P * (r[-1] + 1)], b[:, 0:P * len(r)], nrmw[:, l, j:j + 1], None,
                           ALU.mult).then_inc(aux_taken[l], 1)
                dve.wait_ge(aux_taken[l], aux[0])
                dve.sem_inc(yss_done, 1)

                steps = groups(l)
                n = len(steps)
                aux0 = aux[0]
                assert aux0 == aux_before_attention(l)
                pair_links = 1 + n + n // 2 + len(tiles(l)) - sum(t < CT for t in tiles(l))
                linked = [0]

                def link_pair(hp, ins):
                    linked[0] += 1
                    ins.then_inc(pair_chain[l], 1)
                    dve.wait_ge(pair_chain[l], hp * pair_links + linked[0])

                def row_max(hp, i):
                    s = i % 2
                    dve.wait_ge(s_done[l], hp * n + i + 1)
                    top = nc.vector.tensor_reduce(mx[s][:, 0:1], bank(2 * s + 1)[:, 0:256], AX_X, ALU.max)
                    ada_turn(hp, i)
                    if steps[i] >= 2 * CT:
                        _, first = window(steps[i] - 2 * CT)
                        link_pair(hp, nc.vector.tensor_tensor_reduce(
                            out=Pr[s][:, 0:512].rearrange("p (r k) -> p r k", k=64),
                            in0=bank(2 * s).rearrange("p (r k) -> p r k", k=64),
                            in1=tab[:, :, first:first + WIN_H].rearrange("p k r -> p r k")[:, :, ::-1],
                            scale=1.0, scalar=BIG, op0=ALU.add, op1=ALU.max, accum_out=mx[s][:, 1:2]))
                        TS(mx[s][:, 1:2], mx[s][:, 1:2], mx[s][:, 0:1], -1.0, ALU.max,
                           ALU.mult).then_inc(nm_ready[l], 1)
                    else:
                        link_pair(hp, top)
                        TS(mx[s][:, 1:2], mx[s][:, 0:1], -1.0, None, ALU.mult).then_inc(nm_ready[l], 1)

                def inverse_sums(hp, k):
                    s4 = (2 * k) % 4
                    dve.wait_ge(p_ready[l], hp * n + 2 * k + 2)
                    if tiles(l)[k] >= CT:
                        link_pair(hp, TT(inv[k % 2], sums[:, s4:s4 + 2, 0], sums[:, s4:s4 + 2, 1], ALU.add))
                        nc.vector.reciprocal(inv[k % 2], inv[k % 2]).then_inc(inv_ready[l], 1)
                    else:
                        nc.vector.reciprocal(inv[k % 2], sums[:, s4:s4 + 2, 1]).then_inc(inv_ready[l], 1)

                def gate_rows(hp, k):
                    t = tiles(l)[k]
                    b = bank(6 + k % 2)
                    dve.wait_ge(inv_done[l], hp * (n // 2) + k + 1)
                    for e in range(2):
                        r = slice(64 * e, 64 * e + 64)
                        src = b[r, 128:384].rearrange("p (u c) -> p u c", u=2)[:, :, 64 * e:64 * e + 64]
                        last = TT(zr[k % 2][r].rearrange("p (u c) -> p u c", u=2),
                                  zT[r, P * t:P * t + P].rearrange("p (u c) -> p u c", u=2), src, ALU.mult)
                    link_pair(hp, last)
                    out = yT[:, bass.ds(hp + 2, 1), :].rearrange("p a b -> p (a b)")[:, P * t:P * t + P]
                    TT(out, b[:, 0:P], zr[k % 2], ALU.mult).then_inc(yna_taken[l], 1)

                def ada_turn(hp, i):
                    m, b = i // 2 - 1, bank(2 * (i % 2) + 1)
                    if l + 1 == DEPTH or i % 2 or not 0 <= m <= 6:
                        return
                    if m < 6:
                        nc.vector.tensor_copy(adarow[m % 2][0:2, :], b[0:2, 256:384]).then_inc(row_ready, 1)
                    if m:
                        nc.vector.tensor_copy(mod[:, l + 1, bass.ds(6 * hp + (m - 1), 1), :].rearrange("p a b -> p (a b)"),
                                              b[:, 384:386]).then_inc(ada_taken[l + 1], 1)

                for e in range(2):
                    r = slice(64 * e, 64 * e + 64)
                    nc.vector.memset(qbd[r, steps[0]:, 64 - 64 * e:P - 64 * e], 0.0)
                dve.sem_inc(yna_taken[l], 1)
                with dve.Fori(0, PAIRS) as hp:
                    for r, ts in enumerate(EVEN + ODD):
                        dve.wait_ge(aux_done[l], V_ROUNDS * hp + (aux0 + r + 1))
                        dst = vtok if r < len(EVEN) else vodd
                        nc.vector.tensor_copy(dst[:, ts[0]:ts[-1] + 1, :], bank(6 + r % 2)[:, 0:P * len(ts)].rearrange(
                            "p (c n) -> p c n", n=P)).then_inc(aux_taken[l], 1)
                    dve.wait_ge(tab_loaded[l], 32 * hp + 32)
                    link_pair(hp, TT(tab, tab, colmask[:].unsqueeze(2).broadcast_to([P, GRID_W, TW]), ALU.add))
                    row_max(hp, 0)
                    row_max(hp, 1)
                    for i in range(n):
                        k = i // 2
                        dve.wait_ge(pT_done[l], hp * n + i + 1)
                        if steps[i] >= 2 * CT:
                            nc.vector.tensor_copy(PT[i % 2][:, 0:512], bank(4)).then_inc(ptA_ready[l], 1)
                        else:
                            dve.sem_inc(ptA_ready[l], 1)
                        if i + 2 < n:
                            row_max(hp, i + 2)
                        if i % 2:
                            inverse_sums(hp, k)
                        elif k:
                            gate_rows(hp, k - 1)
                    gate_rows(hp, n // 2 - 1)
                    assert linked[0] == pair_links
                if l + 1 < DEPTH:
                    finish_mod(l + 1)

                o = 0 if l < DEPTH - 1 else CTX
                dve.wait_ge(yna_taken[l], PAIRS * (n // 2) + 1)
                for k in range(KC):
                    dve.wait_ge(yhi_ready[l], k + 1)
                    TT(hLo[:, k, o:T], yT[:, k, o:T], hHi[:, k, o:T].bitcast(F32), ALU.subtract).then_inc(ylo_ready[l], 1)
                for v in range(2 if l < DEPTH - 1 else 1):
                    dve.wait_ge(gb_done[l], v + 1)
                    nc.vector.tensor_copy(gbc[v], bank(6, 2)).then_inc(gb_taken[l], 1)
                dve.wait_ge(gb_taken[l], 2 if l < DEPTH - 1 else 1)
                for i, t in enumerate(tiles(l)):
                    dve.wait_ge(osd_done[l], i + 1)
                    link(nc.vector.reciprocal(rstd2[:, t:t + 1], rstd2[:, t:t + 1]))
                    if i >= 2:
                        dve.wait_ge(stored[i % 2], stores(l, i - 2))
                    STT(osb[i % 2], bank(2 * (i % 2), 2), rstd2[:, t:t + 1], gbc[1 if t < CT else 0],
                        ALU.mult, ALU.mult).then_inc(o_ready[l], 1)

        @block.tensor
        def _(pe):
            mm, tp = nc.tensor.matmul, nc.tensor.transpose

            def ada_row(out, w, last_sem):
                for k in range(KC):
                    last = mm(out, ccol[:, k, :], w[:, k, :], start=(k == 0), stop=(k == KC - 1))
                last.then_inc(last_sem, 1)

            def ada_first_layer():
                for i, (b0, nb, place) in enumerate(ADA0):
                    pe.wait_ge(ada_first[i], 16)
                    for b in range(b0, b0 + nb):
                        if b >= 2:
                            pe.wait_ge(ada_taken[0], b - 1)
                        w = place[:, DM * (b - b0):DM * (b - b0 + 1)].rearrange("p (k c) -> p k c", k=KC)
                        ada_row(bank(6 + b % 2)[0:2, 384:512], w, ada_mm[0])
                        if b:
                            ada_column(b - 1)
                ada_column(NADA - 1)

            def ada_column(b):
                pe.wait_ge(row_ready, b + 1)
                tp(bank(6 + b % 2)[:, 256:258], adarow[b % 2][0:2, :], ident[0:2, 0:2]).then_inc(col_done, 1)

            def proj_mm(l, j, s):
                for ci, (a, n) in enumerate(CHUNKS):
                    if (a, n) not in chunks(l, j):
                        continue
                    out = PS[:, slot_cols(s) + a:slot_cols(s) + a + n]
                    k3 = [(w, x, k) for k in range(KC) for w, x in ((whi, hHi), (whi, hLo), (wlo, hHi))]
                    for q, (w, x, k) in enumerate(k3):
                        last = mm(out, w[s][:, k, :], x[:, k, a:a + n], start=(q == 0), stop=(q == len(k3) - 1))
                return last

            def proj(l, j):
                pe.wait_ge(w_split[l], j + 1)
                if j >= 2:
                    pe.wait_ge(proj_taken[l], j - 1)
                proj_mm(l, j, j % 2).then_inc(proj_done[l], 1)

            pe.wait_ge(consts, 16 * N_CONSTS)
            pe.wait_ge(silu_c, 1)
            ada_first_layer()
            pe.wait_ge(ada_taken[0], NADA)

            for l in range(DEPTH):
                aux = [0]

                def aux_open():
                    if aux[0] >= 2:
                        pe.wait_ge(aux_taken[l], aux[0] - 1)
                    return bank(6 + aux[0] % 2)

                def aux_close(last):
                    aux[0] += 1
                    last.then_inc(aux_done[l], 1)

                for t in range(NT):
                    pe.wait_ge(xn_ready[l], t + 1)
                    if l and t == 0:
                        pe.wait_ge(gb_taken[l - 1], 2)
                    if t >= 2:
                        pe.wait_ge(xnT_taken[l], t - 1)
                    for k in range(KC):
                        last = tp(bank(4 + 2 * (t % 2), 2)[:, P * k:P * k + P], xt[t % 3][:, P * k:P * k + P], ident[:])
                    last.then_inc(xnT_done[l], 1)

                pe.wait_ge(xnT_taken[l], NT)
                pe.wait_ge(hhi_ready[l], NT)
                pe.wait_ge(hlo_ready[l], NT)
                pe.wait_ge(wdt_split, l + 1)
                if l:
                    pe.wait_ge(o_ready[l - 1], len(tiles(l - 1)))
                k3 = [(w, x, k) for k in range(KC) for w, x in ((wdtHi, hHi), (wdtHi, hLo), (wdtLo, hHi))]
                for a, n in CHUNKS:
                    for q, (w, x, k) in enumerate(k3):
                        last = mm(PS[0:8, slot_cols(1) + a:slot_cols(1) + a + n], w[:, k, :], x[:, k, a:a + n],
                                  start=(q == 0), stop=(q == len(k3) - 1))
                last.then_inc(dtT_done, 1)
                proj(l, 0)
                pe.wait_ge(dtT_ready, l + 1)
                b = aux_open()
                for c in range(NT):
                    last = tp(b[:, 8 * c:8 * c + 8], dtT[:, P * c:P * c + P], ident[0:8, 0:8])
                aux_close(last)
                proj(l, 1)
                pe.wait_ge(da_ready, l + 1)
                b = aux_open()
                mm(b[:, 0:40], maskF[:], s_t0[:, 0:40], start=True, stop=True)
                aux_close(mm(b[:, 40:80], maskB[:], s_t0[:, 40:80], start=True, stop=True))
                proj(l, 2)
                proj(l, 3)
                pe.wait_ge(acs_ready, l + 1)
                b = aux_open()
                mm(b[:, 0:40], ident[:, P - 1:P].broadcast_to([P, P]), s_ac[:, 0:40], start=True, stop=True)
                aux_close(mm(b[:, 40:80], ident[:, 0:1].broadcast_to([P, P]), s_ac[:, 40:80], start=True, stop=True))
                for j in range(4, 10):
                    proj(l, j)

                def rot(j):
                    src = {8: CTt[0], 9: CTt[1], 10: BTt[0], 11: BTt[1]}[j]
                    pe.wait_ge(silu_done[l], j - 7)
                    for h in range(2):
                        b = aux_open()
                        aux_close(mm(b, perm[:], src[:, CTX + 512 * h:CTX + 512 * h + 512], start=True, stop=True))

                def to_tok(src, ts):
                    for r in rounds(ts):
                        b = aux_open()
                        for i, c in enumerate(r):
                            last = tp(b[:, P * i:P * i + P], src[:, P * c:P * c + P], ident[:])
                        aux_close(last)

                allt = list(range(NT))
                rot(8)
                proj(l, 10)
                rot(9)
                proj(l, 11)
                rot(10)
                proj(l, 12)
                rot(11)
                pe.wait_ge(rope_done[l], 4)
                to_tok(BTt[0], allt)
                proj(l, 13)
                to_tok(BTt[1], allt)
                pe.wait_ge(silu_done[l], 5)
                to_tok(cv, allt)
                proj(l, 14)
                pe.wait_ge(silu_done[l], 6)
                to_tok(cv, allt)
                proj(l, 15)
                pe.wait_ge(proj_taken[l], 16)
                to_tok(ubuf[0], tiles(l))
                to_tok(ubuf[1], tiles(l))

                for i in range(NT - 1):
                    c = BO[i]
                    pe.wait_ge(xwb_ready[l], i + 1)
                    b = aux_open()
                    for g in range(SG):
                        last = mm(b[:, P * g:P * g + P], btok[:, c, g, :], xw[i % 2][:, P * g:P * g + P],
                                  start=True, stop=True)
                    aux_close(last)
                pe.wait_ge(aux_taken[l], aux[0])

                ys = tiles(l)

                def ssd_front(i):
                    c = ys[i]
                    for d in range(2):
                        if i:
                            pe.wait_ge(bc_taken[l], 2 * (i - 1) + d + 1)
                        for h in range(SH):
                            a = 40 * d + 4 * c + h
                            last = tp(bank(1 + d)[:, P * h:P * h + P], s_ac[:, a:a + 1].broadcast_to([P, P]), ident[:])
                        last.then_inc(bc_done[l], 1)
                    if i:
                        pe.wait_ge(g_taken[l], i)
                    for g in range(SG):
                        last = mm(bank(0)[:, P * g:P * g + P], BTt[g][:, P * c:P * c + P], CTt[g][:, P * c:P * c + P],
                                  start=True, stop=True)
                    last.then_inc(g_done[l], 1)

                ssd_front(0)
                for c in range(NT):
                    yi, s = c - ys[0], c % 2
                    if yi >= 0 and yi + 1 < len(ys):
                        ssd_front(yi + 1)
                    pe.wait_ge(xp_ready[l], c + 1)
                    if c:
                        pe.wait_ge(prevf_ready[l], c)
                    if c < NT - 1:
                        for g in range(SG):
                            last = mm(bank(5)[:, P * g:P * g + P], btok[:, c, g, :], xw[s][:, P * g:P * g + P],
                                      start=True, stop=True)
                        last.then_inc(stf_done[l], 1)
                    if yi >= 0:
                        if yi:
                            pe.wait_ge(yo_taken[l], yi)
                        for d, prev in enumerate([prevf[s], prevb[:, c, :]]):
                            for g in range(SG):
                                last = mm(bank(4)[:, 256 * d + P * g:256 * d + P * g + P], CTt[g][:, P * c:P * c + P],
                                          prev[:, P * g:P * g + P], start=True, stop=True)
                        last.then_inc(yo_done[l], 1)
                        pe.wait_ge(mix_ready[l], yi + 1)
                        if yi >= 2:
                            pe.wait_ge(y_gated[l], yi - 1)
                        for h in range(SH):
                            g = h // 2
                            for d in range(2):
                                last = mm(bank(3 if yi % 2 else 6)[:, P * h:P * h + P], Ed[yi % 2][d][:, h, :],
                                          xp[d][s][:, P * g:P * g + P], start=(d == 0), stop=(d == 1))
                        last.then_inc(yd_done[l], 1)
                pe.wait_ge(yn_ready, l + 1)
                for j in range(2):
                    for r in rounds(ys):
                        b = aux_open()
                        for i, c in enumerate(r):
                            last = tp(b[:, P * i:P * i + P], ztok[:, c, P * j:P * j + P], ident[:])
                        aux_close(last)
                pe.wait_ge(aux_taken[l], aux[0])

                steps = groups(l)
                n = len(steps)
                aux0 = aux[0]

                def scores(hp, i):
                    s, q, m = i % 2, qbd[:, steps[i], :], i // 2 - 1
                    with_ada = l + 1 < DEPTH and i % 2 == 0 and 0 <= m <= 6
                    if with_ada and m:
                        pe.wait_ge(row_ready, 6 * hp + (NADA * (l + 1) + m))
                    if with_ada and m < 6:
                        pe.wait_ge(ada_loaded[m % 2], 48 * hp + 16 * (m // 2 + 1))
                        ada_row(bank(2 * s + 1)[0:2, 256:384], adaw[m % 2], ada_mm[l + 1])
                    if steps[i] >= 2 * CT:
                        k0 = CTX + GRID_W * window(steps[i] - 2 * CT)[0]
                        mm(bank(2 * s), q, kT[:, k0:k0 + 512], start=True, stop=True)
                    if with_ada and m:
                        tp(bank(2 * s + 1)[:, 384:386], adarow[(m - 1) % 2][0:2, :], ident[0:2, 0:2])
                    mm(bank(2 * s + 1)[:, 0:256], q, kT[:, 0:CTX], start=True, stop=True).then_inc(s_done[l], 1)

                def flip(hp, i):
                    s = i % 2
                    pe.wait_ge(p_ready[l], hp * n + i + 1)
                    if steps[i] >= 2 * CT:
                        for m in range(4):
                            tp(bank(4)[:, P * m:P * m + P], Pr[s][:, P * m:P * m + P], ident[:])
                    for m in range(2):
                        last = tp(bank(5)[:, P * m:P * m + P], Pr[s][:, 512 + P * m:640 + P * m], ident[:])
                    last.then_inc(pT_done[l], 1)

                def values(hp, i):
                    s, k = i % 2, i // 2
                    pe.wait_ge(ptA_ready[l], hp * n + i + 1)
                    pe.wait_ge(ptB_ready[l], hp * n + i + 1)
                    if i % 2 == 0:
                        pe.wait_ge(yna_taken[l], hp * (n // 2) + (k - 1 if k >= 2 else 0) + 1)
                    parts = [(vtok[:, m], 512 + P * m) for m in range(CT)]
                    if steps[i] >= 2 * CT:
                        r0 = window(steps[i] - 2 * CT)[0]
                        src, kt = (vodd, r0 // 2) if r0 % 2 else (vtok, CT + r0 // 2)
                        parts += [(src[:, kt + m], P * m) for m in range(4)]
                    for e in range(2):
                        out = bank(6 + k % 2)[64 * e:64 * e + 64, 64 * (i % 2):64 * (i % 2) + 64]
                        for m, (v, a) in enumerate(parts):
                            last = mm(out, v[:, 64 * e:64 * e + 64], PT[s][:, a + 64 * e:a + 64 * e + 64],
                                      start=(m == 0), stop=(m == len(parts) - 1))
                    last.then_inc(o_done[l], 1)

                def spread_inverse(hp, k):
                    pe.wait_ge(inv_ready[l], hp * (n // 2) + k + 1)
                    for u in range(2):
                        last = tp(bank(6 + k % 2)[:, P * (u + 1):P * (u + 2)], inv[k % 2][:, u:u + 1].broadcast_to([P, P]),
                                  ident[:])
                    last.then_inc(inv_done[l], 1)

                with pe.Fori(0, PAIRS) as hp:
                    for i in range(4):
                        j = Q0 + i
                        pe.wait_ge(w_split[l], 4 * hp + (j + 1))
                        pe.wait_ge(proj_taken[l], 4 * hp + (j - 1))
                        proj_mm(l, j, j % 2).then_inc(proj_done[l], 1)
                    pe.wait_ge(proj_taken[l], 4 * hp + (Q0 + 4))
                    pe.wait_ge(yna_taken[l], hp * (n // 2) + 1)
                    for r, ts in enumerate(EVEN + ODD):
                        if r >= 2:
                            pe.wait_ge(aux_taken[l], V_ROUNDS * hp + (aux0 + r - 1))
                        for i, c in enumerate(ts):
                            a = P * c if r < len(EVEN) else CTX + GRID_W + P * c
                            last = tp(bank(6 + r % 2)[:, P * i:P * i + P], vT[:, a:a + P], ident[:])
                        last.then_inc(aux_done[l], 1)
                    scores(hp, 0)
                    scores(hp, 1)
                    pe.wait_ge(aux_taken[l], V_ROUNDS * hp + (aux0 + V_ROUNDS))
                    for i in range(n):
                        k = i // 2
                        flip(hp, i)
                        if i + 2 < n:
                            scores(hp, i + 2)
                        if i % 2 == 0 and k:
                            spread_inverse(hp, k - 1)
                        values(hp, i)
                    spread_inverse(hp, n // 2 - 1)

                pe.wait_ge(yna_taken[l], PAIRS * (n // 2) + 1)
                pe.wait_ge(ylo_ready[l], KC)
                for v in range(2 if l < DEPTH - 1 else 1):
                    if v:
                        pe.wait_ge(gb_taken[l], v)
                    for k in range(KC):
                        last = tp(bank(6, 2)[:, P * k:P * k + P], mod[:, l, 2 * KC + k, v:v + 1].broadcast_to([P, P]), ident[:])
                    last.then_inc(gb_done[l], 1)
                for j in range(NB_IN, NB):
                    proj(l, j)
                pe.wait_ge(proj_taken[l], NB)
                for i, t in enumerate(tiles(l)):
                    if i >= 2:
                        pe.wait_ge(o_ready[l], i - 1)
                    for k in range(KC):
                        last = tp(bank(2 * (i % 2), 2)[:, P * k:P * k + P], yT[:, k, P * t:P * t + P], ident[:])
                    last.then_inc(oT_done[l], 1)


def _constants():
    f = np.float32
    j, i = np.arange(P)[:, None], np.arange(P)[None, :]
    n_freq = SN // 4
    inv_freq = (f(10000.0) ** (-np.arange(n_freq, dtype=f) / f(n_freq))).astype(f)
    pos = np.arange(SEQ)
    ang_r = (pos // GRID_W).astype(f)[None, :] * inv_freq[:, None]
    ang_c = (pos % GRID_W).astype(f)[None, :] * inv_freq[:, None]
    ang = np.concatenate([ang_r, ang_r, ang_c, ang_c]).astype(f)
    perm = np.zeros((P, P), f)
    for base in (0, SN // 2):
        for a in range(n_freq):
            perm[base + n_freq + a, base + a] = -1.0
            perm[base + a, base + n_freq + a] = 1.0
    cols = np.arange(GRID_W)
    lo = np.clip(cols - WIN_W // 2, 0, GRID_W - WIN_W)[:, None]
    inside = (cols[None, :] >= lo) & (cols[None, :] < lo + WIN_W)
    colmask = np.where(np.concatenate([inside, inside])[:, ::-1], 0.0, NEG).astype(f)
    return dict(ident=np.eye(P, dtype=f), maskF=(j <= i).astype(f), maskB=(j >= i).astype(f), perm=perm,
                colmask=colmask, rope_cos=np.cos(ang).astype(f), rope_sin=np.sin(ang).astype(f))


def _layout(x, c, ctx, c_ctx, w_ada, b_ada, g_pre, g_post, w_in, conv_a_w, rpb, ssd_conv_w, ssd_conv_b,
            dt_bias_f, dt_bias_b, a_log_f, a_log_b, ssd_d, ssd_norm_w, w_out):
    def by_channel(a):
        return np.moveaxis(a.reshape(*a.shape[:-1], -1, P), -1, 0)

    def blocks(w):
        return w.reshape(KC, P, -1, P).transpose(2, 1, 0, 3)

    cols = block_columns()
    w_blocks = np.stack([np.concatenate([
        blocks(np.concatenate([w_in[l][:, s:s + P] for s in cols], axis=1)), blocks(w_out[l])]) for l in range(DEPTH)])
    conv_w = np.concatenate([ssd_conv_w, ssd_conv_b[:, None, :]], axis=1)
    conv_w = conv_w.reshape(DEPTH, 4, 6, P)[:, :, [4, 5, 2, 3, 0, 1]].transpose(3, 0, 2, 1)
    table = np.pad(rpb.transpose(0, 1, 3, 2)[:, :, ::-1], ((0, 0), (0, 0), (48, 48), (0, 1)))
    arrays = dict(
        tokens=np.concatenate([ctx[0], x[0]]),
        ccol=np.stack([by_channel(c[0]), by_channel(c_ctx)], axis=-1),
        w_ada=np.stack([blocks(w_ada[l]) for l in range(DEPTH)]),
        b_ada=by_channel(b_ada), g_pre=by_channel(g_pre), g_post=by_channel(g_post),
        w_blocks=w_blocks,
        w_dt=w_in[:, :, SPLIT_IN[10]:].reshape(DEPTH, KC, P, 8).transpose(0, 2, 1, 3),
        conv_w=conv_w, conv_a=conv_a_w.reshape(DEPTH, 3, 2, P).transpose(3, 0, 2, 1),
        norm_w=by_channel(ssd_norm_w), rpb=table,
        dt_bias=np.concatenate([dt_bias_f, dt_bias_b], axis=1).reshape(-1),
        a_log=np.concatenate([a_log_f, a_log_b], axis=1).reshape(-1),
        ssd_d=ssd_d.reshape(-1))
    return arrays | _constants()


def build(nc, arrays):
    A = {name: nc.dram_tensor(f"in_{name}", a.shape, mybir.dt.from_np(a.dtype), kind="ExternalInput").ap()
         for name, a in arrays.items()}
    A["x_mid"] = nc.dram_tensor("x_mid", (T, DM), F32, kind="Internal").ap()
    A["out"] = nc.dram_tensor("out_x", (SEQ, DM), F32, kind="ExternalOutput").ap()
    trunk(nc, A)


def kernel(**inputs):
    import concourse.bacc as bacc
    from concourse.bass_utils import run_bass_kernel_spmd

    arrays = {k: np.ascontiguousarray(v) for k, v in _layout(**{k: np.asarray(v) for k, v in inputs.items()}).items()}
    nc = bacc.Bacc("TRN2", target_bir_lowering=False, num_devices=1)
    build(nc, arrays)
    r = run_bass_kernel_spmd(nc, [{f"in_{k}": v for k, v in arrays.items()}], core_ids=[0])
    return r.results[0]["out_x"].reshape(1, SEQ, DM)
```

```python
from contextlib import ExitStack

import numpy as np

import concourse.bass as bass
from concourse import mybir

F32 = mybir.dt.float32
F32R = mybir.dt.float32r
ACT = mybir.ActivationFunctionType
ALU = mybir.AluOpType
AX_X = mybir.AxisListType.X

P = 128
DM = 1024
KC = DM // P
SEQ, CTX, DEPTH = 1024, 256, 2
T = CTX + SEQ
NT = T // P
CT = CTX // P
LT = SEQ // P
GRID_W = 64
ROWS = SEQ // GRID_W
EPS = 1e-6
CONV, NA, SSD = 256, 512, 256
HEADS, DH = 8, 64
WIN_H, WIN_W = 8, 16
PAIRS = HEADS // 2
SH, SP_ = 4, 64
SG, SN = 2, 128
SCALE = DH ** -0.5
NEG = -1e30
TW = 16
NB_IN = 32
NB = NB_IN + DM // P
NADA = 3 * DM // P
CHUNKS = [(0, CTX), (CTX, 512), (CTX + 512, 512)]
Q0 = 16
BIG = -3.0e38
N_CONSTS = 12
SPLIT_IN = np.cumsum([0, 256, 256, 256, 256, 512, 512, 512, 512, 768, 256, 8])


def block_columns():
    s_in, s_b, s_c, s_z, q, k, v, z, xbc, ssz, _ = SPLIT_IN[:11]
    cols = []
    x, b, c = xbc, xbc + SSD, xbc + SSD + SG * SN
    cols += [c, c + P, b, b + P, x, x + P]
    cols += [ssz, ssz + P]
    for j in range(2):
        cols += [s_c + P * j, s_z + P * j, s_in + P * j, s_b + P * j]
    for j in range(PAIRS):
        cols += [v + P * j, z + P * j, q + P * j, k + P * j]
    return [int(c) for c in cols]


def window(r):
    r0 = min(max(r - WIN_H // 2, 0), ROWS - WIN_H)
    return r0, r0 - r + WIN_H - 1


def trunk(nc, A):
    ctx = ExitStack()
    with ctx:
        def sb(name, shape, dt=F32):
            return ctx.enter_context(nc.sbuf_tensor(name, shape, dt))

        def sem(name):
            return ctx.enter_context(nc.semaphore(name))

        def sems(name, n=DEPTH):
            return [sem(f"{name}{i}") for i in range(n)]

        hHi_at = (nc.sbuf_base + 31) // 32 * 32
        hHi = sb("hHi", [P, KC, T], F32R)
        hLo_at = (nc.sbuf_base + 31) // 32 * 32
        hLo = sb("hLo", [P, KC, T], F32R)
        adaF = nc.alloc_sbuf_tensor_at("adaF", [P, KC * T], F32, offset=hHi_at)
        hraw = nc.alloc_sbuf_tensor_at("hraw", [P, KC, T], F32, offset=hLo_at)
        yT_at = (nc.sbuf_base + 31) // 32 * 32
        yT = sb("yT", [P, KC, T])
        wyT = nc.alloc_sbuf_tensor_at("wyT", [P, KC * T], F32R, offset=yT_at)
        wraw = [sb(f"wraw{i}", [P, KC, P]) for i in range(2)]
        whi = [sb(f"whi{i}", [P, KC, P], F32R) for i in range(2)]
        wlo = [sb(f"wlo{i}", [P, KC, P], F32R) for i in range(2)]
        RN = 14848
        region_at = (nc.sbuf_base + 31) // 32 * 32
        R = sb("region", [P, RN])
        wada = nc.alloc_sbuf_tensor_at("wada", [P, 2 * DM], F32R, offset=region_at + 4 * 12800)
        ident = sb("ident", [P, P])
        maskF = sb("maskF", [P, P])
        maskB = sb("maskB", [P, P])
        colmask = sb("colmask", [P, GRID_W])
        ccol = sb("ccol", [P, KC, 2])
        mod = sb("mod", [P, DEPTH, NADA, 2])
        bada = sb("bada", [P, DEPTH, NADA])
        gpre = sb("gpre", [P, DEPTH, KC])
        gpost = sb("gpost", [P, DEPTH, KC])
        cw = sb("cw", [P, DEPTH, 6, 4])
        caw = sb("caw", [P, DEPTH, 2, 3])
        nrmw = sb("nrmw", [P, DEPTH, 2])
        dtb = sb("dtb", [P, DEPTH, 8])
        alog = sb("alog", [P, DEPTH, 8])
        dsk = sb("dsk", [P, DEPTH, SH])
        wdt2 = sb("wdt2", [P, KC, 16], F32R)
        st = sb("st", [P, 64])
        eps_col = sb("eps_col", [P, 1])
        sm = sb("sm", [P, 5, 80])

        def reg(a, n):
            return R[:, a:a + n]

        junk = reg(6144, DM)
        gbc = [reg(0, DM), reg(DM, DM)]
        xres = [reg(2048 + DM * i, DM) for i in range(2)]
        osb = [reg(4096 + DM * i, DM) for i in range(2)]
        xt = [reg(7168 + DM * i, DM) for i in range(3)]
        h32 = [reg(10240 + DM * i, DM).rearrange("p (k c) -> p k c", k=KC) for i in range(2)]
        adaw = [reg(12800 + DM * i, DM).rearrange("p (k c) -> p k c", k=KC) for i in range(2)]
        yflat = yT[:, :, :].rearrange("p a b -> p (a b)")
        ADA0 = [(0, 2, reg(12800, 2 * DM)), (2, 3, reg(0, 3 * DM)), (5, 3, reg(3 * DM, 3 * DM)),
                (8, 5, adaF[:, 0:5 * DM]), (13, 4, adaF[:, 5 * DM:9 * DM])]
        N0 = 17
        GATES0 = [(N0, 5, yflat[:, 0:5 * DM]), (N0 + 5, 2, yflat[:, 6 * T:6 * T + 2 * DM])]
        grow = reg(14600, P)
        CTt = [reg(T * g, T) for g in range(2)]
        BTt = [reg(2 * T + T * g, T) for g in range(2)]
        xtok = reg(5120, 2560).rearrange("p (c n) -> p c n", c=NT)
        btok = reg(7680, 2560).rearrange("p (c g n) -> p c g n", c=NT, g=SG)
        ubuf = [reg(10240 + 1284 * i, 1284) for i in range(2)]
        cv = reg(12808, T)
        rtmp = reg(14088, 512)
        dtT = cv[0:16, :]
        wdt = reg(12320, 64).rearrange("p (k n) -> p k n", k=KC)
        ztok = yT[:, 2:4, :].rearrange("p a (b n) -> p (a b) n", n=256)
        spare = yT[:, 4:6, :].rearrange("p a b -> p (a b)")
        cosT, sinT = spare[:, 0:1024], spare[:, 1024:2048]
        prevb = reg(10240, 2560).rearrange("p (c n) -> p c n", c=NT)
        Ed = [[reg(12800 + 1024 * s + 512 * d, 512).rearrange("p (h i) -> p h i", h=SH) for d in range(2)]
              for s in range(2)]
        xp = [[spare[:, 512 * d + 256 * s:512 * d + 256 * s + 256] for s in range(2)] for d in range(2)]
        xw = [spare[:, 1536 + 256 * i:1792 + 256 * i] for i in range(2)]
        prevf = [spare[:, 1024 + 256 * i:1280 + 256 * i] for i in range(2)]
        gu = spare[:, 0:T + 3]
        GM = [spare[:, 2048 + 256 * i:2304 + 256 * i].rearrange("p (g i) -> p g i", g=SG) for i in range(2)]
        late = yT[:, 6:8, :].rearrange("p a b -> p (a b)")
        gc, gz = late[:, 0:T], late[:, T:2 * T]
        rott = reg(5120, SEQ)
        yacc, yt2, yxd = [[late[:, 512 * j + 256 * i:512 * j + 256 * i + 256] for i in range(2)] for j in range(3)]
        qbd = reg(0, 2 * T).rearrange("p (g c) -> p g c", c=P)
        kT, zT = reg(2 * T, T), reg(3 * T, T)
        vtok = reg(4 * T, T).rearrange("p (c n) -> p c n", c=NT)
        vodd = reg(5 * T, P * (LT - 1)).rearrange("p (c n) -> p c n", c=LT - 1)
        tab = reg(7296, 1024).rearrange("p (k r) -> p k r", r=TW)
        Pr = [reg(8320 + 768 * i, 768) for i in range(2)]
        PT = [reg(9856 + 768 * i, 768) for i in range(2)]
        vT = reg(9856, T)
        OUT_ORDER = [0, 1, 6, 7, 2, 3, 4, 5]
        halves = lambda x: [x[:, 0:512], x[:, 512:1024]]
        flat = lambda x: x[:].rearrange("p k c -> p (k c)")
        WOUT_AT = (0, 6 * T, 2 * DM, 4 * DM)
        wout = [(halves(flat(whi[i])), halves(flat(wlo[i]))) for i in range(2)]
        wout += [(halves(wyT[:, a:a + DM]), halves(wyT[:, a + DM:a + 2 * DM])) for a in WOUT_AT]
        wout += [(halves(wada[:, 0:DM]), halves(wada[:, DM:2 * DM]))]
        wout += [(halves(wyT[:, 6 * DM:7 * DM]), [wyT[:, a:a + 512] for a in (7 * DM, 6 * T + 2 * DM)])]

        def whole(m):
            if m < 2:
                return flat(whi[m]), flat(wlo[m])
            if m == 6:
                return wada[:, 0:DM], wada[:, DM:2 * DM]
            a = WOUT_AT[m - 2]
            return wyT[:, a:a + DM], wyT[:, a + DM:a + 2 * DM]
        zr = [reg(11392 + 128 * i, 128) for i in range(2)]
        adarow = [reg(11648 + 128 * i, 128) for i in range(2)]

        ss, rstd = st[:, 0:10], st[:, 10:20]
        ss2, rstd2 = st[:, 20:30], st[:, 30:40]
        mx = [st[:, 40 + 2 * i:42 + 2 * i] for i in range(2)]
        sums = st[:, 44:52].rearrange("p (s u) -> p s u", u=2)
        inv = [st[:, 52 + 2 * i:54 + 2 * i] for i in range(2)]
        s_dt, s_ac, s_ea, s_we, s_de = [sm[:, i, :] for i in range(5)]
        s_t0, s_t1 = reg(14088, 80), reg(14168, 80)

        def dth(x, d, c):
            return x[:, 40 * d + 4 * c:40 * d + 4 * c + 4]

        def hb(x, n):
            return x.unsqueeze(2).broadcast_to([P, SH, n])

        def by_head(x, n=SP_):
            return x.rearrange("p (h n) -> p h n", h=SH)

        PS = ctx.enter_context(nc.psum_tensor("PS", [P, 4096], F32))

        def bank(b, n=1):
            return PS[:, 512 * b:512 * (b + n)]

        def diagonal(b):
            x = b.rearrange("p (h r x) -> p h r x", h=SH, r=2)[:, 0::2, 0, :]
            (pstep, pn), (gstep, gn), (xs, xn) = x.ap
            return bass.AP(tensor=x.tensor, offset=x.offset, ap=[[pstep, pn], [gstep, gn], [P + SP_, 2], [xs, xn]])

        first_consts, consts = sem("first_consts"), sem("consts")
        hlo_dve = sem("hlo_dve")
        silu_c = sem("silu_c")
        dtT_done, dtT_ready = sem("dtT_done"), sem("dtT_ready")
        eps_ok = sem("eps_ok")
        aneg_ok = sem("aneg_ok")
        ada_loaded = sems("ada_loaded", 2)
        ada_first = sems("ada_first", 7)
        ada_mm, ada_taken, mod_ready = sems("ada_mm"), sems("ada_taken"), sems("mod_ready")
        x_loaded = sems("x_loaded", 3)
        rstd_ok, xn_ready = sems("rstd_ok"), sems("xn_ready")
        sd_done = sems("sd_done")
        xnT_done, xnT_taken, h32_ready = sems("xnT_done"), sems("xnT_taken"), sems("h32_ready")
        hhi_ready, hlo_ready = sems("hhi_ready"), sems("hlo_ready")
        w_loaded = sems("w_loaded", 2)
        w_split, proj_done, proj_taken = sems("w_split"), sems("proj_done"), sems("proj_taken")
        wdt_loaded, wdt_split = sem("wdt_loaded"), sem("wdt_split")
        rope_loaded, rot_ready = sem("rope_loaded"), sem("rot_ready")
        aux_done, aux_taken = sems("aux_done"), sems("aux_taken")
        dt_abs, dt_exp = sem("dt_abs"), sem("dt_exp")
        small_in, small_exp = sem("small_in"), sem("small_exp")
        da_ready, acs_ready = sem("da_ready"), sem("acs_ready")
        convA_done, conv_done, silu_done, rope_done = (sem("convA_done"), sem("conv_done"),
                                                       sem("silu_done"), sem("rope_done"))
        xwb_ready = sem("xwb_ready")
        g_done, bc_done, g_taken, bc_taken, exp_ready = (sems("g_done"), sems("bc_done"), sems("g_taken"),
                                                          sems("bc_taken"), sems("exp_ready"))
        mix_ready, xp_ready, prevf_ready = sems("mix_ready"), sems("xp_ready"), sems("prevf_ready")
        ssd_in, fwd_in, nf_ready = sem("ssd_in"), sem("fwd_in"), sems("nf_ready")
        yo_done, stf_done, yd_done, yo_taken = (sems("yo_done"), sems("stf_done"), sems("yd_done"),
                                                sems("yo_taken"))
        y_gated, ysq_done, yn_ready, yss_done = (sems("y_gated"), sem("ysq_done"), sem("yn_ready"),
                                                 sem("yss_done"))
        tab_loaded = sems("tab_loaded")
        s_done, nm_ready, p_ready, pT_done = sems("s_done"), sems("nm_ready"), sems("p_ready"), sems("pT_done")
        ptA_ready, ptB_ready, o_done = sems("ptA_ready"), sems("ptB_ready"), sems("o_done")
        inv_ready, inv_done, yna_taken = sems("inv_ready"), sems("inv_done"), sems("yna_taken")
        row_ready, col_done = sem("row_ready"), sem("col_done")
        k_part, k_part_taken = sem("k_part"), sem("k_part_taken")
        w0_high = sem("w0_high")
        wlast_high, wlast_split = sem("wlast_high"), sem("wlast_split")
        yhi_ready, ylo_ready, ylast_ready = sems("yhi_ready"), sems("ylo_ready"), sem("ylast_ready")
        gb_done, gb_taken = sems("gb_done"), sems("gb_taken")
        out_done, osd_done, o_ready = sems("out_done"), sems("osd_done"), sems("o_ready")
        xres_loaded = sems("xres_loaded", 2)
        res_added = sems("res_added")
        stored = sems("stored", 2)
        pair_chain = sems("pair_chain")
        act_chain, dve_chain, pool_chain = sem("act_chain"), sem("dve_chain"), sem("pool_chain")

        def chunks(l, j):
            if l < DEPTH - 1:
                return CHUNKS
            full = j in (2, 3, 4, 5) or (Q0 <= j < NB_IN and (j - Q0) % 4 in (0, 3))
            return CHUNKS if full else CHUNKS[1:]

        def tiles(l):
            return list(range(NT)) if l < DEPTH - 1 else list(range(CT, NT))

        def rounds(ts):
            return [ts[i:i + 4] for i in range(0, len(ts), 4)]

        def slot_cols(j):
            base = 1536 * (j % 2) + 256
            return base

        def aux_before_states(l):
            return (3 + 4 * len(rounds(range(NT))) + 2 * len(rounds(tiles(l)))
                    + (2 * (NADA - N0) if l == 0 else 0))

        def groups(l):
            return [g for t in query_tiles(l) for g in (2 * t, 2 * t + 1)]

        def query_tiles(l):
            return list(range(CT, NT)) + [t for t in tiles(l) if t < CT]

        def aux_before_attention(l):
            return aux_before_states(l) + NT - 1 + 2 * len(rounds(tiles(l)))

        EVEN, ODD = rounds(list(range(NT))), rounds(list(range(LT - 1)))
        V_ROUNDS = len(EVEN) + len(ODD)

        def stores(l, i):
            return 16 * (l * (NT // 2) + i // 2 + 1)

        TURN_AFTER = {4: [0, 1], 7: [2, 3], 9: [4], 12: [5], 13: [6], 15: [7], 16: [8], 17: [9]}
        junk2 = late[:, 1536:1792]
        BO = [1, 0] + list(range(NT - 1, CT - 1, -1))
        x_in, x_mid = A["tokens"], A["x_mid"]

        block = ctx.enter_context(nc.Block())

        @block.sync
        def _(sp):
            for dst, src in [(ccol, "ccol"), (ident, "ident")]:
                sp.dma_start(dst[:], A[src]).then_inc(first_consts, 16)

            def load_ada(l, b):
                if b >= 2:
                    sp.wait_ge(ada_mm[l], b - 1)
                sp.dma_start(adaw[b % 2], A["w_ada"][l, b]).then_inc(ada_loaded[b % 2], 16)

            def load_w(l, j):
                if j >= 2:
                    sp.wait_ge(w_split[l], j - 1)
                elif l and j == 0:
                    sp.wait_ge(w_split[l - 1], NB - 1)
                elif l:
                    sp.wait_ge(wlast_split, l)
                sp.dma_start(wraw[j % 2][:], A["w_blocks"][l, j]).then_inc(w_loaded[j % 2], 16)

            def load_first(i):
                b, n, dst = (ADA0 + GATES0)[i]
                sp.dma_start(dst.rearrange("p (b n) -> p b n", b=n),
                             A["w_ada"][0, b:b + n].rearrange("b p k c -> p b (k c)")).then_inc(ada_first[i], 16)

            def load_x(t):
                if t >= 3:
                    sp.wait_ge(xnT_done[0], t - 2)
                sp.dma_start(xt[t % 3], x_in[P * t:P * t + P, :]).then_inc(x_loaded[t % 3], 16)

            def load_res(l, i, t):
                if i >= 2:
                    sp.wait_ge(res_added[l], i - 1)
                else:
                    sp.wait_ge(yna_taken[l], PAIRS * len(tiles(l)) + 1)
                if l:
                    sp.wait_ge(stored[t % 2], stores(0, t))
                src = x_mid if l else x_in
                sp.dma_start(xres[i % 2], src[P * t:P * t + P, :]).then_inc(xres_loaded[i % 2], 16)

            for l in range(DEPTH):
                if l == 0:
                    load_first(0)
                    for t in range(3):
                        load_x(t)
                    load_first(1)
                    load_first(2)
                    for dst, src in [(maskF, "maskF"), (maskB, "maskB"), (colmask, "colmask"),
                                     (bada, "b_ada"), (gpre, "g_pre"), (gpost, "g_post"), (cw, "conv_w"),
                                     (caw, "conv_a"), (nrmw, "norm_w")]:
                        sp.dma_start(dst[:], A[src]).then_inc(consts, 16)
                    for dst, src in [(dtb, "dt_bias"), (alog, "a_log"), (dsk, "ssd_d")]:
                        sp.dma_start(dst[:].rearrange("p l n -> p (l n)"),
                                     A[src].partition_broadcast(P)).then_inc(consts, 16)
                    load_w(l, 0)
                    load_w(l, 1)
                    sp.dma_start(wdt[:], A["w_dt"][l]).then_inc(wdt_loaded, 16)
                    load_x(3)
                    load_x(4)
                    load_first(3)
                    load_x(5)
                    load_x(6)
                    load_first(4)
                    for t in range(7, NT):
                        load_x(t)
                    load_first(5)
                    load_first(6)
                else:
                    load_w(l, 0)
                    load_w(l, 1)
                    for i, t in enumerate(tiles(l - 1)):
                        if i >= 2:
                            load_res(l - 1, i, t)
                for j in range(2, Q0):
                    load_w(l, j)
                    if j == 3:
                        if l:
                            sp.wait_ge(out_done[l - 1], NT)
                        sp.dma_start(cosT, A["rope_cos"]).then_inc(rope_loaded, 16)
                        sp.dma_start(sinT, A["rope_sin"]).then_inc(rope_loaded, 16)
                n_steps = len(groups(l))
                for hp in range(PAIRS):
                    for i in range(4):
                        load_w(l, Q0 + 4 * hp + i)
                    if hp == 0:
                        sp.wait_ge(yss_done, l + 1)
                    else:
                        sp.wait_ge(nm_ready[l], n_steps * hp)
                    for e in range(2):
                        src = bass.AP(tensor=A["rpb"].tensor,
                                      offset=(l * HEADS + 2 * hp + e) * 127 * TW,
                                      ap=[[TW, GRID_W], [1, GRID_W * TW]])
                        dst = tab[GRID_W * e:GRID_W * (e + 1)].rearrange("p k r -> p (k r)")
                        sp.dma_start(dst, src).then_inc(tab_loaded[l], 16)
                    for b in range(6):
                        if hp == PAIRS - 1 and b % 2 == 0 and b < 4:
                            load_w(l, NB_IN + b)
                            load_w(l, NB_IN + b + 1)
                        if l + 1 < DEPTH:
                            load_ada(l + 1, 6 * hp + b)
                for j in range(NB_IN + 4, NB):
                    load_w(l, j)
                for i, t in enumerate(tiles(l)[:2]):
                    load_res(l, i, t)
                if l + 1 < DEPTH:
                    sp.dma_start(wdt[:], A["w_dt"][l + 1]).then_inc(wdt_loaded, 16)
            for i, t in enumerate(tiles(DEPTH - 1)):
                if i >= 2:
                    load_res(DEPTH - 1, i, t)
            for i in (LT - 2, LT - 1):
                sp.wait_ge(stored[i % 2], stores(DEPTH - 1, i))

        @block.gpsimd
        def _(pool):
            chain = [0]

            def link(ins):
                chain[0] += 1
                ins.then_inc(pool_chain, 1)
                pool.wait_ge(pool_chain, chain[0])

            def split_w(l, j):
                s = j % 2
                pool.wait_ge(w_loaded[s], 16 * (l * (NB // 2) + j // 2 + 1))
                if j >= 2:
                    pool.wait_ge(proj_done[l], j - 1)
                elif l:
                    pool.wait_ge(out_done[l - 1], len(tiles(l - 1)))
                link(pool.tensor_copy(whi[s][:], wraw[s][:]))
                pool.tensor_tensor(wlo[s][:], wraw[s][:], whi[s][:].bitcast(F32), ALU.subtract).then_inc(w_split[l], 1)

            def back_input(l, i):
                if i == 0:
                    pool.wait_ge(ssd_in, l + 1)
                if i >= 2:
                    pool.wait_ge(aux_done[l], aux_before_states(l) + i - 1)
                nc.gpsimd.tensor_tensor(by_head(xw[i % 2]), by_head(xtok[:, BO[i], :]), hb(dth(s_we, 1, BO[i]), SP_),
                                        ALU.mult).then_inc(xwb_ready, 1)

            def ssd_inputs(l):
                TT = nc.gpsimd.tensor_tensor
                y0, a0 = tiles(l)[0], aux_before_states(l)

                def scaled(c):
                    s, yi = c % 2, c - y0
                    x_c = by_head(xtok[:, c, :])
                    if c < 2:
                        pool.wait_ge(aux_done[l], a0 + NT - 1)
                    else:
                        pool.wait_ge(stf_done[l], c - 1)
                    if c < NT - 1:
                        last = TT(by_head(xw[s]), x_c, hb(dth(s_we, 0, c), SP_), ALU.mult)
                    if c == 0:
                        pool.wait_ge(fwd_in, l + 1)
                    if yi >= 2:
                        pool.wait_ge(y_gated[l], yi - 1)
                    if yi >= 0:
                        for d in range(2):
                            TT(by_head(xp[d][s]), x_c, hb(dth(s_dt, d, c), SP_), ALU.mult)
                        last = TT(by_head(yxd[s]), x_c, hb(dsk[:, l], SP_), ALU.mult)
                    last.then_inc(xp_ready[l], 1)

                scaled(0)
                for c in range(NT):
                    if c + 1 < NT:
                        if c:
                            pool.wait_ge(prevf_ready[l], c)
                        if c > y0:
                            pool.wait_ge(yo_done[l], c - y0)
                        TT(by_head(prevf[(c + 1) % 2]), by_head(prevf[c % 2]), hb(dth(s_de, 0, c), SP_),
                           ALU.mult).then_inc(nf_ready[l], 1)
                        scaled(c + 1)

            def residual(l, i, t):
                pool.wait_ge(o_ready[l], i + 1)
                pool.wait_ge(xres_loaded[i % 2], stores(l, i))
                link(pool.tensor_tensor(osb[i % 2], osb[i % 2], xres[i % 2], ALU.add))
                pool.sem_inc(res_added[l], 1)
                dst = x_mid[P * t:P * t + P, :] if l < DEPTH - 1 else A["out"][P * (t - CT):P * (t - CT) + P, :]
                pool.dma_start(dst, osb[i % 2]).then_inc(stored[i % 2], 16)

            def low_part(l, t):
                pool.wait_ge(hhi_ready[l], t + 1)
                c = slice(P * t, P * t + P)
                pool.tensor_tensor(hLo[:, :, c], h32[t % 2], hHi[:, :, c].bitcast(F32), ALU.subtract).then_inc(hlo_ready[l], 1)

            def split_out(l, m):
                s, j = m % 2, NB_IN + m
                pool.wait_ge(w_loaded[s], 16 * (l * (NB // 2) + j // 2 + 1))
                if m < 2:
                    pool.wait_ge(proj_done[l], j - 1)
                elif m == 6:
                    if l + 1 < DEPTH:
                        pool.wait_ge(ada_mm[l + 1], NADA)
                if m in (2, 3, 4, 5):
                    pool.wait_ge(ylo_ready[l], (2, 4, 6, 7)[m - 2])
                hi, lo = whole(m)
                link(pool.tensor_copy(hi, flat(wraw[s])))
                pool.tensor_tensor(lo, flat(wraw[s]), hi.bitcast(F32), ALU.subtract).then_inc(w_split[l], 1)

            def y_low(l, m):
                k, o = OUT_ORDER[m], P * tiles(l)[0]
                pool.wait_ge(yhi_ready[l], m + 1)
                pool.tensor_tensor(hLo[:, k, o:T], yT[:, k, o:T], hHi[:, k, o:T].bitcast(F32), ALU.subtract).then_inc(ylo_ready[l], 1)

            for l in range(DEPTH):
                if l == 0:
                    split_w(l, 0)
                    split_w(l, 1)
                    for k in range(1, KC, 2):
                        pool.wait_ge(h32_ready[0], k + 1)
                        pool.tensor_tensor(hLo[:, k, :], hraw[:, k, :], hHi[:, k, :].bitcast(F32),
                                           ALU.subtract).then_inc(hlo_ready[0], 1)
                for j in range(2, Q0 + 2):
                    split_w(l, j)
                    if j >= 11:
                        for i in range(2 * (j - 11), min(2 * (j - 11) + 2, NT - 1)):
                            back_input(l, i)
                ssd_inputs(l)
                for j in range(Q0 + 2, NB_IN):
                    split_w(l, j)
                split_out(l, 0)
                split_out(l, 1)
                for m in range(3):
                    y_low(l, 2 * m)
                    y_low(l, 2 * m + 1)
                    split_out(l, 2 + m)
                y_low(l, 6)
                split_out(l, 5)
                split_out(l, 6)
                for i, t in enumerate(tiles(l)):
                    if l + 1 < DEPTH and t == NT - 1:
                        pool.wait_ge(w0_high, l + 1)
                        pool.tensor_tensor(wlo[0][:], wraw[0][:], whi[0][:].bitcast(F32), ALU.subtract).then_inc(w_split[l + 1], 1)
                    residual(l, i, t)
                    if l + 1 < DEPTH:
                        if i:
                            low_part(l + 1, t - 1)
                if l + 1 < DEPTH:
                    low_part(l + 1, NT - 1)
                    split_w(l + 1, 1)

        @block.scalar
        def _(act):
            chain = [0]

            def link(ins):
                chain[0] += 1
                ins.then_inc(act_chain, 1)
                act.wait_ge(act_chain, chain[0])

            def take(l, j, dst, func=ACT.Copy, scale=1.0, padded=False):
                act.wait_ge(proj_done[l], j + 1)
                b = slot_cols(j)
                if padded:
                    if len(chunks(l, j)) == 3:
                        nc.scalar.activation(dst[:, 1:1 + CTX], PS[:, b:b + CTX], func, scale=scale)
                    last = nc.scalar.activation(dst[:, 2 + CTX:2 + CTX + SEQ], PS[:, b + CTX:b + T], func, scale=scale)
                else:
                    o = 0 if len(chunks(l, j)) == 3 else CTX
                    last = nc.scalar.activation(dst[:, o:T], PS[:, b + o:b + T], func, scale=scale)
                last.then_inc(proj_taken[l], 1)

            def norm_stats(l, t):
                if l == 0:
                    act.wait_ge(x_loaded[t % 3], 16 * (t // 3 + 1))
                    src = xt[t % 3]
                else:
                    act.wait_ge(res_added[l - 1], t + 1)
                    src = osb[t % 2]
                link(nc.scalar.activation(junk, src, ACT.Square, accum_out=ss[:, t:t + 1]))
                nc.scalar.activation(rstd[:, t:t + 1], ss[:, t:t + 1], ACT.Sqrt, scale=1.0 / DM,
                                     bias=eps_col[:, 0:1]).then_inc(sd_done[l], 1)
                act.wait_ge(rstd_ok[l], t + 1)
                if l and t >= 3:
                    act.wait_ge(xnT_done[l], t - 2)
                nc.scalar.activation(xt[t % 3], src, ACT.Copy, scale=rstd[:, t:t + 1]).then_inc(xn_ready[l], 1)

            def high_part(l, t):
                act.wait_ge(h32_ready[l], t + 1)
                nc.scalar.activation(hHi[:, :, P * t:P * t + P], h32[t % 2], ACT.Copy).then_inc(hhi_ready[l], 1)

            act.wait_ge(first_consts, 32)
            act.wait_ge(eps_ok, 1)
            link(nc.scalar.activation(ccol[:], ccol[:], ACT.Silu))
            act.sem_inc(silu_c, 1)

            for l in range(DEPTH):
                if l == 0:
                    for t in range(NT):
                        norm_stats(l, t)
                    act.wait_ge(consts, 16 * N_CONSTS)
                    nc.scalar.activation(alog[:], alog[:], ACT.Exp).then_inc(aneg_ok, 1)
                    act.wait_ge(mod_ready[0], 1)
                    act.wait_ge(xnT_taken[0], NT)
                    for k in range(KC):
                        for v, a, n in ((1, 0, CTX), (0, CTX, SEQ)):
                            last = nc.scalar.activation(hHi[:, k, a:a + n], hraw[:, k, a:a + n], ACT.Identity,
                                                        scale=mod[:, 0, KC + k, v:v + 1], bias=mod[:, 0, k, v:v + 1])
                        last.then_inc(hhi_ready[0], 1)

                def silu(j):
                    act.wait_ge(conv_done, 6 * l + j + 1)
                    o = 0 if len(chunks(l, j)) == 3 else CTX
                    dst = {0: CTt[0], 1: CTt[1], 2: BTt[0], 3: BTt[1], 4: cv, 5: cv}[j]
                    nc.scalar.activation(dst[:, o:T], cv[:, o:T], ACT.Silu).then_inc(silu_done, 1)
                    if j < 4:
                        act.wait_ge(silu_done, 6 * l + j + 1)
                        if j:
                            act.wait_ge(rope_done, 4 * l + j)
                        for a in range(0, P, 64):
                            nc.scalar.activation(rott[a:a + 32], dst[a + 32:a + 64, CTX:T], ACT.Copy, scale=-1.0)
                            last = nc.scalar.activation(rott[a + 32:a + 64], dst[a:a + 32, CTX:T], ACT.Copy)
                        last.then_inc(rot_ready, 1)

                if l:
                    for i in (NT - 2, NT - 1):
                        act.wait_ge(stored[i % 2], stores(l - 1, i))
                for j in range(6):
                    if j == 0:
                        act.wait_ge(dtT_ready, l + 1)
                    if j >= 2:
                        act.wait_ge(conv_done, 6 * l + j - 1)
                    take(l, j, ubuf[j % 2], padded=True)
                    if j == 0:
                        act.wait_ge(dt_abs, l + 1)
                        nc.scalar.activation(s_t1, s_t1, ACT.Exp, scale=-1.0).then_inc(dt_exp, 1)
                    if j == 2:
                        act.wait_ge(small_in, l + 1)
                        nc.scalar.activation(s_ea, s_ac, ACT.Exp)
                        nc.scalar.activation(s_we, s_we, ACT.Exp)
                        nc.scalar.activation(s_de, s_de, ACT.Exp).then_inc(small_exp, 1)
                    silu(j)
                take(l, 6, ubuf[0], ACT.Silu)
                take(l, 7, ubuf[1], ACT.Silu)
                act.wait_ge(silu_done, 6 * l + 6)
                for j2 in range(2):
                    if j2:
                        act.wait_ge(proj_taken[l], 12)
                    take(l, 8 + 4 * j2, gc)
                    if j2:
                        act.wait_ge(convA_done, 2 * l + 1)
                    take(l, 9 + 4 * j2, gz, ACT.Silu)
                act.wait_ge(convA_done, 2 * l + 2)

                ys = tiles(l)

                def square(i):
                    act.wait_ge(y_gated[l], i + 1)
                    c = ys[i]
                    link(nc.scalar.activation(junk2, ztok[:, c, :], ACT.Square, accum_out=ss[:, c:c + 1]))

                for i, c in enumerate(ys):
                    for d in range(2):
                        act.wait_ge(bc_done[l], 2 * i + d + 1)
                        if i >= 2:
                            act.wait_ge(yd_done[l], i - 1)
                        e = Ed[i % 2][d]
                        for h in range(SH):
                            last = nc.scalar.activation(e[:, h, :], bank(1 + d)[:, P * h:P * h + P], ACT.Relu,
                                                        scale=-1.0, bias=dth(s_ac, d, c)[:, h:h + 1])
                        last.then_inc(bc_taken[l], 1)
                        act.wait_ge(bc_taken[l], 2 * i + d + 1)
                        nc.scalar.activation(e, e, ACT.Exp, scale=-1.0).then_inc(exp_ready[l], 1)
                    if i >= 2:
                        square(i - 2)
                square(len(ys) - 2)
                square(len(ys) - 1)
                a = ys[0]
                nc.scalar.activation(rstd[:, a:NT], ss[:, a:NT], ACT.Sqrt, scale=1.0 / SSD,
                                     bias=eps_col[:, 0:1]).then_inc(ysq_done, 1)

                steps = groups(l)
                n = len(steps)

                def soft(hp, i):
                    s = i % 2
                    act.wait_ge(nm_ready[l], hp * n + i + 1)
                    if steps[i] >= 2 * CT:
                        nc.scalar.activation(Pr[s][:, 0:512], Pr[s][:, 0:512], ACT.Exp, bias=mx[s][:, 1:2],
                                             accum_out=sums[:, i % 4, 0:1])
                    nc.scalar.activation(Pr[s][:, 512:768], bank(2 * s + 1)[:, 0:256], ACT.Exp, bias=mx[s][:, 1:2],
                                         accum_out=sums[:, i % 4, 1:2]).then_inc(p_ready[l], 1)

                def pt_context(hp, i):
                    act.wait_ge(pT_done[l], hp * n + i + 1)
                    nc.scalar.activation(PT[i % 2][:, 512:768], bank(5)[:, 0:256], ACT.Copy).then_inc(ptB_ready[l], 1)

                def y_high(m):
                    k, o = OUT_ORDER[m], P * tiles(l)[0]
                    nc.scalar.activation(hHi[:, k, o:T], yT[:, k, o:T], ACT.Copy).then_inc(yhi_ready[l], 1)

                def pair(hp, last_pair=False):
                    for i, (dst, func) in enumerate([(vT, ACT.Copy), (zT, ACT.Silu), (None, ACT.Copy)]):
                        j = Q0 + i
                        act.wait_ge(proj_done[l], 4 * hp + (j + 1))
                        if i == 1:
                            act.wait_ge(yna_taken[l], hp * len(tiles(l)) + 1)
                        b = slot_cols(j)
                        o = 0 if len(chunks(l, j)) == 3 else CTX
                        if i == 2:
                            for e in range(2):
                                r = slice(64 * e, 64 * e + 64)
                                src = PS[r, b + o:b + T].rearrange("p (g c) -> p g c", c=64)
                                last = nc.scalar.activation(qbd[r, o // 64:, 64 * e:64 * e + 64], src, func, scale=SCALE)
                        else:
                            last = nc.scalar.activation(dst[:, o:T], PS[:, b + o:b + T], func)
                        last.then_inc(proj_taken[l], 1)
                    b, a = slot_cols(Q0 + 3), CHUNKS[-1][0]
                    act.wait_ge(k_part, hp + (PAIRS * l + 1))
                    nc.scalar.activation(kT[:, 0:a], PS[:, b:b + a], ACT.Copy).then_inc(k_part_taken, 1)
                    soft(hp, 0)
                    act.wait_ge(proj_done[l], 4 * hp + (Q0 + 4))
                    nc.scalar.activation(kT[:, a:T], PS[:, b + a:b + T], ACT.Copy).then_inc(proj_taken[l], 1)
                    for i in range(n):
                        if i + 1 < n:
                            soft(hp, i + 1)
                        if i == 0:
                            act.wait_ge(aux_taken[l], V_ROUNDS * hp + (aux_before_attention(l) + V_ROUNDS))
                        pt_context(hp, i)
                        if last_pair and i % 2 == 0 and i // 2 < KC - 1:
                            if i == 0:
                                act.wait_ge(yss_done, l + 1)
                                act.wait_ge(yna_taken[l], (PAIRS - 1) * len(tiles(l)) + 1)
                                act.wait_ge(proj_done[l], NB_IN)
                            y_high(i // 2)

                with act.Fori(0, PAIRS - 1) as hp:
                    pair(hp)
                pair(PAIRS - 1, last_pair=True)
                act.wait_ge(yna_taken[l], PAIRS * len(tiles(l)) + 1)
                y_high(KC - 1)
                act.wait_ge(w_loaded[1], 16 * (l + 1) * (NB // 2))
                act.wait_ge(ylo_ready[l], KC - 1)
                act.wait_ge(ylast_ready, l + 1)
                for to, raw in zip(wout[KC - 1][0], halves(flat(wraw[1]))):
                    last = nc.scalar.activation(to, raw, ACT.Copy)
                last.then_inc(wlast_high, 1)
                for i, t in enumerate(tiles(l)):
                    act.wait_ge(out_done[l], i + 1)
                    if l + 1 < DEPTH and t == NT - 1:
                        act.wait_ge(w_loaded[0], 16 * ((l + 1) * (NB // 2) + 1))
                        nc.scalar.activation(whi[0][:], wraw[0][:], ACT.Copy).then_inc(w0_high, 1)
                    link(nc.scalar.activation(junk, bank(2 * (i % 2), 2), ACT.Square, accum_out=ss2[:, t:t + 1]))
                    nc.scalar.activation(rstd2[:, t:t + 1], ss2[:, t:t + 1], ACT.Sqrt, scale=1.0 / DM,
                                         bias=eps_col[:, 0:1]).then_inc(osd_done[l], 1)
                    if l + 1 < DEPTH:
                        if i:
                            high_part(l + 1, t - 1)
                        norm_stats(l + 1, t)
                if l + 1 < DEPTH:
                    high_part(l + 1, NT - 1)

        @block.vector
        def _(dve):
            chain = [0]

            def link(ins):
                chain[0] += 1
                ins.then_inc(dve_chain, 1)
                dve.wait_ge(dve_chain, chain[0])

            TT, TS, STT = nc.vector.tensor_tensor, nc.vector.tensor_scalar, nc.vector.scalar_tensor_tensor
            nc.vector.memset(eps_col[:], EPS).then_inc(eps_ok, 1)

            def ada_take(l, b):
                if b < N0:
                    dve.wait_ge(ada_mm[l], b + 1)
                    nc.vector.tensor_copy(adarow[b % 2][0:2, :], bank(b % 4)[0:2, 384:512]).then_inc(row_ready, 1)
                if b:
                    dve.wait_ge(col_done, b)
                    nc.vector.tensor_copy(mod[:, l, b - 1, :], bank((b - 1) % 4)[:, 256:258]).then_inc(ada_taken[l], 1)

            def finish_mod(l, a, b):
                link(TT(mod[:, l, a:b], mod[:, l, a:b], bada[:, l, a:b].unsqueeze(2).broadcast_to([P, b - a, 2]), ALU.add))
                for v in range(2):
                    if a == 0:
                        last = STT(mod[:, l, KC:2 * KC, v], mod[:, l, KC:2 * KC, v], 1.0, gpre[:, l], ALU.add, ALU.mult)
                    if b == NADA:
                        last = TT(mod[:, l, 2 * KC:, v], mod[:, l, 2 * KC:, v], gpost[:, l], ALU.mult)
                link(last)
                if a == 0:
                    dve.sem_inc(mod_ready[l], 1)

            def norm_rstd(l, t):
                dve.wait_ge(sd_done[l], t + 1)
                nc.vector.reciprocal(rstd[:, t:t + 1], rstd[:, t:t + 1]).then_inc(rstd_ok[l], 1)

            def norm_mod(l, t):
                v = 1 if t < CT else 0
                dve.wait_ge(xnT_done[l], t + 1)
                if t >= 2:
                    dve.wait_ge(hlo_ready[l], t - 1)
                src = bank(4 + 2 * (t % 2), 2).rearrange("p (k c) -> p k c", k=KC)
                TT(h32[t % 2], src, mod[:, l, KC:2 * KC, v].unsqueeze(2).broadcast_to([P, KC, P]), ALU.mult).then_inc(xnT_taken[l], 1)
                dve.wait_ge(xnT_taken[l], t + 1)
                TT(h32[t % 2], h32[t % 2], mod[:, l, 0:KC, v].unsqueeze(2).broadcast_to([P, KC, P]),
                   ALU.add).then_inc(h32_ready[l], 1)

            def split_wdt(l):
                dve.wait_ge(wdt_loaded, 16 * (l + 1))
                link(nc.vector.tensor_copy(wdt2[:, :, 0:8], wdt[:]))
                TT(wdt2[:, :, 8:16], wdt[:], wdt2[:, :, 0:8].bitcast(F32), ALU.subtract).then_inc(wdt_split, 1)

            for b in range(N0 + 1):
                for t in TURN_AFTER.get(b, []):
                    norm_rstd(0, t)
                ada_take(0, b)
                if b == 12:
                    split_wdt(0)
                if b == N0:
                    dve.wait_ge(consts, 16 * N_CONSTS)
                    dve.wait_ge(ada_taken[0], N0)
                    finish_mod(0, 0, 2 * KC)
                for t in TURN_AFTER.get(b, []):
                    dve.wait_ge(xnT_done[0], t + 1)
                    nc.vector.tensor_copy(hraw[:, :, P * t:P * t + P], bank(4 + 2 * (t % 2), 2).rearrange(
                        "p (k c) -> p k c", k=KC)).then_inc(xnT_taken[0], 1)
            dve.wait_ge(xnT_taken[0], NT)
            for k in range(KC):
                dve.wait_ge(hhi_ready[0], k + 1)
                for v, a, n in ((1, 0, CTX), (0, CTX, SEQ)):
                    last = TS(hraw[:, k, a:a + n], hraw[:, k, a:a + n], mod[:, 0, KC + k, v:v + 1],
                              mod[:, 0, k, v:v + 1], ALU.mult, ALU.add)
                last.then_inc(h32_ready[0], 1)
                if k % 2 == 0:
                    dve.wait_ge(h32_ready[0], k + 1)
                    TT(hLo[:, k, :], hraw[:, k, :], hHi[:, k, :].bitcast(F32), ALU.subtract).then_inc(hlo_dve, 1)
            dve.wait_ge(aneg_ok, 1)
            link(TS(alog[:], alog[:], -1.0, None, ALU.mult))

            for l in range(DEPTH):
                aux = [0]

                def aux_wait():
                    dve.wait_ge(aux_done[l], aux[0] + 1)
                    b = bank(6 + aux[0] % 2)
                    aux[0] += 1
                    return b

                dve.wait_ge(dtT_done, l + 1)
                nc.vector.tensor_copy(dtT[:, 0:CTX], bank(0 if l else 3)[0:16, 0:CTX])
                nc.vector.tensor_copy(dtT[:, CTX:T], bank(4, 2)[0:16, :]).then_inc(dtT_ready, 1)
                raw = aux_wait()
                bias = dtb[:, l].rearrange("p (d h) -> p d h", d=2).unsqueeze(2).broadcast_to([P, 2, NT, SH])
                v4 = lambda x: x.rearrange("p (d c h) -> p d c h", d=2, c=NT)
                raw = raw[:, 0:160].rearrange("p (c w d h) -> p w d c h", w=2, d=2, c=NT)
                link(TT(v4(s_t0), raw[:, 0], bias, ALU.add))
                link(TT(v4(s_t0), raw[:, 1], v4(s_t0), ALU.add))
                dve.sem_inc(aux_taken[l], 1)
                link(TS(s_t1, s_t0, -1.0, None, ALU.mult))
                TT(s_t1, s_t0, s_t1, ALU.max).then_inc(dt_abs, 1)
                dve.wait_ge(dt_exp, l + 1)
                link(TS(s_dt, s_t1, 2.0, None, ALU.add))
                link(nc.vector.reciprocal(s_dt, s_dt))
                link(TT(s_t1, s_t1, s_dt, ALU.mult))
                link(TT(s_dt, s_t1, s_t1, ALU.mult))
                link(TS(s_we, s_dt, 1.0 / 17, None, ALU.mult))
                for k in range(7, 0, -1):
                    link(STT(s_we, s_we, 1.0 / (2 * k + 1), s_dt, ALU.add, ALU.mult))
                link(STT(s_we, s_we, 1.0, s_t1, ALU.add, ALU.mult))
                link(TS(s_t0, s_t0, 0.0, None, ALU.max))
                link(STT(s_dt, s_we, 2.0, s_t0, ALU.mult, ALU.add))
                an = alog[:, l].rearrange("p (d h) -> p d h", d=2).unsqueeze(2).broadcast_to([P, 2, NT, SH])
                TT(v4(s_t0), v4(s_dt), an, ALU.mult).then_inc(da_ready, 1)
                def gate_input(j2):
                    j = 10 + 4 * j2
                    dve.wait_ge(proj_done[l], j + 1)
                    dve.wait_ge(proj_taken[l], j)
                    o, b = P * tiles(l)[0], slot_cols(j)
                    if o == 0:
                        TT(gu[:, 1:1 + CTX], PS[:, b:b + CTX], gc[:, 0:CTX], ALU.mult)
                    TT(gu[:, 2 + CTX:2 + T], PS[:, b + CTX:b + T], gc[:, CTX:T], ALU.mult).then_inc(proj_taken[l], 1)
                    dve.wait_ge(proj_taken[l], j + 1)
                    link(conv_taps(gu, caw[:, l, j2], None, o))

                def gate_output(j2):
                    j = 11 + 4 * j2
                    dve.wait_ge(proj_done[l], j + 1)
                    o, b = P * tiles(l)[0], slot_cols(j)
                    TT(cv[:, o:T], cv[:, o:T], PS[:, b + o:b + T], ALU.mult).then_inc(proj_taken[l], 1)
                    dve.wait_ge(proj_taken[l], j + 1)
                    TT(yT[:, j2, o:T], cv[:, o:T], gz[:, o:T], ALU.mult).then_inc(convA_done, 1)
                    dve.wait_ge(convA_done, 2 * l + j2 + 1)

                def conv_taps(u, w, b, o):
                    spans = ([(0, 0, CTX)] if o == 0 else []) + [(CTX, CTX + 1, SEQ)]
                    for a, s, n in spans:
                        if b is None:
                            last = TS(cv[:, a:a + n], u[:, s:s + n], w[:, 0:1], None, ALU.mult)
                        else:
                            last = TS(cv[:, a:a + n], u[:, s:s + n], w[:, 0:1], b, ALU.mult, ALU.add)
                    link(last)
                    for k in (1, 2):
                        for a, s, n in spans:
                            last = STT(cv[:, a:a + n], u[:, s + k:s + k + n], w[:, k:k + 1], cv[:, a:a + n],
                                       ALU.mult, ALU.add)
                        if k == 1:
                            link(last)
                    return last

                def zero_ends(u):
                    for a in (0, 1 + CTX, 2 + T):
                        last = nc.vector.memset(u[:, a:a + 1], 0.0)
                    return last

                def conv(j):
                    dve.wait_ge(proj_taken[l], j + 1)
                    if j:
                        dve.wait_ge(silu_done, 6 * l + j)
                    o = 0 if len(chunks(l, j)) == 3 else CTX
                    conv_taps(ubuf[j % 2], cw[:, l, j], cw[:, l, j, 3:4], o).then_inc(conv_done, 1)

                def rope(j):
                    dst = {0: CTt[0], 1: CTt[1], 2: BTt[0], 3: BTt[1]}[j]
                    if j == 0:
                        dve.wait_ge(rope_loaded, 32 * (l + 1))
                    lat = slice(CTX, T)
                    dve.wait_ge(rot_ready, 4 * l + j + 1)
                    TT(rott, rott, sinT, ALU.mult)
                    link(TT(dst[:, lat], dst[:, lat], cosT, ALU.mult))
                    last = TT(dst[:, lat], dst[:, lat], rott, ALU.add)
                    last.then_inc(rope_done, 1)
                    dve.wait_ge(rope_done, 4 * l + j + 1)

                def to_tok(dst, r):
                    b = aux_wait()
                    nc.vector.tensor_copy(dst[:, r[0]:r[-1] + 1], b[:, 0:P * len(r)].rearrange("p (c n) -> p c n", n=P)).then_inc(aux_taken[l], 1)
                    dve.wait_ge(aux_taken[l], aux[0])

                def back_state(i):
                    c, nxt = BO[i], BO[i + 1]
                    link(TT(by_head(prevb[:, nxt, :]), by_head(prevb[:, c, :]), hb(dth(s_de, 1, c), SP_), ALU.mult))
                    b = aux_wait()
                    TT(prevb[:, nxt, :], prevb[:, nxt, :], b[:, 0:256], ALU.add).then_inc(aux_taken[l], 1)
                    dve.wait_ge(aux_taken[l], aux[0])

                def gate_row():
                    if l == 0:
                        b = aux_wait()
                        nc.vector.tensor_copy(grow[0:2, :], b[0:2, 0:P]).then_inc(aux_taken[l], 1)

                def gate_column(n):
                    if l == 0:
                        b = aux_wait()
                        nc.vector.tensor_copy(mod[:, 0, n, :], b[:, 0:2]).then_inc(aux_taken[l], 1)

                ALL, OWN = rounds(range(NT)), rounds(tiles(l))
                zero_ends(ubuf[0])
                link(zero_ends(ubuf[1]))
                conv(0)
                cs = aux_wait()
                nc.vector.tensor_copy(s_ac, cs[:, 0:80]).then_inc(aux_taken[l], 1)
                dve.wait_ge(aux_taken[l], 2)
                dve.sem_inc(acs_ready, 1)
                rope(0)
                conv(1)
                rope(1)
                ends = aux_wait()
                nc.vector.tensor_copy(s_de, ends[:, 0:80]).then_inc(aux_taken[l], 1)
                dve.wait_ge(aux_taken[l], aux[0])
                link(TT(s_we, s_de, s_ac, ALU.subtract))
                link(TS(s_we, s_we, 0.0, None, ALU.min))
                dve.sem_inc(small_in, 1)
                conv(2)
                rope(2)
                conv(3)
                rope(3)
                conv(4)
                gate_row()
                to_tok(btok[:, :, 0, :], ALL[0])
                to_tok(btok[:, :, 0, :], ALL[1])
                for r in ALL:
                    to_tok(xtok[:, :, 0:P], r)
                conv(5)
                gate_column(22)
                to_tok(btok[:, :, 0, :], ALL[2])
                gate_row()
                to_tok(btok[:, :, 1, :], ALL[0])
                gate_column(23)
                gate_row()
                to_tok(btok[:, :, 1, :], ALL[1])
                gate_column(21)
                to_tok(btok[:, :, 1, :], ALL[2])
                gate_row()
                to_tok(xtok[:, :, P:2 * P], ALL[0])
                gate_column(20)
                gate_row()
                to_tok(xtok[:, :, P:2 * P], ALL[1])
                gate_column(19)
                to_tok(xtok[:, :, P:2 * P], ALL[2])
                dve.wait_ge(small_exp, l + 1)
                link(TT(s_we, s_we, s_dt, ALU.mult))
                dve.sem_inc(ssd_in, 1)
                for i, (j2, r) in enumerate((j2, r) for j2 in range(2) for r in OWN):
                    if i == 1:
                        gate_row()
                    if i == 2:
                        gate_column(18)
                    if i == 3:
                        gate_row()
                    to_tok(ztok[:, :, P * j2:P * j2 + P], r)
                    if i == 3:
                        gate_column(17)
                if l == 0:
                    dve.wait_ge(aux_taken[l], aux[0])
                    finish_mod(0, 2 * KC, NADA)
                nc.vector.memset(prevb[:, BO[0], :], 0.0)
                link(zero_ends(gu))
                gate_input(0)
                back_state(0)
                back_state(1)
                gate_output(0)
                for i in range(2, 8):
                    back_state(i)
                gate_input(1)
                back_state(8)
                gate_output(1)
                link(nc.vector.memset(prevf[0], 0.0))
                dve.sem_inc(fwd_in, 1)

                ys = tiles(l)

                def mix(i):
                    dve.wait_ge(g_done[l], i + 1)
                    gsrc = bank(7 * (i % 2))[:, 0:256].rearrange("p (g i) -> p g i", g=SG)
                    TT(GM[0], gsrc, maskF[:].unsqueeze(1).broadcast_to([P, SG, P]), ALU.mult)
                    link(TT(GM[1], gsrc, maskB[:].unsqueeze(1).broadcast_to([P, SG, P]), ALU.mult))
                    dve.sem_inc(g_taken[l], 1)
                    for d in range(2):
                        dve.wait_ge(exp_ready[l], 2 * i + d + 1)
                        e = Ed[i % 2][d].rearrange("p (g r) i -> p g r i", g=SG)
                        last = TT(e, e, GM[d].unsqueeze(2).broadcast_to([P, SG, SH // SG, P]), ALU.mult)
                    last.then_inc(mix_ready[l], 1)

                mix(0)
                for c in range(NT):
                    yi, s = c - ys[0], c % 2
                    if c < NT - 1:
                        nf = prevf[(c + 1) % 2]
                        dve.wait_ge(nf_ready[l], c + 1)
                        dve.wait_ge(stf_done[l], c + 1)
                        TT(nf, nf, bank(5)[:, 0:256], ALU.add).then_inc(prevf_ready[l], 1)
                    if yi < 0:
                        continue
                    dve.wait_ge(yo_done[l], yi + 1)
                    yo = bank(4)
                    TT(by_head(yacc[s]), by_head(yo[:, 0:256]), hb(dth(s_ea, 0, c), SP_), ALU.mult)
                    link(TT(by_head(yt2[s]), by_head(yo[:, 256:512]), hb(dth(s_ea, 1, c), SP_), ALU.mult))
                    dve.sem_inc(yo_taken[l], 1)
                    link(TT(yacc[s], yacc[s], yt2[s], ALU.add))
                    dve.wait_ge(xp_ready[l], c + 1)
                    link(TT(yacc[s], yacc[s], yxd[s], ALU.add))
                    if yi + 1 < len(ys):
                        mix(yi + 1)
                    dve.wait_ge(yd_done[l], yi + 1)
                    y4 = yacc[s].rearrange("p (g r x) -> p g r x", g=SG, r=2)
                    link(TT(y4, y4, diagonal(bank(3 if yi % 2 else 6)), ALU.add))
                    TT(ztok[:, c, :], ztok[:, c, :], yacc[s], ALU.mult).then_inc(y_gated[l], 1)
                a = ys[0]
                dve.wait_ge(ysq_done, l + 1)
                link(nc.vector.reciprocal(rstd[:, a:NT], rstd[:, a:NT]))
                TT(ztok[:, a:NT, :], ztok[:, a:NT, :], rstd[:, a:NT].unsqueeze(2).broadcast_to([P, NT - a, 256]),
                   ALU.mult).then_inc(yn_ready, 1)
                for j in range(2):
                    for r in rounds(ys):
                        b = aux_wait()
                        TS(yT[:, 6 + j, P * r[0]:P * (r[-1] + 1)], b[:, 0:P * len(r)], nrmw[:, l, j:j + 1], None,
                           ALU.mult).then_inc(aux_taken[l], 1)
                dve.wait_ge(aux_taken[l], aux[0])
                dve.sem_inc(yss_done, 1)

                steps = groups(l)
                n = len(steps)
                aux0 = aux[0]
                assert aux0 == aux_before_attention(l)
                pair_links = 1 + n + n // 2 + len(tiles(l)) - sum(t < CT for t in tiles(l))
                linked = [0]

                def link_pair(hp, ins):
                    linked[0] += 1
                    ins.then_inc(pair_chain[l], 1)
                    dve.wait_ge(pair_chain[l], hp * pair_links + linked[0])

                def row_max(hp, i):
                    s = i % 2
                    dve.wait_ge(s_done[l], hp * n + i + 1)
                    top = nc.vector.tensor_reduce(mx[s][:, 0:1], bank(2 * s + 1)[:, 0:256], AX_X, ALU.max)
                    ada_turn(hp, i)
                    if steps[i] >= 2 * CT:
                        _, first = window(steps[i] - 2 * CT)
                        link_pair(hp, nc.vector.tensor_tensor_reduce(
                            out=Pr[s][:, 0:512].rearrange("p (r k) -> p r k", k=64),
                            in0=bank(2 * s).rearrange("p (r k) -> p r k", k=64),
                            in1=tab[:, :, first:first + WIN_H].rearrange("p k r -> p r k")[:, :, ::-1],
                            scale=1.0, scalar=BIG, op0=ALU.add, op1=ALU.max, accum_out=mx[s][:, 1:2]))
                        TS(mx[s][:, 1:2], mx[s][:, 1:2], mx[s][:, 0:1], -1.0, ALU.max,
                           ALU.mult).then_inc(nm_ready[l], 1)
                    else:
                        link_pair(hp, top)
                        TS(mx[s][:, 1:2], mx[s][:, 0:1], -1.0, None, ALU.mult).then_inc(nm_ready[l], 1)

                def inverse_sums(hp, k):
                    s4 = (2 * k) % 4
                    dve.wait_ge(p_ready[l], hp * n + 2 * k + 2)
                    if query_tiles(l)[k] >= CT:
                        link_pair(hp, TT(inv[k % 2], sums[:, s4:s4 + 2, 0], sums[:, s4:s4 + 2, 1], ALU.add))
                        nc.vector.reciprocal(inv[k % 2], inv[k % 2]).then_inc(inv_ready[l], 1)
                    else:
                        nc.vector.reciprocal(inv[k % 2], sums[:, s4:s4 + 2, 1]).then_inc(inv_ready[l], 1)

                def gate_rows(hp, k):
                    t = query_tiles(l)[k]
                    b = bank(6 + k % 2)
                    dve.wait_ge(inv_done[l], hp * (n // 2) + k + 1)
                    for e in range(2):
                        r = slice(64 * e, 64 * e + 64)
                        src = b[r, 128:384].rearrange("p (u c) -> p u c", u=2)[:, :, 64 * e:64 * e + 64]
                        last = TT(zr[k % 2][r].rearrange("p (u c) -> p u c", u=2),
                                  zT[r, P * t:P * t + P].rearrange("p (u c) -> p u c", u=2), src, ALU.mult)
                    link_pair(hp, last)
                    out = yT[:, bass.ds(hp + 2, 1), :].rearrange("p a b -> p (a b)")[:, P * t:P * t + P]
                    TT(out, b[:, 0:P], zr[k % 2], ALU.mult).then_inc(yna_taken[l], 1)

                def ada_turn(hp, i):
                    m, b = i // 2 - 1, bank(2 * (i % 2) + 1)
                    if l + 1 == DEPTH or i % 2 or not 0 <= m <= 6:
                        return
                    if m < 6:
                        nc.vector.tensor_copy(adarow[m % 2][0:2, :], b[0:2, 256:384]).then_inc(row_ready, 1)
                    if m:
                        nc.vector.tensor_copy(mod[:, l + 1, bass.ds(6 * hp + (m - 1), 1), :].rearrange("p a b -> p (a b)"),
                                              b[:, 384:386]).then_inc(ada_taken[l + 1], 1)

                for e in range(2):
                    r = slice(64 * e, 64 * e + 64)
                    last = nc.vector.memset(qbd[r, min(steps):, 64 - 64 * e:P - 64 * e], 0.0)
                last.then_inc(yna_taken[l], 1)
                def pair(hp):
                    linked[0] = 0
                    dve.wait_ge(tab_loaded[l], 32 * hp + 32)
                    link_pair(hp, TT(tab, tab, colmask[:].unsqueeze(2).broadcast_to([P, GRID_W, TW]), ALU.add))
                    for r, ts in enumerate(EVEN + ODD):
                        dve.wait_ge(aux_done[l], V_ROUNDS * hp + (aux0 + r + 1))
                        dst = vtok if r < len(EVEN) else vodd
                        nc.vector.tensor_copy(dst[:, ts[0]:ts[-1] + 1, :], bank(6 + r % 2)[:, 0:P * len(ts)].rearrange(
                            "p (c n) -> p c n", n=P)).then_inc(aux_taken[l], 1)
                    row_max(hp, 0)
                    row_max(hp, 1)
                    for i in range(n):
                        k = i // 2
                        dve.wait_ge(pT_done[l], hp * n + i + 1)
                        if steps[i] >= 2 * CT:
                            nc.vector.tensor_copy(PT[i % 2][:, 0:512], bank(4)).then_inc(ptA_ready[l], 1)
                        else:
                            dve.sem_inc(ptA_ready[l], 1)
                        if i + 2 < n:
                            row_max(hp, i + 2)
                        if i % 2:
                            inverse_sums(hp, k)
                        elif k:
                            gate_rows(hp, k - 1)
                    gate_rows(hp, n // 2 - 1)
                    assert linked[0] == pair_links

                with dve.Fori(0, PAIRS - 1) as hp:
                    pair(hp)
                pair(PAIRS - 1)
                k, o = OUT_ORDER[KC - 1], P * tiles(l)[0]
                dve.wait_ge(yhi_ready[l], KC)
                TT(hLo[:, k, o:T], yT[:, k, o:T], hHi[:, k, o:T].bitcast(F32), ALU.subtract).then_inc(ylast_ready, 1)
                dve.wait_ge(wlast_high, l + 1)
                for to, raw, hi in zip(wout[KC - 1][1], halves(flat(wraw[1])), wout[KC - 1][0]):
                    last = TT(to, raw, hi.bitcast(F32), ALU.subtract)
                last.then_inc(wlast_split, 1)
                if l + 1 < DEPTH:
                    dve.wait_ge(ada_taken[l + 1], NADA)
                    finish_mod(l + 1, 0, NADA)
                    split_wdt(l + 1)

                for v in range(2 if l < DEPTH - 1 else 1):
                    dve.wait_ge(gb_done[l], v + 1)
                    nc.vector.tensor_copy(gbc[v], bank(6 - 2 * v, 2)).then_inc(gb_taken[l], 1)
                dve.wait_ge(gb_taken[l], 2 if l < DEPTH - 1 else 1)
                for i, t in enumerate(tiles(l)):
                    dve.wait_ge(osd_done[l], i + 1)
                    link(nc.vector.reciprocal(rstd2[:, t:t + 1], rstd2[:, t:t + 1]))
                    if i >= 2:
                        dve.wait_ge(stored[i % 2], stores(l, i - 2))
                        if l + 1 < DEPTH:
                            dve.wait_ge(xn_ready[l + 1], t - 1)
                    STT(osb[i % 2], bank(2 * (i % 2), 2), rstd2[:, t:t + 1], gbc[1 if t < CT else 0],
                        ALU.mult, ALU.mult).then_inc(o_ready[l], 1)
                    if l + 1 < DEPTH:
                        if i:
                            norm_mod(l + 1, t - 1)
                        norm_rstd(l + 1, t)
                if l + 1 < DEPTH:
                    norm_mod(l + 1, NT - 1)

        @block.tensor
        def _(pe):
            mm, tp = nc.tensor.matmul, nc.tensor.transpose

            def ada_row(out, w, last_sem):
                for k in range(KC):
                    last = mm(out, ccol[:, k, :], w[:, k, :], start=(k == 0), stop=(k == KC - 1))
                last.then_inc(last_sem, 1)

            def ada_first_layer():
                for i, (b0, nb, place) in enumerate(ADA0):
                    pe.wait_ge(ada_first[i], 16)
                    for b in range(b0, b0 + nb):
                        if b >= 4:
                            pe.wait_ge(ada_taken[0], b - 3)
                        w = place[:, DM * (b - b0):DM * (b - b0 + 1)].rearrange("p (k c) -> p k c", k=KC)
                        ada_row(bank(b % 4)[0:2, 384:512], w, ada_mm[0])
                        if b:
                            ada_column(b - 1)
                        for t in TURN_AFTER.get(b, []):
                            turn_input(0, t)
                ada_column(N0 - 1)
                for t in TURN_AFTER[N0]:
                    turn_input(0, t)

            def ada_column(b):
                pe.wait_ge(row_ready, b + 1)
                tp(bank(b % 4)[:, 256:258], adarow[b % 2][0:2, :], ident[0:2, 0:2]).then_inc(col_done, 1)

            def proj_chunk(s, a, n):
                out = PS[:, slot_cols(s) + a:slot_cols(s) + a + n]
                k3 = [(w, x, k) for k in range(KC) for w, x in ((whi, hHi), (whi, hLo), (wlo, hHi))]
                for q, (w, x, k) in enumerate(k3):
                    last = mm(out, w[s][:, k, :], x[:, k, a:a + n], start=(q == 0), stop=(q == len(k3) - 1))
                return last

            def proj_mm(l, j, s):
                for a, n in chunks(l, j):
                    last = proj_chunk(s, a, n)
                return last

            def turn_input(l, t):
                pe.wait_ge(xn_ready[l], t + 1)
                if l and t == 0:
                    pe.wait_ge(gb_taken[l - 1], 2)
                if t >= 2:
                    pe.wait_ge(xnT_taken[l], t - 1)
                for k in range(KC):
                    last = tp(bank(4 + 2 * (t % 2), 2)[:, P * k:P * k + P], xt[t % 3][:, P * k:P * k + P], ident[:])
                last.then_inc(xnT_done[l], 1)

            def dt_chunk(out, a, n):
                for k in range(KC):
                    mm(out, wdt2[:, k, :], hHi[:, k, a:a + n], start=(k == 0), stop=False)
                    last = mm(out[0:8], wdt2[:, k, 0:8], hLo[:, k, a:a + n], start=False, stop=(k == KC - 1))
                return last

            def input_ready(l, a, n):
                pe.wait_ge(hhi_ready[l], (a + n) // P)
                pe.wait_ge(hlo_ready[l], (a + n) // P)

            def proj(l, j, beside=()):
                pe.wait_ge(w_split[l], j + 1)
                if j >= 2:
                    pe.wait_ge(proj_taken[l], j - 1)
                cs, n = chunks(l, j), len(beside)
                for c, (a, w) in enumerate(cs):
                    last = proj_chunk(j % 2, a, w)
                    if (a, w) == CHUNKS[-1]:
                        last.then_inc(proj_done[l], 1)
                    for step, *args in beside[c * n // len(cs):(c + 1) * n // len(cs)]:
                        step(*args)

            pe.wait_ge(first_consts, 32)
            pe.wait_ge(silu_c, 1)
            ada_first_layer()
            pe.wait_ge(ada_taken[0], N0)
            pe.wait_ge(xnT_taken[0], NT)
            pe.wait_ge(consts, 16 * N_CONSTS)
            pe.wait_ge(w_split[0], 1)
            pe.wait_ge(wdt_split, 1)
            for k in range(KC):
                if k % 2 == 0:
                    pe.wait_ge(hlo_dve, k // 2 + 1)
                else:
                    pe.wait_ge(hlo_ready[0], k // 2 + 1)
                dt_out = [bank(3)[0:16, 0:CTX], bank(4)[0:16, :], bank(5)[0:16, :]]
                for (a, n), out in zip(CHUNKS, dt_out):
                    mm(out, wdt2[:, k, :], hHi[:, k, a:a + n], start=(k == 0), stop=False)
                for (a, n), out in zip(CHUNKS, dt_out):
                    last = mm(out[0:8], wdt2[:, k, 0:8], hLo[:, k, a:a + n], start=False, stop=(k == KC - 1))
                if k == KC - 1:
                    last.then_inc(dtT_done, 1)
                for q, (w, x) in enumerate(((whi, hHi), (whi, hLo), (wlo, hHi))):
                    for a, n in CHUNKS:
                        last = mm(PS[:, slot_cols(0) + a:slot_cols(0) + a + n], w[0][:, k, :],
                                  x[:, k, a:a + n], start=(k == 0 and q == 0), stop=(k == KC - 1 and q == 2))
            last.then_inc(proj_done[0], 1)

            for l in range(DEPTH):
                aux = [0]

                def aux_open():
                    if aux[0] >= 2:
                        pe.wait_ge(aux_taken[l], aux[0] - 1)
                    return bank(6 + aux[0] % 2)

                def aux_close(last):
                    aux[0] += 1
                    last.then_inc(aux_done[l], 1)

                if l:
                    pe.wait_ge(wdt_split, l + 1)
                    pe.wait_ge(o_ready[l - 1], NT - 1)
                    input_ready(l, *CHUNKS[0])
                    dt_chunk(bank(0)[0:16, 0:CTX], *CHUNKS[0])
                    pe.wait_ge(xnT_taken[l], NT - 1)
                    input_ready(l, *CHUNKS[1])
                    dt_chunk(bank(4)[0:16, :], *CHUNKS[1])
                    turn_input(l, NT - 1)
                    pe.wait_ge(w_split[l], 1)
                    for a, n in chunks(l, 0)[:-1]:
                        proj_chunk(0, a, n)
                    input_ready(l, *CHUNKS[2])
                    dt_chunk(bank(5)[0:16, :], *CHUNKS[2]).then_inc(dtT_done, 1)
                    pe.wait_ge(o_ready[l - 1], NT)
                    proj_chunk(0, *CHUNKS[2]).then_inc(proj_done[l], 1)
                pe.wait_ge(dtT_ready, l + 1)
                b = aux_open()
                for c in range(NT):
                    last = tp(b[:, 16 * c:16 * c + 16], dtT[:, P * c:P * c + P], ident[0:16, 0:16])
                aux_close(last)
                proj(l, 1)

                def to_tok(src, r):
                    b = aux_open()
                    for i, c in enumerate(r):
                        last = tp(b[:, P * i:P * i + P], src[:, P * c:P * c + P], ident[:])
                    aux_close(last)

                def x_tok(j, r):
                    pe.wait_ge(silu_done, 6 * l + j + 1)
                    to_tok(cv, r)

                def b_tok(g, r):
                    pe.wait_ge(rope_done, 4 * l + 3 + g)
                    to_tok(BTt[g], r)

                def z_tok(j2, r):
                    pe.wait_ge(proj_taken[l], 7 + j2)
                    to_tok(ubuf[j2], r)

                def back_state(i):
                    c = BO[i]
                    pe.wait_ge(xwb_ready, (NT - 1) * l + i + 1)
                    b = aux_open()
                    for g in range(SG):
                        last = mm(b[:, P * g:P * g + P], btok[:, c, g, :], xw[i % 2][:, P * g:P * g + P],
                                  start=True, stop=True)
                    aux_close(last)

                ALL, OWN = rounds(range(NT)), rounds(tiles(l))
                pe.wait_ge(da_ready, l + 1)
                b = aux_open()
                mm(b[:, 0:40], maskF[:], s_t0[:, 0:40], start=True, stop=True)
                aux_close(mm(b[:, 40:80], maskB[:], s_t0[:, 40:80], start=True, stop=True))
                proj(l, 2)
                pe.wait_ge(acs_ready, l + 1)
                b = aux_open()
                mm(b[:, 0:40], ident[:, P - 1:P].broadcast_to([P, P]), s_ac[:, 0:40], start=True, stop=True)
                aux_close(mm(b[:, 40:80], ident[:, 0:1].broadcast_to([P, P]), s_ac[:, 40:80], start=True, stop=True))
                proj(l, 3)
                proj(l, 4)
                x0, x1 = [[(x_tok, j, r) for r in ALL] for j in (4, 5)]
                b0, b1 = [[(b_tok, g, r) for r in ALL] for g in range(2)]
                z = [(z_tok, j2, r) for j2 in range(2) for r in OWN]
                def gate_row(b):
                    i = 0 if b < N0 + 5 else 1
                    b0, _, place = GATES0[i]
                    pe.wait_ge(ada_first[len(ADA0) + i], 16)
                    out = aux_open()
                    w = place[:, DM * (b - b0):DM * (b - b0 + 1)].rearrange("p (k c) -> p k c", k=KC)
                    for k in range(KC):
                        last = mm(out[0:2, 0:P], ccol[:, k, :], w[:, k, :], start=(k == 0), stop=(k == KC - 1))
                    aux_close(last)

                def gate_column(b):
                    pe.wait_ge(aux_taken[l], aux[0])
                    aux_close(tp(aux_open()[:, 0:2], grow[0:2, :], ident[0:2, 0:2]))

                def late(step, b):
                    return [(step, b)] if l == 0 else []

                proj(l, 5, late(gate_row, 22) + b0[:2])
                for step, *args in x0:
                    step(*args)
                proj(l, 6, late(gate_column, 22) + b0[2:] + late(gate_row, 23) + b1[:1] + late(gate_column, 23)
                     + late(gate_row, 21) + b1[1:2])
                proj(l, 7, late(gate_column, 21) + b1[2:] + late(gate_row, 20) + x1[:1] + late(gate_column, 20)
                     + late(gate_row, 19) + x1[1:2])
                proj(l, 8, late(gate_column, 19) + x1[2:] + z[:1] + late(gate_row, 18) + z[1:2])
                proj(l, 9, late(gate_column, 18) + z[2:3] + late(gate_row, 17) + z[3:4])
                proj(l, 10, late(gate_column, 17) + z[4:])
                for j in range(11, 16):
                    proj(l, j, [(back_state, i) for i in range(2 * (j - 11), min(2 * (j - 11) + 2, NT - 1))])
                pe.wait_ge(aux_taken[l], aux[0])
                pe.wait_ge(proj_taken[l], 16)

                ys = tiles(l)

                def ssd_front(i):
                    c = ys[i]
                    for d in range(2):
                        if i:
                            pe.wait_ge(bc_taken[l], 2 * (i - 1) + d + 1)
                        for h in range(SH):
                            a = 40 * d + 4 * c + h
                            last = tp(bank(1 + d)[:, P * h:P * h + P], s_ac[:, a:a + 1].broadcast_to([P, P]), ident[:])
                        last.then_inc(bc_done[l], 1)
                    if i >= 2:
                        pe.wait_ge(g_taken[l], i - 1)
                    for g in range(SG):
                        last = mm(bank(7 * (i % 2))[:, P * g:P * g + P], BTt[g][:, P * c:P * c + P], CTt[g][:, P * c:P * c + P],
                                  start=True, stop=True)
                    last.then_inc(g_done[l], 1)

                ssd_front(0)
                for c in range(NT):
                    yi, s = c - ys[0], c % 2
                    if yi >= 0 and yi + 1 < len(ys):
                        ssd_front(yi + 1)
                    pe.wait_ge(xp_ready[l], c + 1)
                    if c:
                        pe.wait_ge(prevf_ready[l], c)
                    if c < NT - 1:
                        for g in range(SG):
                            last = mm(bank(5)[:, P * g:P * g + P], btok[:, c, g, :], xw[s][:, P * g:P * g + P],
                                      start=True, stop=True)
                        last.then_inc(stf_done[l], 1)
                    if yi >= 0:
                        if yi:
                            pe.wait_ge(yo_taken[l], yi)
                        for d, prev in enumerate([prevf[s], prevb[:, c, :]]):
                            for g in range(SG):
                                last = mm(bank(4)[:, 256 * d + P * g:256 * d + P * g + P], CTt[g][:, P * c:P * c + P],
                                          prev[:, P * g:P * g + P], start=True, stop=True)
                        last.then_inc(yo_done[l], 1)
                        pe.wait_ge(mix_ready[l], yi + 1)
                        if yi >= 2:
                            pe.wait_ge(y_gated[l], yi - 1)
                        for h in range(SH):
                            g = h // 2
                            for d in range(2):
                                last = mm(bank(3 if yi % 2 else 6)[:, P * h:P * h + P], Ed[yi % 2][d][:, h, :],
                                          xp[d][s][:, P * g:P * g + P], start=(d == 0), stop=(d == 1))
                        last.then_inc(yd_done[l], 1)
                def turn_ssd_output():
                    pe.wait_ge(yn_ready, l + 1)
                    for j in range(2):
                        for r in rounds(ys):
                            b = aux_open()
                            for i, c in enumerate(r):
                                last = tp(b[:, P * i:P * i + P], ztok[:, c, P * j:P * j + P], ident[:])
                            aux_close(last)
                    pe.wait_ge(aux_taken[l], aux[0])

                pe.wait_ge(y_gated[l], len(ys))
                steps = groups(l)
                n = len(steps)
                aux0 = aux_before_attention(l)

                def scores(hp, i):
                    s, q, m = i % 2, qbd[:, steps[i], :], i // 2 - 1
                    with_ada = l + 1 < DEPTH and i % 2 == 0 and 0 <= m <= 6
                    if with_ada and m:
                        pe.wait_ge(row_ready, 6 * hp + (N0 + NADA * l + m))
                    if with_ada and m < 6:
                        pe.wait_ge(ada_loaded[m % 2], 48 * hp + 16 * (m // 2 + 1))
                        ada_row(bank(2 * s + 1)[0:2, 256:384], adaw[m % 2], ada_mm[l + 1])
                    if steps[i] >= 2 * CT:
                        k0 = CTX + GRID_W * window(steps[i] - 2 * CT)[0]
                        mm(bank(2 * s), q, kT[:, k0:k0 + 512], start=True, stop=True)
                    if with_ada and m:
                        tp(bank(2 * s + 1)[:, 384:386], adarow[(m - 1) % 2][0:2, :], ident[0:2, 0:2])
                    mm(bank(2 * s + 1)[:, 0:256], q, kT[:, 0:CTX], start=True, stop=True).then_inc(s_done[l], 1)

                def flip(hp, i):
                    s = i % 2
                    if i:
                        pe.wait_ge(ptA_ready[l], hp * n + i)
                        pe.wait_ge(ptB_ready[l], hp * n + i)
                    pe.wait_ge(p_ready[l], hp * n + i + 1)
                    if steps[i] >= 2 * CT:
                        for m in range(4):
                            tp(bank(4)[:, P * m:P * m + P], Pr[s][:, P * m:P * m + P], ident[:])
                    for m in range(2):
                        last = tp(bank(5)[:, P * m:P * m + P], Pr[s][:, 512 + P * m:640 + P * m], ident[:])
                    last.then_inc(pT_done[l], 1)

                def values(hp, i):
                    s, k = i % 2, i // 2
                    pe.wait_ge(ptA_ready[l], hp * n + i + 1)
                    pe.wait_ge(ptB_ready[l], hp * n + i + 1)
                    if i % 2 == 0:
                        pe.wait_ge(yna_taken[l], hp * (n // 2) + (k - 1 if k >= 2 else 0) + 1)
                    parts = [(vtok[:, m], 512 + P * m) for m in range(CT)]
                    if steps[i] >= 2 * CT:
                        r0 = window(steps[i] - 2 * CT)[0]
                        src, kt = (vodd, r0 // 2) if r0 % 2 else (vtok, CT + r0 // 2)
                        parts += [(src[:, kt + m], P * m) for m in range(4)]
                    for e in range(2):
                        out = bank(6 + k % 2)[64 * e:64 * e + 64, 64 * (i % 2):64 * (i % 2) + 64]
                        for m, (v, a) in enumerate(parts):
                            last = mm(out, v[:, 64 * e:64 * e + 64], PT[s][:, a + 64 * e:a + 64 * e + 64],
                                      start=(m == 0), stop=(m == len(parts) - 1))
                    last.then_inc(o_done[l], 1)

                def spread_inverse(hp, k):
                    pe.wait_ge(inv_ready[l], hp * (n // 2) + k + 1)
                    for u in range(2):
                        last = tp(bank(6 + k % 2)[:, P * (u + 1):P * (u + 2)], inv[k % 2][:, u:u + 1].broadcast_to([P, P]),
                                  ident[:])
                    last.then_inc(inv_done[l], 1)

                def turn_values(hp, r):
                    ts = (EVEN + ODD)[r]
                    if r >= 2:
                        pe.wait_ge(aux_taken[l], V_ROUNDS * hp + (aux0 + r - 1))
                    for i, c in enumerate(ts):
                        a = P * c if r < len(EVEN) else CTX + GRID_W + P * c
                        last = tp(bank(6 + r % 2)[:, P * i:P * i + P], vT[:, a:a + P], ident[:])
                    last.then_inc(aux_done[l], 1)

                def pair(hp, first=False):
                    for i in range(4):
                        j = Q0 + i
                        if first and i == 1:
                            turn_ssd_output()
                        pe.wait_ge(w_split[l], 4 * hp + (j + 1))
                        pe.wait_ge(proj_taken[l], 4 * hp + (j - 1))
                        if i in (0, 2):
                            proj_mm(l, j, j % 2).then_inc(proj_done[l], 1)
                        elif i == 1:
                            for c, (a, w) in enumerate(chunks(l, j)):
                                last = proj_chunk(j % 2, a, w)
                                if (a, w) == CHUNKS[-1]:
                                    last.then_inc(proj_done[l], 1)
                                if c == 0:
                                    pe.wait_ge(proj_taken[l], 4 * hp + (Q0 + 1))
                                    pe.wait_ge(yna_taken[l], hp * (n // 2) + 1)
                                    turn_values(hp, 0)
                                    turn_values(hp, 1)
                            turn_values(hp, 2)
                        else:
                            for a, w in CHUNKS[:-1]:
                                last = proj_chunk(j % 2, a, w)
                            last.then_inc(k_part, 1)
                            for r in range(3, V_ROUNDS):
                                turn_values(hp, r)
                            pe.wait_ge(k_part_taken, hp + (PAIRS * l + 1))
                            scores(hp, 0)
                            proj_chunk(j % 2, *CHUNKS[-1]).then_inc(proj_done[l], 1)
                    scores(hp, 1)
                    pe.wait_ge(proj_taken[l], 4 * hp + (Q0 + 4))
                    pe.wait_ge(aux_taken[l], V_ROUNDS * hp + (aux0 + V_ROUNDS))
                    for i in range(n):
                        flip(hp, i)
                        if i + 2 < n:
                            scores(hp, i + 2)
                        if i:
                            values(hp, i - 1)
                            if i % 2 == 0:
                                spread_inverse(hp, i // 2 - 1)
                    values(hp, n - 1)
                    spread_inverse(hp, n // 2 - 1)

                pair(0, first=True)
                with pe.Fori(1, PAIRS - 1) as hp:
                    pair(hp)
                pair(PAIRS - 1)

                pe.wait_ge(yna_taken[l], PAIRS * (n // 2) + 1)
                for v in range(2 if l < DEPTH - 1 else 1):
                    for k in range(KC):
                        last = tp(bank(6 - 2 * v, 2)[:, P * k:P * k + P], mod[:, l, 2 * KC + k, v:v + 1].broadcast_to([P, P]), ident[:])
                    last.then_inc(gb_done[l], 1)
                for i, t in enumerate(tiles(l)):
                    if i >= 2:
                        pe.wait_ge(o_ready[l], i - 1)
                    for m, k in enumerate(OUT_ORDER):
                        if i == 0:
                            if m < KC - 1:
                                pe.wait_ge(w_split[l], NB_IN + m + 1)
                                pe.wait_ge(ylo_ready[l], m + 1)
                            else:
                                pe.wait_ge(ylast_ready, l + 1)
                                pe.wait_ge(wlast_split, l + 1)
                        hi, lo = wout[m]
                        for q, (x, w) in enumerate([(hHi, hi), (hHi, lo), (hLo, hi)]):
                            for h in range(2):
                                last = mm(bank(2 * (i % 2) + h), x[:, k, P * t:P * t + P], w[h],
                                          start=(m == 0 and q == 0), stop=(m == KC - 1 and q == 2))
                    last.then_inc(out_done[l], 1)
                    if l + 1 < DEPTH and i:
                        turn_input(l + 1, t - 1)


def _constants():
    f = np.float32
    j, i = np.arange(P)[:, None], np.arange(P)[None, :]
    n_freq = SN // 4
    inv_freq = (f(10000.0) ** (-np.arange(n_freq, dtype=f) / f(n_freq))).astype(f)
    pos = np.arange(SEQ)
    ang_r = (pos // GRID_W).astype(f)[None, :] * inv_freq[:, None]
    ang_c = (pos % GRID_W).astype(f)[None, :] * inv_freq[:, None]
    ang = np.concatenate([ang_r, ang_r, ang_c, ang_c]).astype(f)
    cols = np.arange(GRID_W)
    lo = np.clip(cols - WIN_W // 2, 0, GRID_W - WIN_W)[:, None]
    inside = (cols[None, :] >= lo) & (cols[None, :] < lo + WIN_W)
    colmask = np.where(np.concatenate([inside, inside])[:, ::-1], 0.0, NEG).astype(f)
    return dict(ident=np.eye(P, dtype=f), maskF=(j <= i).astype(f), maskB=(j >= i).astype(f),
                colmask=colmask, rope_cos=np.cos(ang).astype(f), rope_sin=np.sin(ang).astype(f))


def _layout(x, c, ctx, c_ctx, w_ada, b_ada, g_pre, g_post, w_in, conv_a_w, rpb, ssd_conv_w, ssd_conv_b,
            dt_bias_f, dt_bias_b, a_log_f, a_log_b, ssd_d, ssd_norm_w, w_out):
    def by_channel(a):
        return np.moveaxis(a.reshape(*a.shape[:-1], -1, P), -1, 0)

    def blocks(w):
        return w.reshape(KC, P, -1, P).transpose(2, 1, 0, 3)

    cols = block_columns()
    w_blocks = np.stack([np.concatenate([
        blocks(np.concatenate([w_in[l][:, s:s + P] for s in cols], axis=1)), w_out[l].reshape(KC, P, KC, P)[[0, 1, 6, 7, 2, 3, 4, 5]]]) for l in range(DEPTH)])
    conv_w = np.concatenate([ssd_conv_w, ssd_conv_b[:, None, :]], axis=1)
    conv_w = conv_w.reshape(DEPTH, 4, 6, P)[:, :, [4, 5, 2, 3, 0, 1]].transpose(3, 0, 2, 1)
    table = np.pad(rpb.transpose(0, 1, 3, 2)[:, :, ::-1], ((0, 0), (0, 0), (48, 48), (0, 1)))
    arrays = dict(
        tokens=np.concatenate([ctx[0], x[0]]),
        ccol=np.stack([by_channel(c[0]), by_channel(c_ctx)], axis=-1),
        w_ada=np.stack([blocks(w_ada[l]) for l in range(DEPTH)]),
        b_ada=by_channel(b_ada), g_pre=by_channel(g_pre), g_post=by_channel(g_post),
        w_blocks=w_blocks,
        w_dt=w_in[:, :, SPLIT_IN[10]:].reshape(DEPTH, KC, P, 8).transpose(0, 2, 1, 3),
        conv_w=conv_w, conv_a=conv_a_w.reshape(DEPTH, 3, 2, P).transpose(3, 0, 2, 1),
        norm_w=by_channel(ssd_norm_w), rpb=table,
        dt_bias=np.concatenate([dt_bias_f, dt_bias_b], axis=1).reshape(-1),
        a_log=np.concatenate([a_log_f, a_log_b], axis=1).reshape(-1),
        ssd_d=ssd_d.reshape(-1))
    return arrays | _constants()


def build(nc, arrays):
    A = {name: nc.dram_tensor(f"in_{name}", a.shape, mybir.dt.from_np(a.dtype), kind="ExternalInput").ap()
         for name, a in arrays.items()}
    A["x_mid"] = nc.dram_tensor("x_mid", (T, DM), F32, kind="Internal").ap()
    A["out"] = nc.dram_tensor("out_x", (SEQ, DM), F32, kind="ExternalOutput").ap()
    trunk(nc, A)


def kernel(**inputs):
    import concourse.bacc as bacc
    from concourse.bass_utils import run_bass_kernel_spmd

    arrays = {k: np.ascontiguousarray(v) for k, v in _layout(**{k: np.asarray(v) for k, v in inputs.items()}).items()}
    nc = bacc.Bacc("TRN2", target_bir_lowering=False, num_devices=1)
    build(nc, arrays)
    r = run_bass_kernel_spmd(nc, [{f"in_{k}": v for k, v in arrays.items()}], core_ids=[0])
    return r.results[0]["out_x"].reshape(1, SEQ, DM)
```
